# Optimizing a Trainium2 kernel written in Bass

```python
import math
import jax, jax.numpy as jnp
from jax import lax
import numpy as np

D_MODEL = 1024
BATCH = 1
SEQ = 256
DEPTH = 1

D_MIX = 2 * D_MODEL
ATTN_WIDTH = D_MIX // 2
V_HEAD_DIM = 128
QK_HEAD_DIM = V_HEAD_DIM // 2
ATTN_HEADS = ATTN_WIDTH // V_HEAD_DIM
Q_WIDTH = ATTN_HEADS * 2 * QK_HEAD_DIM
K_WIDTH = ATTN_HEADS * 2 * QK_HEAD_DIM
V_WIDTH = ATTN_HEADS * V_HEAD_DIM
LRU_WIDTH = D_MIX - ATTN_WIDTH
LRU_BLOCKS = 8
LRU_BLOCK = LRU_WIDTH // LRU_BLOCKS
LRU_C = 8.0
CONV_WIDTH = 4
Q_BLOCK = 128
NORM_EPS = 1e-6
IN_SPLITS = (Q_WIDTH, K_WIDTH, V_WIDTH, ATTN_WIDTH, LRU_WIDTH, LRU_WIDTH)
D_IN_PROJ = sum(IN_SPLITS)
SPLIT_POINTS = tuple(int(v) for v in np.cumsum(IN_SPLITS)[:-1])


def rmsnorm(x, g):
    xf = x.astype(jnp.float32)
    y = xf * lax.rsqrt(jnp.mean(xf * xf, axis=-1, keepdims=True) + NORM_EPS)
    return (y * g.astype(jnp.float32)).astype(x.dtype)

def lambda_init_for(layer_idx):
    return 0.8 - 0.6 * math.exp(-0.3 * layer_idx)

def diff_attention(q, k, v, lam):
    S = q.shape[1]
    scale = QK_HEAD_DIM ** -0.5
    outs = []
    for i in range(S // Q_BLOCK):
        q0 = i * Q_BLOCK
        end = q0 + Q_BLOCK
        s = jnp.einsum('bqhcd,bkhcd->bhcqk', q[:, q0:end], k[:, :end],
                       preferred_element_type=jnp.float32) * scale
        qpos = q0 + jnp.arange(Q_BLOCK)
        kpos = jnp.arange(end)
        causal = kpos[None, :] <= qpos[:, None]
        p = jax.nn.softmax(jnp.where(causal, s, -jnp.inf), axis=-1)
        w = p[:, :, 0] - lam * p[:, :, 1]
        outs.append(jnp.einsum('bhqk,bkhe->bqhe', w, v[:, :end].astype(jnp.float32)))
    return jnp.concatenate(outs, axis=1)

def causal_depthwise_conv(x, w, b):
    y = lax.conv_general_dilated(
        x, w[:, None, :].astype(x.dtype), window_strides=(1,), padding=[(CONV_WIDTH - 1, 0)],
        dimension_numbers=('NWC', 'WIO', 'NWC'), feature_group_count=x.shape[-1])
    return y + b.astype(x.dtype)

def _lin_combine(c1, c2):
    a1, b1 = c1
    a2, b2 = c2
    return a1 * a2, a2 * b1 + b2

def rg_lru(xc, w_r, b_r, w_i, b_i, lam_param):
    B, S, _ = xc.shape
    xb = xc.reshape(B, S, LRU_BLOCKS, LRU_BLOCK).astype(jnp.float32)
    r = jax.nn.sigmoid(jnp.einsum('bsnc,ncd->bsnd', xb, w_r.astype(jnp.float32)).reshape(B, S, LRU_WIDTH)
                       + b_r.astype(jnp.float32))
    gi = jax.nn.sigmoid(jnp.einsum('bsnc,ncd->bsnd', xb, w_i.astype(jnp.float32)).reshape(B, S, LRU_WIDTH)
                        + b_i.astype(jnp.float32))
    log_a = -LRU_C * r * jax.nn.softplus(-lam_param.astype(jnp.float32))
    a = jnp.exp(log_a)
    mult = jnp.sqrt(jnp.maximum(-jnp.expm1(2.0 * log_a), 0.0))
    bterm = mult * gi * xc.astype(jnp.float32)
    _, h = lax.associative_scan(_lin_combine, (a, bterm), axis=1)
    return h

def first_inputs(seed: int = 0) -> dict:
    key = jax.random.key(seed)
    ks = jax.random.split(key, 20)
    f32 = jnp.float32
    x = jax.random.normal(ks[0], (BATCH, SEQ, D_MODEL), f32)
    pre_norm_g = 1.0 + 0.05 * jax.random.normal(ks[1], (DEPTH, D_MODEL), f32)
    w_in = jax.random.normal(ks[2], (DEPTH, D_MODEL, D_IN_PROJ), f32) * D_MODEL ** -0.5
    lambda_q1 = 0.1 * jax.random.normal(ks[3], (DEPTH, QK_HEAD_DIM), f32)
    lambda_k1 = 0.1 * jax.random.normal(ks[4], (DEPTH, QK_HEAD_DIM), f32)
    lambda_q2 = 0.1 * jax.random.normal(ks[5], (DEPTH, QK_HEAD_DIM), f32)
    lambda_k2 = 0.1 * jax.random.normal(ks[6], (DEPTH, QK_HEAD_DIM), f32)
    subln_g = 1.0 + 0.05 * jax.random.normal(ks[7], (DEPTH, V_HEAD_DIM), f32)
    conv_w = jax.random.normal(ks[8], (DEPTH, CONV_WIDTH, LRU_WIDTH), f32) * CONV_WIDTH ** -0.5
    conv_b = 0.02 * jax.random.normal(ks[9], (DEPTH, LRU_WIDTH), f32)
    w_rgate = jax.random.normal(ks[10], (DEPTH, LRU_BLOCKS, LRU_BLOCK, LRU_BLOCK), f32) * LRU_BLOCK ** -0.5
    b_rgate = 0.02 * jax.random.normal(ks[11], (DEPTH, LRU_WIDTH), f32)
    w_igate = jax.random.normal(ks[12], (DEPTH, LRU_BLOCKS, LRU_BLOCK, LRU_BLOCK), f32) * LRU_BLOCK ** -0.5
    b_igate = 0.02 * jax.random.normal(ks[13], (DEPTH, LRU_WIDTH), f32)
    a0 = jax.random.uniform(ks[14], (DEPTH, LRU_WIDTH), f32, 0.9, 0.999)
    s0 = a0 ** (1.0 / LRU_C)
    lru_lambda = jnp.log(s0) - jnp.log1p(-s0)
    w_out = jax.random.normal(ks[15], (DEPTH, D_MIX, D_MODEL), f32) * D_MIX ** -0.5
    post_norm_g = 1.0 + 0.05 * jax.random.normal(ks[16], (DEPTH, D_MODEL), f32)
    return {"x": x, "pre_norm_g": pre_norm_g, "w_in": w_in,
            "lambda_q1": lambda_q1, "lambda_k1": lambda_k1,
            "lambda_q2": lambda_q2, "lambda_k2": lambda_k2, "subln_g": subln_g,
            "conv_w": conv_w, "conv_b": conv_b,
            "w_rgate": w_rgate, "b_rgate": b_rgate, "w_igate": w_igate, "b_igate": b_igate,
            "lru_lambda": lru_lambda, "w_out": w_out, "post_norm_g": post_norm_g}

def first_block(x, pre_norm_g, w_in, lambda_q1, lambda_k1, lambda_q2, lambda_k2, subln_g,
              conv_w, conv_b, w_rgate, b_rgate, w_igate, b_igate, lru_lambda, w_out, post_norm_g):
    B, S, _ = x.shape
    for l in range(DEPTH):
        h = rmsnorm(x, pre_norm_g[l])
        proj = jnp.einsum('bsd,de->bse', h, w_in[l])
        q, k, v, g_attn, x_lru, g_lru = jnp.split(proj, SPLIT_POINTS, axis=-1)

        lam_init = lambda_init_for(l)
        lam = (jnp.exp(jnp.sum(lambda_q1[l].astype(jnp.float32) * lambda_k1[l].astype(jnp.float32)))
               - jnp.exp(jnp.sum(lambda_q2[l].astype(jnp.float32) * lambda_k2[l].astype(jnp.float32)))
               + lam_init)
        qh = q.reshape(B, S, ATTN_HEADS, 2, QK_HEAD_DIM)
        kh = k.reshape(B, S, ATTN_HEADS, 2, QK_HEAD_DIM)
        vh = v.reshape(B, S, ATTN_HEADS, V_HEAD_DIM)
        o = diff_attention(qh, kh, vh, lam)
        o = rmsnorm(o, subln_g[l]) * (1.0 - lam_init)
        y_attn = o.reshape(B, S, ATTN_WIDTH).astype(x.dtype) * jax.nn.silu(g_attn)

        xc = causal_depthwise_conv(x_lru, conv_w[l], conv_b[l])
        hr = rg_lru(xc, w_rgate[l], b_rgate[l], w_igate[l], b_igate[l], lru_lambda[l])
        y_lru = hr.astype(x.dtype) * jax.nn.silu(g_lru)

        y = jnp.concatenate([y_attn, y_lru], axis=-1)
        y = jnp.einsum('bse,ed->bsd', y, w_out[l])
        x = x + rmsnorm(y, post_norm_g[l])
    return x


D_MIX_2 = D_MODEL
HG_WIDTH = D_MIX_2 // 2
HG_DK = 128
HG_DV = 128
HG_HEADS = HG_WIDTH // HG_DV
HG_CHUNK = 64
NSA_WIDTH = D_MIX_2 - HG_WIDTH
NSA_DH = 64
NSA_HEADS = NSA_WIDTH // NSA_DH
NSA_KV_HEADS = 2
NSA_GROUP = NSA_HEADS // NSA_KV_HEADS
CMP_LEN = 32
CMP_STRIDE = 16
SLC_LEN = 64
SLC_TOPK = 16
WIN = 512
PLE_DIM = 256
PEER_HEADS = 8
PEER_NKEYS = 128
PEER_N = PEER_NKEYS * PEER_NKEYS
PEER_DKEY = 256
PEER_TOPK = 16
PEER_TOKEN_BLOCK = 128
EPS = 1e-6

KV_WIDTH = NSA_KV_HEADS * NSA_DH
SPLIT_SIZES = (HG_WIDTH, HG_WIDTH, HG_WIDTH, HG_WIDTH, NSA_WIDTH,
               KV_WIDTH, KV_WIDTH, KV_WIDTH, KV_WIDTH, KV_WIDTH, KV_WIDTH, 3 * NSA_HEADS)
SPLIT_POINTS_2 = tuple(int(v) for v in np.cumsum(SPLIT_SIZES)[:-1])
D_IN = int(sum(SPLIT_SIZES))


def rmsnorm_2(x, g):
    x32 = x.astype(jnp.float32)
    y = x32 * lax.rsqrt(jnp.mean(x32 * x32, axis=-1, keepdims=True) + EPS)
    return (y * g.astype(jnp.float32)).astype(x.dtype)

def alibi_slopes(n_heads):
    return jnp.asarray(2.0 ** (-8.0 * np.arange(1, n_heads + 1) / n_heads), dtype=jnp.float32)

def masked_softmax(s, mask):
    s = jnp.where(mask, s, -jnp.inf)
    m = jnp.max(s, axis=-1, keepdims=True)
    m = jnp.where(jnp.isfinite(m), m, 0.0)
    e = jnp.where(mask, jnp.exp(s - m), 0.0)
    return e / jnp.maximum(jnp.sum(e, axis=-1, keepdims=True), 1e-30)

def hgrn2_mixer(q, f_logit, i_val, g, lb, out_gain):
    B, T, _ = q.shape
    f32 = jnp.float32
    C = HG_CHUNK
    n_chunk = T // C
    forget = lb + (1.0 - lb) * jax.nn.sigmoid(f_logit.astype(f32))
    log_f = jnp.log(forget)
    key = 1.0 - forget
    query = jax.nn.silu(q.astype(f32)) * HG_DK ** -0.5

    def chunks(a, d):
        return a.reshape(B, n_chunk, C, HG_HEADS, d).transpose(0, 3, 1, 2, 4)

    qc = chunks(query, HG_DK)
    kc = chunks(key, HG_DK)
    vc = chunks(i_val.astype(f32), HG_DV)
    G = jnp.cumsum(chunks(log_f, HG_DK), axis=3)
    G_ref = G[:, :, :, C // 2 - 1:C // 2]
    G_last = G[:, :, :, C - 1:C]
    causal = jnp.tril(jnp.ones((C, C), dtype=bool))
    a = jnp.einsum('bhntk,bhnsk->bhnts', qc * jnp.exp(G - G_ref), kc * jnp.exp(G_ref - G))
    o_intra = jnp.einsum('bhnts,bhnsv->bhntv', jnp.where(causal, a, 0.0), vc)
    q_in = jnp.moveaxis(qc * jnp.exp(G), 2, 0)
    k_in = jnp.moveaxis(kc * jnp.exp(G_last - G), 2, 0)
    v_in = jnp.moveaxis(vc, 2, 0)
    d_in = jnp.moveaxis(jnp.exp(G_last[:, :, :, 0]), 2, 0)

    def step(S, xs):
        q_t, k_t, v_t, d_t = xs
        o_t = jnp.einsum('bhtk,bhkv->bhtv', q_t, S)
        S = d_t[..., None] * S + jnp.einsum('bhtk,bhtv->bhkv', k_t, v_t)
        return S, o_t

    S0 = jnp.zeros((B, HG_HEADS, HG_DK, HG_DV), f32)
    _, o_inter = lax.scan(step, S0, (q_in, k_in, v_in, d_in))
    o = o_intra + jnp.moveaxis(o_inter, 0, 2)
    o = o.transpose(0, 2, 3, 1, 4).reshape(B, T, HG_HEADS, HG_DV)
    gate = jax.nn.silu(g.astype(f32)).reshape(B, T, HG_HEADS, HG_DV)
    return (rmsnorm_2(o, out_gain.reshape(HG_HEADS, HG_DV)) * gate).reshape(B, T, HG_WIDTH)

def cmp_to_slc(imp, n_slc):
    ratio = SLC_LEN // CMP_STRIDE
    span = CMP_LEN // CMP_STRIDE
    weights = np.convolve(np.ones(ratio), np.ones(span))
    n_cmp = imp.shape[-1]
    pad = n_slc * ratio + ratio + span - n_cmp
    padded = jnp.pad(imp, [(0, 0)] * (imp.ndim - 1) + [(0, pad)])
    out = float(weights[0]) * padded[..., 0:n_slc * ratio:ratio]
    for o in range(1, len(weights)):
        out = out + float(weights[o]) * padded[..., o:o + n_slc * ratio:ratio]
    return out

def nsa_mixer(q, k_cmp, v_cmp, k_slc, v_slc, k_win, v_win, gate_logit,
              q_gain, k_gain, cmp_pe, cmp_w1, cmp_w2, out_gain):
    B, T, _ = q.shape
    f32 = jnp.float32
    G, R = NSA_KV_HEADS, NSA_GROUP

    def heads(a, n):
        return a.astype(f32).reshape(B, T, n, NSA_DH).transpose(0, 2, 1, 3)

    qh = rmsnorm_2(heads(q, NSA_HEADS), q_gain) * NSA_DH ** -0.5
    qg = qh.reshape(B, G, R, T, NSA_DH)
    n_cmp = (T - CMP_LEN) // CMP_STRIDE + 1

    def compress(a, pe, w1, w2):
        c = a.reshape(B, G, T // CMP_STRIDE, CMP_STRIDE, NSA_DH)
        blk = jnp.concatenate([c[:, :, j:j + n_cmp] for j in range(CMP_LEN // CMP_STRIDE)], axis=3)
        blk = (blk + pe).reshape(B, G, n_cmp, CMP_LEN * NSA_DH)
        return jax.nn.gelu(blk @ w1) @ w2

    kc = rmsnorm_2(compress(heads(k_cmp, G), cmp_pe[0], cmp_w1[0], cmp_w2[0]), k_gain[0])
    vc = compress(heads(v_cmp, G), cmp_pe[1], cmp_w1[1], cmp_w2[1])
    cmp_end = jnp.arange(n_cmp) * CMP_STRIDE + CMP_LEN - 1
    n_slc = T // SLC_LEN
    top_n = min(SLC_TOPK, n_slc)
    k_sb = rmsnorm_2(heads(k_slc, G), k_gain[1]).reshape(B, G, n_slc, SLC_LEN, NSA_DH)
    v_sb = heads(v_slc, G).reshape(B, G, n_slc, SLC_LEN, NSA_DH)
    pad_w = ((0, 0), (0, 0), (WIN, 0), (0, 0))
    k_wp = jnp.pad(rmsnorm_2(heads(k_win, G), k_gain[2]), pad_w)
    v_wp = jnp.pad(heads(v_win, G), pad_w)
    gates = jax.nn.sigmoid(gate_logit.astype(f32)).reshape(B, T, NSA_HEADS, 3).transpose(0, 2, 1, 3)
    gates = gates.reshape(B, G, R, T, 3)
    slopes = alibi_slopes(NSA_HEADS).reshape(1, G, R, 1, 1)
    gather_blocks = jax.vmap(jax.vmap(lambda blocks, ix: blocks[ix]))

    def query_block(b):
        t0 = b * Q_BLOCK
        qb = lax.dynamic_slice_in_dim(qg, t0, Q_BLOCK, axis=3)
        gb = lax.dynamic_slice_in_dim(gates, t0, Q_BLOCK, axis=3)
        t = t0 + jnp.arange(Q_BLOCK)
        dist_c = t[:, None] - cmp_end[None, :]
        s_c = jnp.einsum('bgrtd,bgnd->bgrtn', qb, kc) - slopes * dist_c
        p_c = masked_softmax(s_c, dist_c >= 0)
        o_c = jnp.einsum('bgrtn,bgnd->bgrtd', p_c, vc)
        imp = cmp_to_slc(jnp.sum(p_c, axis=2), n_slc)
        blk_id = jnp.arange(n_slc)[None, :]
        cur = (t // SLC_LEN)[:, None]
        forced = (blk_id == 0) | (blk_id == cur) | (blk_id == cur - 1)
        imp = jnp.where(forced, jnp.inf, jnp.where(blk_id <= cur, imp, -jnp.inf))
        _, sel = lax.top_k(imp, top_n)
        ks = gather_blocks(k_sb, sel).reshape(B, G, Q_BLOCK, top_n * SLC_LEN, NSA_DH)
        vs = gather_blocks(v_sb, sel).reshape(B, G, Q_BLOCK, top_n * SLC_LEN, NSA_DH)
        pos = (sel[..., None] * SLC_LEN + jnp.arange(SLC_LEN)).reshape(B, G, Q_BLOCK, top_n * SLC_LEN)
        dist_s = (t[:, None] - pos)[:, :, None]
        s_s = jnp.einsum('bgrtd,bgtmd->bgrtm', qb, ks) - slopes * dist_s
        p_s = masked_softmax(s_s, dist_s >= 0)
        o_s = jnp.einsum('bgrtm,bgtmd->bgrtd', p_s, vs)
        kw = lax.dynamic_slice_in_dim(k_wp, t0, WIN + Q_BLOCK, axis=2)
        vw = lax.dynamic_slice_in_dim(v_wp, t0, WIN + Q_BLOCK, axis=2)
        pos_w = t0 - WIN + jnp.arange(WIN + Q_BLOCK)
        dist_w = t[:, None] - pos_w[None, :]
        valid_w = (dist_w >= 0) & (dist_w < WIN) & (pos_w[None, :] >= 0)
        s_w = jnp.einsum('bgrtd,bgsd->bgrts', qb, kw) - slopes * dist_w
        p_w = masked_softmax(s_w, valid_w)
        o_w = jnp.einsum('bgrts,bgsd->bgrtd', p_w, vw)
        return gb[..., 0:1] * o_c + gb[..., 1:2] * o_s + gb[..., 2:3] * o_w

    o = lax.map(query_block, jnp.arange(T // Q_BLOCK))
    o = o.transpose(1, 0, 4, 2, 3, 5).reshape(B, T, NSA_HEADS, NSA_DH)
    return rmsnorm_2(o, out_gain.reshape(NSA_HEADS, NSA_DH)).reshape(B, T, NSA_WIDTH)

def peer_ffn(h, wq, sub_keys, u, v):
    B, T, D = h.shape
    f32 = jnp.float32
    tokens = h.reshape(-1, PEER_TOKEN_BLOCK, D)

    def token_block(xt):
        q = (xt @ wq).astype(f32).reshape(PEER_TOKEN_BLOCK, PEER_HEADS, 2, PEER_DKEY // 2)
        s = jnp.einsum('thcd,hckd->thck', q, sub_keys.astype(f32))
        top_s, top_i = lax.top_k(s, PEER_TOPK)
        cand = top_s[:, :, 0, :, None] + top_s[:, :, 1, None, :]
        best_s, best_c = lax.top_k(cand.reshape(PEER_TOKEN_BLOCK, PEER_HEADS, PEER_TOPK * PEER_TOPK), PEER_TOPK)
        i1 = jnp.take_along_axis(top_i[:, :, 0], best_c // PEER_TOPK, axis=-1)
        i2 = jnp.take_along_axis(top_i[:, :, 1], best_c % PEER_TOPK, axis=-1)
        expert = i1 * PEER_NKEYS + i2
        w = jax.nn.softmax(best_s, axis=-1)
        act = jax.nn.gelu(jnp.einsum('thkd,td->thk', u[expert].astype(f32), xt.astype(f32)))
        return jnp.einsum('thk,thkd->td', w * act, v[expert].astype(f32))

    return lax.map(token_block, tokens).reshape(B, T, D).astype(h.dtype)

def second_inputs(seed: int = 0) -> dict:
    key = jax.random.key(seed)
    ks = jax.random.split(key, 21)
    n = jax.random.normal
    f32 = jnp.float32

    def gain(k, shape):
        return 1.0 + 0.02 * n(k, shape, f32)

    return {
        'x': n(ks[0], (BATCH, SEQ, D_MODEL), f32),
        'p': n(ks[1], (DEPTH, BATCH, SEQ, PLE_DIM), f32),
        'mix_norm': gain(ks[2], (DEPTH, D_MODEL)),
        'w_in': n(ks[3], (DEPTH, D_MODEL, D_IN), f32) * D_MODEL ** -0.5,
        'hg_lb_logits': 0.1 * n(ks[4], (DEPTH + 1, HG_WIDTH), f32),
        'hg_out_norm': gain(ks[5], (DEPTH, HG_WIDTH)),
        'nsa_q_norm': gain(ks[6], (DEPTH, NSA_DH)),
        'nsa_k_norm': gain(ks[7], (DEPTH, 3, NSA_DH)),
        'cmp_pe': 0.02 * n(ks[8], (DEPTH, 2, CMP_LEN, NSA_DH), f32),
        'cmp_w1': n(ks[9], (DEPTH, 2, CMP_LEN * NSA_DH, NSA_DH), f32) * (CMP_LEN * NSA_DH) ** -0.5,
        'cmp_w2': n(ks[10], (DEPTH, 2, NSA_DH, NSA_DH), f32) * NSA_DH ** -0.5,
        'nsa_out_norm': gain(ks[11], (DEPTH, NSA_WIDTH)),
        'w_out': n(ks[12], (DEPTH, D_MIX_2, D_MODEL), f32) * D_MIX_2 ** -0.5,
        'ffn_norm': gain(ks[13], (DEPTH, D_MODEL)),
        'peer_wq': n(ks[14], (DEPTH, D_MODEL, PEER_HEADS * PEER_DKEY), f32) * D_MODEL ** -0.5,
        'peer_keys': n(ks[15], (DEPTH, PEER_HEADS, 2, PEER_NKEYS, PEER_DKEY // 2), f32) * (PEER_DKEY // 2) ** -0.5,
        'peer_u': n(ks[16], (DEPTH, PEER_N, D_MODEL), f32) * D_MODEL ** -0.5,
        'peer_v': n(ks[17], (DEPTH, PEER_N, D_MODEL), f32) * PEER_HEADS ** -0.5,
        'ple_proj': n(ks[18], (DEPTH, PLE_DIM, D_MODEL), f32) * PLE_DIM ** -0.5,
        'ple_gate_norm': gain(ks[19], (DEPTH, D_MODEL)),
        'ple_gate_w': n(ks[20], (DEPTH, D_MODEL, D_MODEL), f32) * D_MODEL ** -0.5,
    }

def second_block(x, p, mix_norm, w_in, hg_lb_logits, hg_out_norm, nsa_q_norm, nsa_k_norm,
              cmp_pe, cmp_w1, cmp_w2, nsa_out_norm, w_out, ffn_norm, peer_wq, peer_keys,
              peer_u, peer_v, ple_proj, ple_gate_norm, ple_gate_w):
    lb_table = jnp.cumsum(jax.nn.softmax(hg_lb_logits.astype(jnp.float32), axis=0), axis=0)
    h = x
    for i in range(DEPTH):
        a = rmsnorm_2(h, mix_norm[i])
        proj = a @ w_in[i]
        (hg_q, hg_f, hg_i, hg_g, n_q, n_kc, n_vc, n_ks, n_vs, n_kw, n_vw, n_gate) = jnp.split(proj, SPLIT_POINTS_2, axis=-1)
        o_hg = hgrn2_mixer(hg_q, hg_f, hg_i, hg_g, lb_table[i], hg_out_norm[i])
        o_nsa = nsa_mixer(n_q, n_kc, n_vc, n_ks, n_vs, n_kw, n_vw, n_gate,
                          nsa_q_norm[i], nsa_k_norm[i], cmp_pe[i], cmp_w1[i], cmp_w2[i], nsa_out_norm[i])
        mixed = jnp.concatenate([o_hg, o_nsa], axis=-1).astype(h.dtype)
        h = h + mixed @ w_out[i]
        h = h + peer_ffn(rmsnorm_2(h, ffn_norm[i]), peer_wq[i], peer_keys[i], peer_u[i], peer_v[i])
        gate = jax.nn.sigmoid(rmsnorm_2(h, ple_gate_norm[i]) @ ple_gate_w[i])
        h = h + (p[i] @ ple_proj[i]) * gate
    return h


def setup_inputs(seed=0):
    out = dict(first_inputs(seed))
    for name, value in second_inputs(seed + 1).items():
        if name != "x":
            out[name + "_2"] = value
    return out


def reference(
    x, pre_norm_g, w_in, lambda_q1, lambda_k1, lambda_q2, lambda_k2, subln_g, conv_w, conv_b,
    w_rgate, b_rgate, w_igate, b_igate, lru_lambda, w_out, post_norm_g, p_2, mix_norm_2, w_in_2,
    hg_lb_logits_2, hg_out_norm_2, nsa_q_norm_2, nsa_k_norm_2, cmp_pe_2, cmp_w1_2, cmp_w2_2,
    nsa_out_norm_2, w_out_2, ffn_norm_2, peer_wq_2, peer_keys_2, peer_u_2, peer_v_2, ple_proj_2,
    ple_gate_norm_2, ple_gate_w_2,
):
    x = first_block(
        x, pre_norm_g, w_in, lambda_q1, lambda_k1, lambda_q2, lambda_k2, subln_g, conv_w,
        conv_b, w_rgate, b_rgate, w_igate, b_igate, lru_lambda, w_out, post_norm_g,
    )
    return second_block(
        x, p_2, mix_norm_2, w_in_2, hg_lb_logits_2, hg_out_norm_2, nsa_q_norm_2, nsa_k_norm_2,
        cmp_pe_2, cmp_w1_2, cmp_w2_2, nsa_out_norm_2, w_out_2, ffn_norm_2, peer_wq_2,
        peer_keys_2, peer_u_2, peer_v_2, ple_proj_2, ple_gate_norm_2, ple_gate_w_2,
    )


_drawn_inputs = setup_inputs


def setup_inputs(seed=0):
    import zlib

    import numpy as np

    out = dict(_drawn_inputs(seed))
    spreads = {}
    factors = {'lambda_q2': 38.515,
     'b_rgate': 8.0,
     'b_igate': 8.0,
     'mix_norm_2': 3.0,
     'hg_lb_logits_2': 8.0,
     'hg_out_norm_2': 16.321,
     'nsa_q_norm_2': 6.206,
     'nsa_k_norm_2': 6.361,
     'cmp_pe_2': 20.529,
     'nsa_out_norm_2': 31.098,
     'ffn_norm_2': 24.295,
     'ple_gate_norm_2': 200.0,
     'p_2': 2.9,
     'ple_proj_2': 2.901,
     'ple_gate_w_2': 4.114}
    for name, (base, spread) in spreads.items():
        noise = np.random.default_rng([zlib.crc32(name.encode()), seed]).standard_normal(out[name].shape)
        drawn = base * np.exp(spread * noise) if base else spread * noise
        out[name] = __import__('jax').numpy.asarray(drawn.astype(out[name].dtype))
    for name, factor in factors.items():
        out[name] = (out[name] * factor).astype(out[name].dtype)
    return out
```

```python
import math
from contextlib import ExitStack

import numpy as np

import concourse.bass as bass
from concourse import mybir

F32 = mybir.dt.float32
U32 = mybir.dt.uint32
I32 = mybir.dt.int32
ALU = mybir.AluOpType
ACT = mybir.ActivationFunctionType
AX = mybir.AxisListType.X

P = 128
SEQ = 256
D = 1024
NT = SEQ // P
KC = D // P
HALF = 512
UNIT = KC * HALF
RING = 4
EPS = 1e-6
NEG = -1e30
LOWEST = -3e38

HEADS = 8
QK = 64
SCALE1 = QK ** -0.5
LAM_INIT = 0.8 - 0.6 * math.exp(-0.3 * 0)
LRU_C = 8.0
TAPS = 4
PAD = 4
XS = SEQ + PAD
GRP = 4

HG_HEADS = 4
CH = 64
NCH = SEQ // CH
DH = 64
NKV = 2
REP = 4
NSA_HEADS = NKV * REP
CMP_LEN = 32
CMP_STRIDE = 16
NCMP = (SEQ - CMP_LEN) // CMP_STRIDE + 1
SLOPES = [2.0 ** (-8.0 * (h + 1) / NSA_HEADS) for h in range(NSA_HEADS)]
GATES = 3 * NSA_HEADS
PEER_HEADS = 8
NKEYS = 128
TOPK = 16
NSLOT = PEER_HEADS * TOPK
PLE = 256
NQW = 2 * HALF + 2 * NKV * DH + GATES
NORMED = HALF + 2 * NKV * DH

UNITS = ["xl0", "xl1", "q0", "q1", "lru", "k0", "k1", "v0", "v1", "ga0", "ga1", "gl0", "gl1",
         "wol0", "wol1", "woa0", "woa1",
         "hf", "hq", "hi", "hg", "nq", "nk", "nv", "cmp", "wp0", "wp1",
         "wq0", "wq1", "wq2", "wq3", "keys", "ple", "gw0", "gw1"]
UNIT_AT = {name: n for n, name in enumerate(UNITS)}
OUTS = ["xl0", "xl1", "q0", "q1", "k0", "k1", "v0", "v1", "ga0", "ga1", "gl0", "gl1", "wo0", "wo1",
        "hf", "hq", "hi", "hg", "nq", "nk", "nv", "wp0", "wp1", "wq0", "wq1", "wq2", "wq3", "ple0", "ple1"]
OUT_AT = {name: n for n, name in enumerate(OUTS)}

COLS = [("pre_g", KC), ("conv_w", TAPS * KC), ("conv_b", KC), ("b_r", KC), ("b_i", KC),
        ("lam", KC), ("sub_g", 1),
        ("mix_g", KC), ("ffn_g", KC), ("gate_g", KC), ("lb0", HG_HEADS), ("lb1", HG_HEADS), ("out2_g", KC),
        ("nq_g", 1), ("nk_g", 3), ("pe", 2 * CMP_LEN), ("cmp_w2", 2 * DH)]
COL_AT, NCOL = {}, 0
for _name, _width in COLS:
    COL_AT[_name] = (NCOL, NCOL + _width)
    NCOL += _width

SEMS = ["x_loaded", "cols_loaded", "rows_loaded", "lambdas_loaded", "consts_made", "identity_made",
        "unit_used", "proj_moved", "squares_summed", "std_made", "scaled", "turned", "normed", "dve_step",
        "act_step", "pool_step", "lambda_sums", "lambda_exps", "conv_done", "rgate_full", "rgate_moved",
        "igate_moved", "decay_log", "tanh_made", "mult_sq", "mult_made", "lru_done", "scores_full",
        "bias_made", "probs_made", "weights_made", "weights_turned", "turned_moved", "heads_full",
        "heads_moved", "head_sums", "head_std", "head_gated", "attn_turned", "attn_moved", "ple_full",
        "lb_shifted", "lb_exp", "post_std", "block1_done", "stored", "bias2_made", "scan_mask_made",
        "forget_made", "log_made", "shift_made", "shift_exp", "last_made", "last_exp", "recur_ready",
        "keys_turned", "keys_moved", "intra_full", "intra_moved", "intra_masked", "update_full",
        "states_made", "o_full", "o_moved", "o_sums", "o_std", "nsa_sums", "nsa_std", "nsa_scaled",
        "nsa_turned", "nsa_normed", "cmp_in", "hid_made", "cmp_full", "cmp_sums", "cmp_std", "cmp_ready",
        "cmp_turned", "cmpT_made", "cs_full", "cs_shifted", "cs_exp", "cs_ready", "cs_turned", "csT_moved",
        "co_full", "co_used", "att_full", "att_bias", "att_exp", "att_turned", "att_moved", "ao_full",
        "ao_used", "nsa_osums", "nsa_ostd", "nsa_out", "mix_turned", "mixT_made", "h_made", "pscore_full",
        "pscore_moved", "choice_step", "top_shift", "top_exp", "top_summed", "chosen", "cur_made", "pace",
        "u_free", "gelu_made", "w_made", "diag_made", "v_free", "h2_made", "ple_used", "gate_full",
        "gate_moved", "y_made"]


UPDATE_BANKS = (3, 0, 1)
NBUF = 8
BATCH = 4
DIAGS = 4
LAST_HEAD = NT * PEER_HEADS - 1


def two_blocks(nc, x, wall, cols, rows, lambdas, peer_u, peer_v, out):
    with ExitStack() as ctx:
        def sb(name, words, dt=F32):
            return ctx.enter_context(nc.sbuf_tensor(name, [P, words], dt))

        s = {n: ctx.enter_context(nc.semaphore(n)) for n in SEMS}
        unit_ready = [ctx.enter_context(nc.semaphore(f"unit_ready{i}")) for i in range(RING)]

        ring = sb("ring", RING * UNIT)
        xs = sb("xs", NT * D)
        hT = sb("hT", KC * SEQ)
        colt = sb("colt", NCOL)
        post_g = sb("post_g", D)
        ident = sb("ident", P)
        mask1 = sb("mask1", SEQ)
        stat = sb("stat", 64)
        zero = sb("zero", P)

        xl = sb("xl", KC * XS)
        xc_rg = sb("xc_rg", 2 * KC * SEQ)
        xc, rg = xc_rg[:, 0:KC * SEQ], xc_rg[:, KC * SEQ:2 * KC * SEQ]
        ig = sb("ig", KC * SEQ)
        lt = sb("lt", KC * SEQ)
        gl = sb("gl", KC * SEQ)
        qT = sb("qT", KC * SEQ)
        kT = sb("kT", KC * SEQ)
        vv = sb("vv", NT * D)
        ga = sb("ga", NT * D)
        sm = sb("sm", 2 * GRP * SEQ)
        tail = sb("tail", 2 * D)
        wT = tail[:, 0:D]
        oh = tail[:, D:D + HALF]
        osq = tail[:, D + HALF:2 * D]
        lamt = sb("lamt", 4 * QK)
        small = sb("small", 256)

        nq = sb("nq", NT * NQW)
        small2 = sb("small2", 1536)
        diag = sb("diag", DIAGS * P)

        class at2:
            key = kT[:, 0:D]
            log_f = kT[:, D:2 * D]
            cum = qT[:, 0:D]
            shift = qT[:, D:2 * D]
            q1, k2 = xc[:, 0:D], xc[:, D:2 * D]
            q3, k4 = rg[:, 0:D], rg[:, D:2 * D]
            query = ig[:, 0:D]
            scan_mask = lt[:, 0:D]
            k_tok = lt[:, D:2 * D]
            v = ga[:, 0:D]
            gate = ga[:, D:2 * D]
            intra = gl[:, 0:HALF]
            states = gl[:, HALF:4 * HALF]
            o = xl[:, 0:D]
            osq = xl[:, D:2 * D]
            nT = vv
            pe0, pe1 = lt[:, 0:HALF], lt[:, HALF:D]
            sc = sm
            pT = kT
            cT = xc
            no = ig[:, 0:D]
            tmp = ig[:, D:2 * D]
            bias = tail

        bias_c = small2[:, 0:256]
        mask_c = small2[:, 256:512]
        e_c = small2[:, 512:768]
        dist_c = small2[:, 768:800]
        dist_ci = small2[:, 800:832].bitcast(I32)
        iota16 = small2[:, 832:848]
        iota16i = small2[:, 848:864].bitcast(I32)
        gain8 = small2[:, 864:872]
        st2 = small2[:, 872:1000]
        lbt = small2[:, 1000:1032]
        hid = small2[:, 1032:1064]
        kcT = small2[:, 1064:1080]
        cmp_tok = small2[:, 1080:1336]
        last_exp = small2[:, 1336:1352]
        dots = small2[:, 1352:1384]
        acts = small2[:, 1384:1416]
        wk = small2[:, 1416:1448]
        cur = [[small2[:, 1448 + n * TOPK:1448 + (n + 1) * TOPK].bitcast(U32) for n in (2 * k, 2 * k + 1)]
               for k in range(2)]

        def choice(at, words, dt=F32):
            a = xl[:, at:at + words]
            return a if dt == F32 else a.bitcast(dt)

        halves = choice(0, 2 * NKEYS)
        pairs = choice(256, TOPK * TOPK)
        hot = choice(512, TOPK * TOPK)
        v16, i16, i16f = choice(768, 2 * TOPK), choice(800, 2 * TOPK, U32), choice(832, 2 * TOPK)
        best, best_at = choice(864, TOPK), choice(880, TOPK, U32)
        places_i, places = choice(896, 2 * TOPK, U32), choice(928, 2 * TOPK)
        keys_f = choice(960, 2 * TOPK)
        top_w = [choice(992 + n * TOPK, TOPK) for n in range(2)]
        top_sum = choice(1024, 1)
        all_experts = choice(1040, NT * NSLOT, U32)

        pp = ctx.enter_context(nc.psum_tensor("pp", [P, 2, 2, HALF], F32))
        pa = ctx.enter_context(nc.psum_tensor("pa", [P, 4 * HALF], F32))

        def col(name, n=0, k=1):
            a = COL_AT[name][0]
            return colt[:, a + n:a + n + k]

        def slot(u):
            a = (u % RING) * UNIT
            return ring[:, a:a + UNIT].rearrange("p (k n) -> p k n", k=KC)

        x3 = xs[:, :].rearrange("p (t d) -> p t d", t=NT)
        h3 = hT[:, :].rearrange("p (k n) -> p k n", k=KC)
        xl3 = xl[:, :].rearrange("p (k n) -> p k n", k=KC)
        xc3 = xc[:, :].rearrange("p (k n) -> p k n", k=KC)
        rg3 = rg[:, :].rearrange("p (k n) -> p k n", k=KC)
        ig3 = ig[:, :].rearrange("p (k n) -> p k n", k=KC)
        gl3 = gl[:, :].rearrange("p (k n) -> p k n", k=KC)
        qT3 = qT[:, :].rearrange("p (h n) -> p h n", h=HEADS)
        kT3 = kT[:, :].rearrange("p (h n) -> p h n", h=HEADS)
        v3 = vv[:, :].rearrange("p (t d) -> p t d", t=NT)
        ga3 = ga[:, :].rearrange("p (t d) -> p t d", t=NT)
        pa8 = pa[:, :].rearrange("p (k n) -> p k n", k=8)

        ring_free = [(UNIT_AT["keys"] % RING) * UNIT, (UNIT_AT["ple"] % RING) * UNIT]
        rows_at = [ring[:, a + n * D:a + (n + 1) * D] for a in ring_free for n in range(4)] \
            + [b[:, n * D:(n + 1) * D] for b in (ga, gl, sm, tail) for n in range(2)]
        u_rows, v_rows = rows_at[:NBUF], rows_at[NBUF:]
        u_here = [ctx.enter_context(nc.semaphore(f"u_here{i}")) for i in range(NBUF)]
        v_here = [ctx.enter_context(nc.semaphore(f"v_here{i}")) for i in range(NBUF)]

        nq3 = nq[:, :].rearrange("p (t n) -> p t n", t=NT)
        nT3 = at2.nT[:, :].rearrange("p (k n) -> p k n", k=KC)
        def peer_q(j):
            return (qT if j < PEER_HEADS else kT)[:, (j % PEER_HEADS) * SEQ:(j % PEER_HEADS + 1) * SEQ]

        STEPS2 = [(t, w) for t in range(NT) for w in range(2)]

        def score2(buf, t):
            return buf[:, :].rearrange("p (h n) -> p h n", h=NSA_HEADS)[:, :, 0:P * (t + 1)]

        STEPS = [(g, t) for g in range(HEADS // GRP) for t in range(NT)]

        def score_bank(t):
            n = P * (t + 1)
            return pa[:, :].rearrange("p (c h n) -> p c h n", c=2, h=GRP)[:, :, :, 0:n]

        def score_sbuf(t):
            n = P * (t + 1)
            return sm[:, :].rearrange("p (c h n) -> p c h n", c=2, h=GRP)[:, :, :, 0:n]

        block = ctx.enter_context(nc.Block())

        @block.sync
        def _(sp):
            sp.dma_start(x3, x.rearrange("(t p) d -> p t d", p=P)).then_inc(s["x_loaded"], 16)
            sp.dma_start(colt[:, :], cols).then_inc(s["cols_loaded"], 16)
            for u in range(len(UNITS)):
                if u >= RING:
                    sp.wait_ge(s["unit_used"], u - RING + 1)
                a = (u % RING) * UNIT
                sp.dma_start(ring[:, a:a + UNIT], wall[u]).then_inc(unit_ready[u % RING], 16)
            for t in range(NT):
                sp.wait_ge(s["y_made"], t + 1)
                sp.dma_start(out[t * P:(t + 1) * P, :], x3[:, t, :]).then_inc(s["stored"], 16)
            sp.wait_ge(s["stored"], 16 * NT)

        @block.gpsimd
        def _(pool):
            def step(ins):
                step.n += 1
                ins.then_inc(s["pool_step"], 1)
                pool.wait_ge(s["pool_step"], step.n)
            step.n = 0

            pool.dma_start(lamt[:, :], lambdas.broadcast_to([P, 4 * QK])).then_inc(s["lambdas_loaded"], 16)
            pool.dma_start(post_g[:, :], rows[0:1, :].broadcast_to([P, D])).then_inc(s["rows_loaded"], 16)
            nc.gpsimd.memset(ident[:, :], 0.0)
            nc.gpsimd.memset(zero[:, :], 0.0)
            step(nc.gpsimd.memset(mask1[:, :], 0.0))
            nc.gpsimd.affine_select(out=ident[:, :], in_=ident[:, :], compare_op=ALU.not_equal, fill=1.0,
                                    base=0, pattern=[[-1, P]], channel_multiplier=1).then_inc(s["identity_made"], 1)
            nc.gpsimd.affine_select(out=mask1[:, :], in_=mask1[:, :], compare_op=ALU.is_ge, fill=NEG,
                                    base=P, pattern=[[-1, SEQ]], channel_multiplier=1).then_inc(s["consts_made"], 1)
            nc.gpsimd.iota(dist_ci.rearrange("p (t n) -> p t n", t=NT), pattern=[[P, NT], [-CMP_STRIDE, 16]],
                           base=1 - CMP_LEN, channel_multiplier=1)
            step(nc.gpsimd.iota(iota16i, pattern=[[1, 16]], base=0, channel_multiplier=0))
            nc.gpsimd.tensor_copy(iota16, iota16i)
            step(nc.gpsimd.tensor_copy(dist_c, dist_ci))
            bc = bias_c.rearrange("p (g t r n) -> p g t r n", g=NKV, t=NT, r=REP)
            mc = mask_c.rearrange("p (g t r n) -> p g t r n", g=NKV, t=NT, r=REP)
            dc = dist_c.rearrange("p (t n) -> p t n", t=NT)
            for h in range(NSA_HEADS):
                ins = nc.gpsimd.tensor_scalar(mc[:, h // REP, :, h % REP, :], dc, 0.0, None, ALU.is_ge)
            step(ins)
            step(nc.gpsimd.affine_select(out=dist_c, in_=dist_c, compare_op=ALU.is_ge, fill=-NEG, base=1 - CMP_LEN,
                                         pattern=[[P, NT], [-CMP_STRIDE, 16]], channel_multiplier=1))
            for h in range(NSA_HEADS):
                ins = nc.gpsimd.tensor_scalar(bc[:, h // REP, :, h % REP, :], dc, -SLOPES[h], None, ALU.mult)
            step(ins)
            pool.wait_ge(s["block1_done"], 1)
            b3 = at2.bias[:, :].rearrange("p (h n) -> p h n", h=NSA_HEADS)
            step(nc.gpsimd.iota(b3[:, 7, :].bitcast(I32), pattern=[[-1, SEQ]], base=P, channel_multiplier=1))
            step(nc.gpsimd.tensor_copy(mask1[:, :], b3[:, 7, :].bitcast(I32)))
            step(nc.gpsimd.affine_select(out=mask1[:, :], in_=mask1[:, :], compare_op=ALU.is_ge, fill=-NEG,
                                         base=P, pattern=[[-1, SEQ]], channel_multiplier=1))
            step(nc.gpsimd.memset(at2.scan_mask, 1.0))
            nc.gpsimd.memset(at2.scan_mask.rearrange("p (c n) -> p c n", n=CH)[:, :, 0:1], 0.0)\
                .then_inc(s["scan_mask_made"], 1)
            for h in range(NSA_HEADS):
                ins = nc.gpsimd.tensor_scalar(b3[:, h, :], mask1[:, :], -SLOPES[h], None, ALU.mult)
            ins.then_inc(s["bias2_made"], 1)
            pool.wait_ge(s["block1_done"], NT)
            pool.dma_start(post_g[:, :], rows[1:2, :].broadcast_to([P, D])).then_inc(s["rows_loaded"], 16)
            pool.wait_ge(s["bias2_made"], 1)
            pool.wait_ge(s["intra_moved"], 1)
            for half in range(2):
                if half:
                    pool.wait_ge(s["intra_masked"], 1)
                a = at2.intra[half * CH:(half + 1) * CH, :].rearrange("p (c n) -> p c n", n=CH)
                nc.gpsimd.affine_select(out=a, in_=a, compare_op=ALU.is_ge, fill=0.0, base=0,
                                        pattern=[[0, HG_HEADS * NT], [1, CH]], channel_multiplier=-1)\
                    .then_inc(s["intra_masked"], 1)

            pool.wait_ge(s["intra_masked"], 2)
            def indices(kind, parity, head):
                pool.wait_ge(s["chosen"], head + 1)
                pool.sem_inc(s["pace"], 1)
                nc.gpsimd.tensor_copy(cur[kind][parity], all_experts[:, bass.ds(head * TOPK, TOPK)])\
                    .then_inc(s["cur_made"], 1)

            def gather(kind, parity, head, k):
                table, rows_to, here, free = ((peer_u, u_rows, u_here, "u_free"),
                                              (peer_v, v_rows, v_here, "v_free"))[kind]
                if k % BATCH == 0:
                    pool.wait_ge(s[free], head * TOPK + k + BATCH)
                    pool.sem_inc(s["pace"], 1)
                nc.gpsimd.indirect_dma_start(out=rows_to[k % NBUF], out_offset=None, in_=table,
                                             in_offset=bass.IndirectOffsetOnAxis(ap=cur[kind][parity][:, k:k + 1], axis=0))\
                    .then_inc(here[k % NBUF], 16)

            def gather_step(n, parity):
                indices(0, parity, n + 1)
                indices(1, parity, n)
                pool.wait_ge(s["cur_made"], 2 * n + 3)
                for k in range(TOPK):
                    gather(0, parity, n + 1, k)
                    gather(1, parity, n, k)

            pool.wait_ge(s["unit_used"], UNIT_AT["ple"] + 1)
            indices(0, 1, 0)
            pool.wait_ge(s["cur_made"], 1)
            for k in range(TOPK):
                gather(0, 1, 0, k)
            last = LAST_HEAD
            with pool.Fori(0, last // 2) as pair:
                for parity in range(2):
                    gather_step(pair * 2 + parity, parity)
            gather_step(last - 1, 0)
            indices(1, 1, last)
            pool.wait_ge(s["cur_made"], 2 * last + 2)
            for k in range(TOPK):
                gather(1, 1, last, k)

        @block.tensor
        def _(pe):
            outs = [0]

            def begin_output():
                if outs[0] >= 2:
                    pe.wait_ge(s["proj_moved"], outs[0] - 1)
                buf = pp[:, outs[0] % 2]
                outs[0] += 1
                return buf

            def take_unit(name):
                u = UNIT_AT[name]
                pe.wait_ge(unit_ready[u % RING], 16 * (u // RING + 1))
                return slot(u)

            def turn_norm(m, src):
                pe.wait_ge(s["scaled"], m + 1)
                for k in range(KC):
                    ins = nc.tensor.transpose(pa[:, (m % NT) * D + k * P:(m % NT) * D + (k + 1) * P],
                                              src[:, k * P:(k + 1) * P], ident[:, :])
                ins.then_inc(s["turned"], 1)

            def feature_major(name):
                w = take_unit(name)
                buf = begin_output().rearrange("p a (b n) -> p (a b) n", b=2)
                for c in range(4):
                    for k in range(KC):
                        ins = nc.tensor.matmul(buf[:, c, :], w[:, k, c * P:(c + 1) * P], h3[:, k, :],
                                               start=(k == 0), stop=(k == KC - 1))
                return ins

            def token_major(name, width=HALF):
                w = take_unit(name)
                buf = begin_output()
                for t in range(NT):
                    for k in range(KC):
                        ins = nc.tensor.matmul(buf[:, t, 0:width], h3[:, k, t * P:(t + 1) * P], w[:, k, 0:width],
                                               start=(k == 0), stop=(k == KC - 1))
                return ins

            def done(ins, name):
                ins.then_inc(s["unit_used"], 1)

            def scores(a):
                g, t = STEPS[a]
                if a == 0:
                    pe.wait_ge(s["igate_moved"], 1)
                    pe.wait_ge(s["proj_moved"], OUT_AT["k1"] + 1)
                else:
                    pe.wait_ge(s["turned_moved"], a)
                    pe.wait_ge(s["heads_moved"], a)
                n = P * (t + 1)
                for c in range(2):
                    for h in range(GRP):
                        ins = nc.tensor.matmul(score_bank(t)[:, c, h, :],
                                               qT3[c * QK:(c + 1) * QK, g * GRP + h, t * P:(t + 1) * P],
                                               kT3[c * QK:(c + 1) * QK, g * GRP + h, 0:n], start=True, stop=True)
                ins.then_inc(s["scores_full"], 1)

            def turn_weights(a):
                g, t = STEPS[a]
                pe.wait_ge(s["weights_made"], a + 1)
                for h in range(GRP):
                    for kb in range(t + 1):
                        n = h * (t + 1) + kb
                        ins = nc.tensor.transpose(pa[:, n * P:(n + 1) * P],
                                                  score_sbuf(t)[:, 0, h, kb * P:(kb + 1) * P], ident[:, :])
                ins.then_inc(s["weights_turned"], 1)

            def values(a):
                g, t = STEPS[a]
                pe.wait_ge(s["turned_moved"], a + 1)
                pe.wait_ge(s["proj_moved"], OUT_AT["v1"] + 1)
                for h in range(GRP):
                    for kb in range(t + 1):
                        n = h * (t + 1) + kb
                        ins = nc.tensor.matmul(pa[:, 2 * HALF + h * P:2 * HALF + (h + 1) * P],
                                               wT[:, n * P:(n + 1) * P],
                                               v3[:, kb, (g * GRP + h) * P:(g * GRP + h + 1) * P],
                                               start=(kb == 0), stop=(kb == t))
                ins.then_inc(s["heads_full"], 1)

            pe.wait_ge(s["identity_made"], 1)
            for t in range(NT):
                turn_norm(t, vv[:, t * D:(t + 1) * D])
            pe.wait_ge(s["normed"], NT)
            for name in ("xl0", "xl1", "q0", "q1"):
                done(feature_major(name), name)
            w = take_unit("lru").rearrange("p k n -> p (k n)")
            pe.wait_ge(s["conv_done"], 1)
            for n in range(KC):
                ins = nc.tensor.matmul(pa8[:, n, :], w[:, n * P:(n + 1) * P], xc3[:, n, :], start=True, stop=True)
            ins.then_inc(s["rgate_full"], 1)
            pe.wait_ge(s["rgate_moved"], 1)
            for n in range(KC):
                ins = nc.tensor.matmul(pa8[:, n, :], w[:, D + n * P:D + (n + 1) * P], xc3[:, n, :],
                                       start=True, stop=True)
            ins.then_inc(s["unit_used"], 1)
            for name in ("k0", "k1"):
                done(feature_major(name), name)
            for name in ("v0", "v1"):
                done(token_major(name), name)
            for a, name in enumerate(("ga0", "ga1", "gl0", "gl1")):
                scores(a)
                done(token_major(name) if name[:2] == "ga" else feature_major(name), name)
                turn_weights(a)
                values(a)
            bufs = [begin_output(), begin_output()]
            pe.wait_ge(s["lru_done"], 1)
            for c in range(2):
                w = take_unit(f"wol{c}")
                for t in range(NT):
                    for k in range(KC):
                        ins = nc.tensor.matmul(bufs[c][:, t, :], gl3[:, k, t * P:(t + 1) * P], w[:, k, :],
                                               start=(k == 0), stop=False)
                ins.then_inc(s["unit_used"], 1)
            for t in range(NT):
                pe.wait_ge(s["head_gated"], NT + 1 + t)
                if t == 0:
                    pe.wait_ge(s["heads_moved"], len(STEPS))
                for k in range(KC):
                    ins = nc.tensor.transpose(pa[:, t * D + k * P:t * D + (k + 1) * P],
                                              ga3[:, t, k * P:(k + 1) * P], ident[:, :])
                ins.then_inc(s["attn_turned"], 1)
            pe.wait_ge(s["attn_moved"], NT)
            for c in range(2):
                w = take_unit(f"woa{c}")
                for t in range(NT):
                    for k in range(KC):
                        ins = nc.tensor.matmul(bufs[c][:, t, :], h3[:, k, t * P:(t + 1) * P], w[:, k, :],
                                               start=False, stop=(k == KC - 1))
                ins.then_inc(s["unit_used"], 1)


            for t in range(NT):
                turn_norm(2 + t, vv[:, t * D:(t + 1) * D])
            pe.wait_ge(s["normed"], 2 * NT)
            for name in ("hf", "hq"):
                done(feature_major(name), name)
            for name in ("hi", "hg", "nq"):
                done(token_major(name), name)
            pe.wait_ge(s["recur_ready"], 1)
            for h in range(HG_HEADS):
                for t in range(NT):
                    n = h * NT + t
                    ins = nc.tensor.transpose(pa[:, n * P:(n + 1) * P],
                                              at2.k4[:, h * SEQ + t * P:h * SEQ + (t + 1) * P], ident[:, :])
            ins.then_inc(s["keys_turned"], 1)
            for h in range(HG_HEADS):
                for c in range(NCH):
                    a = h * SEQ + c * CH
                    o = 2 * HALF + (h * NT + c // 2) * CH
                    half = slice((c % 2) * CH, (c % 2 + 1) * CH)
                    ins = nc.tensor.matmul(pa[half, o:o + CH], at2.k2[:, a:a + CH], at2.q1[:, a:a + CH],
                                           start=True, stop=True)
            ins.then_inc(s["intra_full"], 1)
            done(token_major("nk"), "nk")
            pe.wait_ge(s["keys_moved"], 1)
            pe.wait_ge(s["proj_moved"], OUT_AT["hi"] + 1)
            for c, bank in enumerate(UPDATE_BANKS):
                half = slice((c % 2) * CH, (c % 2 + 1) * CH)
                for h in range(HG_HEADS):
                    n = h * NT + c // 2
                    ins = nc.tensor.matmul(pa[:, bank * HALF + h * P:bank * HALF + (h + 1) * P],
                                           at2.k_tok[half, n * P:(n + 1) * P],
                                           at2.v[half, (c // 2) * HALF + h * P:(c // 2) * HALF + (h + 1) * P],
                                           start=True, stop=True)
            ins.then_inc(s["update_full"], 1)
            done(token_major("nv", NQW - 2 * HALF), "nv")
            pe.wait_ge(s["intra_masked"], 2)
            pe.wait_ge(s["states_made"], 1)
            for c in range(NCH):
                half = slice((c % 2) * CH, (c % 2 + 1) * CH)
                for h in range(HG_HEADS):
                    o = pa[half, c * HALF + h * P:c * HALF + (h + 1) * P]
                    n = (h * NT + c // 2) * CH
                    ins = nc.tensor.matmul(o, at2.intra[half, n:n + CH],
                                           at2.v[half, (c // 2) * HALF + h * P:(c // 2) * HALF + (h + 1) * P],
                                           start=True, stop=(c == 0))
                    if c:
                        a = h * SEQ + c * CH
                        ins = nc.tensor.matmul(o, at2.q3[:, a:a + CH],
                                               at2.states[:, (c - 1) * HALF + h * P:(c - 1) * HALF + (h + 1) * P],
                                               start=False, stop=True)
            ins.then_inc(s["o_full"], 1)

            pe.wait_ge(s["o_moved"], 1)
            for t in range(NT):
                pe.wait_ge(s["nsa_scaled"], t + 1)
                for k in range(KC):
                    ins = nc.tensor.transpose(pa[:, t * D + k * P:t * D + (k + 1) * P],
                                              nq3[:, t, k * P:(k + 1) * P], ident[:, :])
                ins.then_inc(s["nsa_turned"], 1)
            w = take_unit("cmp").rearrange("p k n -> p (k n)")
            pe.wait_ge(s["cmp_in"], 1)
            for g in range(NKV):
                half = slice(g * DH, (g + 1) * DH)
                for kv in range(2):
                    for j in range(CMP_LEN):
                        src = (at2.pe0 if j < CMP_STRIDE else at2.pe1)[half, kv * SEQ:(kv + 1) * SEQ]
                        a = j if j >= CMP_STRIDE else j
                        n = (kv * CMP_LEN + j) * DH
                        ins = nc.tensor.matmul(pa[half, g * HALF + kv * 16:g * HALF + kv * 16 + NCMP],
                                               w[half, n:n + DH],
                                               src[:, a:a + CMP_STRIDE * (NCMP - 1) + 1:CMP_STRIDE],
                                               start=(j == 0), stop=(j == CMP_LEN - 1))
            ins.then_inc(s["unit_used"], 1)
            pe.wait_ge(s["hid_made"], 1)
            for g in range(NKV):
                half = slice(g * DH, (g + 1) * DH)
                for kv in range(2):
                    ins = nc.tensor.matmul(pa[0:NCMP, (2 + g) * HALF + kv * DH:(2 + g) * HALF + (kv + 1) * DH],
                                           hid[half, kv * 16:kv * 16 + NCMP], col("cmp_w2", kv * DH, DH)[half, :],
                                           start=True, stop=True)
            ins.then_inc(s["cmp_full"], 1)
            pe.wait_ge(s["cmp_ready"], 1)
            nc.tensor.transpose(pa[:, 0:NCMP], cmp_tok[0:NCMP, 0:P], ident[0:NCMP, 0:NCMP])\
                .then_inc(s["cmp_turned"], 1)
            pe.wait_ge(s["cmpT_made"], 1)
            for g in range(NKV):
                half = slice(g * DH, (g + 1) * DH)
                for t in range(NT):
                    for r in range(REP):
                        a = g * HALF + (t * REP + r) * 16
                        ins = nc.tensor.matmul(pa[:, a:a + NCMP], nT3[half, r, t * P:(t + 1) * P],
                                               kcT[half, 0:NCMP], start=True, stop=True)
            ins.then_inc(s["cs_full"], 1)
            pe.wait_ge(s["cs_ready"], 1)
            for n in range(NT * NSA_HEADS):
                ins = nc.tensor.transpose(pa[0:NCMP, n * P:(n + 1) * P], e_c[:, n * 16:n * 16 + NCMP], ident[:, :])
            ins.then_inc(s["cs_turned"], 1)
            pe.wait_ge(s["csT_moved"], 1)
            for t in range(NT):
                for h in range(NSA_HEADS):
                    n = (h // REP * NT + t) * REP + h % REP
                    ins = nc.tensor.matmul(pa[:, t * HALF + h * DH:t * HALF + (h + 1) * DH],
                                           at2.cT[0:NCMP, n * P:(n + 1) * P],
                                           cmp_tok[0:NCMP, P + h // REP * DH:P + (h // REP + 1) * DH],
                                           start=True, stop=True)
            ins.then_inc(s["co_full"], 1)
            for b, (t, w) in enumerate(STEPS2):
                if b == 0:
                    pe.wait_ge(s["co_used"], 1)
                else:
                    pe.wait_ge(s["ao_used"], b)
                for h in range(NSA_HEADS):
                    half = slice(h // REP * DH, (h // REP + 1) * DH)
                    ins = nc.tensor.matmul(score2(pa, t)[:, h, :], nT3[half, h % REP, t * P:(t + 1) * P],
                                           nT3[half, 4 + w, 0:(t + 1) * P], start=True, stop=True)
                ins.then_inc(s["att_full"], 1)
                pe.wait_ge(s["att_exp"], b + 1)
                for h in range(NSA_HEADS):
                    for kb in range(t + 1):
                        n = h * (t + 1) + kb
                        ins = nc.tensor.transpose(pa[:, n * P:(n + 1) * P],
                                                  score2(at2.sc, t)[:, h, kb * P:(kb + 1) * P], ident[:, :])
                ins.then_inc(s["att_turned"], 1)
                pe.wait_ge(s["att_moved"], b + 1)
                for h in range(NSA_HEADS):
                    for kb in range(t + 1):
                        n = h * (t + 1) + kb
                        a = D + w * P + h // REP * DH
                        ins = nc.tensor.matmul(pa[:, h * DH:(h + 1) * DH], at2.pT[:, n * P:(n + 1) * P],
                                               nq3[:, kb, a:a + DH], start=(kb == 0), stop=(kb == t))
                ins.then_inc(s["ao_full"], 1)

            pe.wait_ge(s["ao_used"], len(STEPS2))
            for t in range(NT):
                pe.wait_ge(s["nsa_out"], t + 1)
                for k in range(KC):
                    src = at2.o if k < 4 else at2.no
                    a = t * HALF + (k % 4) * P
                    ins = nc.tensor.transpose(pa[:, t * D + k * P:t * D + (k + 1) * P], src[:, a:a + P], ident[:, :])
                ins.then_inc(s["mix_turned"], 1)
            pe.wait_ge(s["mixT_made"], NT)
            for name in ("wp0", "wp1"):
                done(token_major(name), name)

            for t in range(NT):
                turn_norm(4 + t, vv[:, t * D:(t + 1) * D])
            pe.wait_ge(s["normed"], 3 * NT)
            for c in range(4):
                done(feature_major(f"wq{c}"), f"wq{c}")
            w = take_unit("keys").rearrange("p k n -> p (k n)")
            pe.wait_ge(s["proj_moved"], OUT_AT["wq3"] + 1)
            for t in range(NT):
                if t:
                    pe.wait_ge(s["pscore_moved"], t)
                for j in range(2 * PEER_HEADS):
                    ins = nc.tensor.matmul(pa[:, j * P:(j + 1) * P], peer_q(j)[:, t * P:(t + 1) * P],
                                           w[:, j * NKEYS:(j + 1) * NKEYS], start=True, stop=True)
                if t == 0:
                    ins.then_inc(s["pscore_full"], 1)
            ins.then_inc(s["unit_used"], 1)
            w = take_unit("ple").rearrange("p k n -> p (k n)")
            for c in range(2):
                buf = begin_output()
                for t in range(NT):
                    for k in range(PLE // P):
                        ins = nc.tensor.matmul(buf[:, t, :], w[:, 2 * D + k * SEQ + t * P:2 * D + k * SEQ + (t + 1) * P],
                                               w[:, k * D + c * HALF:k * D + (c + 1) * HALF],
                                               start=(k == 0), stop=(k == PLE // P - 1))
                ins.then_inc(s["ple_full"], 1)
            pe.wait_ge(s["ple_used"], 1)
            for t in range(NT):
                for c in range(2):
                    ins = nc.tensor.matmul(pp[:, t, c, :], ident[:, :], x3[:, t, c * HALF:(c + 1) * HALF],
                                           start=True, stop=True)
            ins.then_inc(s["unit_used"], 1)
            for t in range(NT):
                with pe.Fori(0, PEER_HEADS // 2) as pair:
                    for odd in range(2):
                        head = t * PEER_HEADS + pair * 2 + odd
                        for k in range(TOPK):
                            pe.wait_ge(s["diag_made"], head * TOPK + k + 1)
                            pe.wait_ge(v_here[k % NBUF], (head * 2 + k // NBUF + 1) * 16)
                            n = k % DIAGS
                            for c in range(2):
                                ins = nc.tensor.matmul(pp[:, t, c, :], diag[:, n * P:(n + 1) * P],
                                                       v_rows[k % NBUF][:, c * HALF:(c + 1) * HALF],
                                                       start=False, stop=True, skip_group_check=True)
                            ins.then_inc(s["v_free"], 1)

            for t in range(NT):
                turn_norm(6 + t, vv[:, t * D:(t + 1) * D])
            pe.wait_ge(s["normed"], 4 * NT)
            for c in range(2):
                w = take_unit(f"gw{c}")
                for t in range(NT):
                    for k in range(KC):
                        ins = nc.tensor.matmul(pp[:, c, t, :], h3[:, k, t * P:(t + 1) * P], w[:, k, :],
                                               start=(k == 0), stop=(k == KC - 1))
                ins.then_inc(s["gate_full"], 1)

        @block.scalar
        def _(act):
            def full(name):
                unit = {"wo0": "woa0", "wo1": "woa1"}.get(name, name)
                act.wait_ge(s["unit_used"], UNIT_AT[unit] + 1)
                return pp[:, OUT_AT[name] % 2]

            def step(ins):
                step.n += 1
                ins.then_inc(s["act_step"], 1)
                act.wait_ge(s["act_step"], step.n)
            step.n = 0

            def move(name, dst, func=ACT.Copy, width=HALF):
                nc.scalar.activation(dst, full(name)[:, :, 0:width], func).then_inc(s["proj_moved"], 1)

            def norm_std(m):
                act.wait_ge(s["squares_summed"], m + 1)
                nc.scalar.activation(stat[:, 16 + m:17 + m], stat[:, m:m + 1], ACT.Sqrt, bias=eps_col, scale=1.0 / D)\
                    .then_inc(s["std_made"], 1)

            eps_col = small[:, 250:251]
            for t in range(NT):
                norm_std(t)
            for c in range(2):
                nc.scalar.activation(xl3[:, 4 * c:4 * c + 4, PAD:XS],
                                     full(f"xl{c}").rearrange("p a (b n) -> p (a b) n", b=2), ACT.Copy)\
                    .then_inc(s["proj_moved"], 1)
            act.wait_ge(s["lambda_sums"], 1)
            nc.scalar.activation(small[:, 2:4], small[:, 0:2], ACT.Exp)
            nc.scalar.activation(small[:, 16:24], small[:, 8:16], ACT.Exp, scale=-1.0).then_inc(s["lambda_exps"], 1)
            for c in range(2):
                move(f"q{c}", qT[:, c * D:(c + 1) * D].rearrange("p (a n) -> p a n", a=2))
            act.wait_ge(s["rgate_full"], 1)
            for n in range(KC):
                ins = nc.scalar.activation(rg3[:, n, :], pa8[:, n, :], ACT.Sigmoid, bias=col("b_r", n))
            ins.then_inc(s["rgate_moved"], 1)
            act.wait_ge(s["unit_used"], UNIT_AT["lru"] + 1)
            for n in range(KC):
                ins = nc.scalar.activation(ig3[:, n, :], pa8[:, n, :], ACT.Sigmoid, bias=col("b_i", n))
            ins.then_inc(s["igate_moved"], 1)
            act.wait_ge(s["decay_log"], 1)
            nc.scalar.activation(lt[:, :], rg[:, :], ACT.Tanh).then_inc(s["tanh_made"], 1)
            step(nc.scalar.activation(xl[:, 0:KC * SEQ], rg[:, :], ACT.Exp, scale=-1.0))
            for c in range(2):
                move(f"k{c}", kT[:, c * D:(c + 1) * D].rearrange("p (a n) -> p a n", a=2))
            act.wait_ge(s["mult_sq"], 1)
            nc.scalar.activation(lt[:, :], lt[:, :], ACT.Sqrt, scale=2.0).then_inc(s["mult_made"], 1)
            for c in range(2):
                move(f"v{c}", v3[:, :, c * HALF:(c + 1) * HALF])
            for a, name in enumerate(("ga0", "ga1", "gl0", "gl1")):
                g, t = STEPS[a]
                act.wait_ge(s["bias_made"], a + 1)
                for n in range(2 * GRP):
                    src = score_sbuf(t)[:, n // GRP, n % GRP, :]
                    ins = nc.scalar.activation(src, src, ACT.Exp, bias=small[:, 40 + n:41 + n], scale=SCALE1,
                                               accum_out=small[:, 48 + n:49 + n])
                ins.then_inc(s["probs_made"], 1)
                if name[:2] == "ga":
                    move(name, ga3[:, :, (a % 2) * HALF:(a % 2 + 1) * HALF], ACT.Silu)
                else:
                    c = a % 2
                    move(name, gl[:, c * D:(c + 1) * D].rearrange("p (a n) -> p a n", a=2), ACT.Silu)
                act.wait_ge(s["weights_turned"], a + 1)
                n = GRP * (t + 1) * P
                nc.scalar.activation(wT[:, 0:n], pa[:, 0:n], ACT.Copy).then_inc(s["turned_moved"], 1)
                act.wait_ge(s["heads_full"], a + 1)
                if a:
                    act.wait_ge(s["head_gated"], a)
                nc.scalar.activation(oh[:, :], pa[:, 2 * HALF:3 * HALF], ACT.Copy).then_inc(s["heads_moved"], 1)
                act.wait_ge(s["head_sums"], a + 1)
                nc.scalar.activation(small[:, 64:68], small[:, 60:64], ACT.Sqrt, bias=eps_col, scale=1.0 / P)\
                    .then_inc(s["head_std"], 1)
            for t in range(NT):
                act.wait_ge(s["attn_turned"], t + 1)
                nc.scalar.activation(h3[:, :, t * P:(t + 1) * P],
                                     pa[:, t * D:(t + 1) * D].rearrange("p (k n) -> p k n", k=KC),
                                     ACT.Copy, scale=small[:, 80:81]).then_inc(s["attn_moved"], 1)
            act.wait_ge(s["lru_done"], 1)
            full("wo0")
            full("wo1")
            for t in range(NT):
                step(nc.scalar.activation(xc[:, t * D:(t + 1) * D].rearrange("p (c n) -> p c n", c=2),
                                          pp[:, :, t, :], ACT.Square, accum_out=stat[:, 32 + t:33 + t]))
                ins = nc.scalar.activation(vv[:, t * D:(t + 1) * D].rearrange("p (c n) -> p c n", c=2),
                                           pp[:, :, t, :], ACT.Copy)
                if t == NT - 1:
                    ins.then_inc(s["proj_moved"], 2)
                nc.scalar.activation(stat[:, 34 + t:35 + t], stat[:, 32 + t:33 + t], ACT.Sqrt, bias=eps_col,
                                     scale=1.0 / D).then_inc(s["post_std"], 1)


            for t in range(NT):
                norm_std(2 + t)
            nc.scalar.activation(at2.key.rearrange("p (a n) -> p a n", a=2), full("hf"), ACT.Sigmoid)\
                .then_inc(s["proj_moved"], 1)
            act.wait_ge(s["lb_shifted"], 1)
            nc.scalar.activation(lbt[:, 4:12], lbt[:, 4:12], ACT.Exp).then_inc(s["lb_exp"], 1)
            move("hq", at2.query.rearrange("p (a n) -> p a n", a=2), ACT.Silu)
            act.wait_ge(s["forget_made"], 1)
            nc.scalar.activation(at2.log_f, at2.key, ACT.Ln).then_inc(s["log_made"], 1)
            move("hi", at2.v.rearrange("p (a n) -> p a n", a=2))
            move("hg", at2.gate.rearrange("p (a n) -> p a n", a=2), ACT.Silu)
            act.wait_ge(s["shift_made"], 1)
            nc.scalar.activation(at2.q1, at2.shift, ACT.Exp)
            nc.scalar.activation(at2.k2, at2.shift, ACT.Exp, scale=-1.0)
            nc.scalar.activation(at2.q3, at2.cum, ACT.Exp)
            nc.scalar.activation(last_exp, at2.cum[:, CH - 1::CH], ACT.Exp).then_inc(s["shift_exp"], 1)
            act.wait_ge(s["last_made"], 1)
            nc.scalar.activation(at2.k4, at2.shift, ACT.Exp).then_inc(s["last_exp"], 1)
            move("nq", nq3[:, :, 0:HALF])
            act.wait_ge(s["keys_turned"], 1)
            nc.scalar.activation(at2.k_tok, pa[:, 0:D], ACT.Copy).then_inc(s["keys_moved"], 1)
            act.wait_ge(s["intra_full"], 1)
            nc.scalar.activation(at2.intra, pa[:, 2 * HALF:3 * HALF], ACT.Copy).then_inc(s["intra_moved"], 1)
            move("nk", nq3[:, :, HALF:2 * HALF])
            buf = full("nv")
            nc.scalar.activation(nq3[:, :, NQW - GATES:NQW], buf[:, :, 2 * NKV * DH:2 * NKV * DH + GATES], ACT.Sigmoid)
            nc.scalar.activation(nq3[:, :, D:NQW - GATES], buf[:, :, 0:2 * NKV * DH], ACT.Copy)\
                .then_inc(s["proj_moved"], 1)
            act.wait_ge(s["o_full"], 1)
            for c in range(NCH):
                half = slice((c % 2) * CH, (c % 2 + 1) * CH)
                ins = nc.scalar.activation(at2.o[half, (c // 2) * HALF:(c // 2 + 1) * HALF],
                                           pa[half, c * HALF:(c + 1) * HALF], ACT.Copy)
            ins.then_inc(s["o_moved"], 1)
            for t in range(NT):
                act.wait_ge(s["nsa_sums"], t + 1)
                nc.scalar.activation(st2[:, 16 + 12 * t:28 + 12 * t], st2[:, 40 + 12 * t:52 + 12 * t], ACT.Sqrt,
                                     bias=eps_col, scale=1.0 / DH).then_inc(s["nsa_std"], 1)
            act.wait_ge(s["o_sums"], 1)
            nc.scalar.activation(st2[:, 0:8], st2[:, 8:16], ACT.Sqrt, bias=eps_col, scale=1.0 / P)\
                .then_inc(s["o_std"], 1)
            act.wait_ge(s["unit_used"], UNIT_AT["cmp"] + 1)
            for g in range(NKV):
                half = slice(g * DH, (g + 1) * DH)
                ins = nc.scalar.activation(hid[half, :].rearrange("p (v n) -> p v n", v=2)[:, :, 0:NCMP],
                                           pa[half, g * HALF:g * HALF + 32].rearrange("p (v n) -> p v n", v=2)
                                           [:, :, 0:NCMP], ACT.Gelu_apprx_tanh)
            ins.then_inc(s["hid_made"], 1)
            act.wait_ge(s["cmp_sums"], 1)
            nc.scalar.activation(st2[0:NCMP, 66:68], st2[0:NCMP, 64:66], ACT.Sqrt, bias=eps_col[0:NCMP, :],
                                 scale=1.0 / DH).then_inc(s["cmp_std"], 1)
            act.wait_ge(s["cmp_turned"], 1)
            nc.scalar.activation(kcT[:, 0:NCMP], pa[:, 0:NCMP], ACT.Copy, scale=col("nk_g", 0))\
                .then_inc(s["cmpT_made"], 1)
            act.wait_ge(s["cs_shifted"], 1)
            ec = e_c.rearrange("p (m n) -> p m n", n=16)[:, :, 0:NCMP]
            nc.scalar.activation(ec, ec, ACT.Exp).then_inc(s["cs_exp"], 1)
            act.wait_ge(s["cs_turned"], 1)
            nc.scalar.activation(at2.cT[0:NCMP, :], pa[0:NCMP, :], ACT.Copy).then_inc(s["csT_moved"], 1)
            for b, (t, w) in enumerate(STEPS2):
                act.wait_ge(s["att_bias"], b + 1)
                for h in range(NSA_HEADS):
                    src = score2(at2.sc, t)[:, h, :]
                    ins = nc.scalar.activation(src, src, ACT.Exp, bias=st2[:, 80 + h:81 + h],
                                               accum_out=st2[:, 88 + h:89 + h])
                ins.then_inc(s["att_exp"], 1)
                act.wait_ge(s["att_turned"], b + 1)
                n = NSA_HEADS * (t + 1) * P
                nc.scalar.activation(at2.pT[:, 0:n], pa[:, 0:n], ACT.Copy).then_inc(s["att_moved"], 1)
            act.wait_ge(s["nsa_osums"], 1)
            nc.scalar.activation(st2[:, 112:128], st2[:, 96:112], ACT.Sqrt, bias=eps_col, scale=1.0 / DH)\
                .then_inc(s["nsa_ostd"], 1)
            for name in ("wp0", "wp1"):
                c = int(name[2])
                move(name, lt[:, :].rearrange("p (t d) -> p t d", t=NT)[:, :, c * HALF:(c + 1) * HALF])

            for t in range(NT):
                norm_std(4 + t)
            for c in range(4):
                b = (qT if c < 2 else kT)[:, (c % 2) * D:(c % 2 + 1) * D]
                move(f"wq{c}", b.rearrange("p (a n) -> p a n", a=2))
            act.wait_ge(s["pscore_full"], 1)
            nc.scalar.activation(xc[:, :], pa[:, :], ACT.Copy).then_inc(s["pscore_moved"], 1)
            act.wait_ge(s["unit_used"], UNIT_AT["keys"] + 1)
            nc.scalar.activation(rg[:, :], pa[:, :], ACT.Copy).then_inc(s["pscore_moved"], 1)
            for c in range(2):
                act.wait_ge(s["ple_full"], c + 1)
                ins = nc.scalar.activation(nq[:, 0:2 * D].rearrange("p (t d) -> p t d", t=NT)
                                           [:, :, c * HALF:(c + 1) * HALF], pp[:, OUT_AT[f"ple{c}"] % 2], ACT.Copy)
                if c == 0:
                    ins.then_inc(s["proj_moved"], 1)
            ins.then_inc(s["ple_used"], 1)
            def top_exp(head, odd):
                act.wait_ge(s["top_shift"], head + 1)
                nc.scalar.activation(top_w[odd], top_w[odd], ACT.Exp).then_inc(s["top_exp"], 1)

            def head_weights(head, odd):
                act.wait_ge(s["u_free"], head * TOPK + NBUF + TOPK)
                mine = slice(odd * TOPK, (odd + 1) * TOPK)
                nc.scalar.activation(acts[:, mine], dots[:, mine], ACT.Gelu_apprx_tanh).then_inc(s["gelu_made"], 1)
                act.wait_ge(s["w_made"], head + 1)
                for k in range(TOPK):
                    act.wait_ge(s["v_free"], head * TOPK + k + 1 + NBUF - DIAGS)
                    n = k % DIAGS
                    a = odd * TOPK + k
                    nc.scalar.activation(diag[:, n * P:(n + 1) * P], ident[:, :], ACT.Copy, scale=wk[:, a:a + 1])\
                        .then_inc(s["diag_made"], 1)

            def tile_sums(t):
                act.wait_ge(s["v_free"], NBUF + (t + 1) * NSLOT)
                nc.scalar.activation(x3[:, t, :].rearrange("p (c n) -> p c n", c=2), pp[:, t, :, :], ACT.Copy)\
                    .then_inc(s["h2_made"], 1)

            top_exp(0, 0)
            with act.Fori(0, PEER_HEADS // 2) as pair:
                for odd in range(2):
                    top_exp(pair * 2 + odd + 1, 1 - odd)
                    head_weights(pair * 2 + odd, odd)
            tile_sums(0)
            with act.Fori(PEER_HEADS // 2, PEER_HEADS - 1) as pair:
                for odd in range(2):
                    top_exp(pair * 2 + odd + 1, 1 - odd)
                    head_weights(pair * 2 + odd, odd)
            top_exp(LAST_HEAD, 1)
            head_weights(LAST_HEAD - 1, 0)
            head_weights(LAST_HEAD, 1)
            tile_sums(1)

            for t in range(NT):
                norm_std(6 + t)
            for c in range(2):
                act.wait_ge(s["gate_full"], c + 1)
                nc.scalar.activation(lt[:, :].rearrange("p (t d) -> p t d", t=NT)[:, :, c * HALF:(c + 1) * HALF],
                                     pp[:, c], ACT.Sigmoid).then_inc(s["gate_moved"], 1)

        @block.vector
        def _(dve):
            counts = {}

            def step(ins, name="dve_step"):
                counts[name] = counts.get(name, 0) + 1
                ins.then_inc(s[name], 1)
                dve.wait_ge(s[name], counts[name])

            V = nc.vector
            eps_col = small[:, 250:251]

            def norm(m, src, junk, dst, gain):
                step(V.tensor_tensor_reduce(out=junk, in0=src, in1=src, scale=1.0, scalar=0.0, op0=ALU.mult,
                                            op1=ALU.add, accum_out=stat[:, m:m + 1]), "squares_summed")
                dve.wait_ge(s["std_made"], m + 1)
                step(V.reciprocal(stat[:, 24 + m:25 + m], stat[:, 16 + m:17 + m]))
                step(V.tensor_scalar(junk, src, stat[:, 24 + m:25 + m], None, ALU.mult), "scaled")

            def norm_out(m, gain):
                t = m % NT
                dve.wait_ge(s["turned"], m + 1)
                step(V.tensor_tensor(h3[:, :, t * P:(t + 1) * P],
                                     pa[:, t * D:(t + 1) * D].rearrange("p (k n) -> p k n", k=KC),
                                     gain.unsqueeze(2).broadcast_to([P, KC, P]), ALU.mult), "normed")

            step(V.memset(eps_col, EPS))
            dve.wait_ge(s["x_loaded"], 16)
            for t in range(NT):
                norm(t, x3[:, t, :], vv[:, t * D:(t + 1) * D], None, None)
            step(V.memset(xl3[:, :, 0:PAD], 0.0))
            dve.wait_ge(s["cols_loaded"], 16)
            for t in range(NT):
                norm_out(t, col("pre_g", 0, KC))

            dve.wait_ge(s["lambdas_loaded"], 16)
            for j in range(2):
                V.tensor_tensor_reduce(out=lamt[:, 2 * j * QK:(2 * j + 1) * QK],
                                       in0=lamt[:, 2 * j * QK:(2 * j + 1) * QK],
                                       in1=lamt[:, (2 * j + 1) * QK:(2 * j + 2) * QK], scale=1.0, scalar=0.0,
                                       op0=ALU.mult, op1=ALU.add, accum_out=small[:, j:j + 1])
            step(V.tensor_scalar(small[:, 24:32], col("lam", 0, KC), -1.0, None, ALU.mult))
            step(V.tensor_tensor(small[:, 8:16], small[:, 24:32], col("lam", 0, KC), ALU.max), "lambda_sums")
            V.tensor_scalar(small[:, 80:81], col("sub_g"), 1.0 - LAM_INIT, None, ALU.mult)

            for c in range(2):
                dve.wait_ge(s["proj_moved"], OUT_AT[f"xl{c}"] + 1)
                for j in range(TAPS):
                    for k in range(4 * c, 4 * c + 4):
                        src = xl3[:, k, PAD - TAPS + 1 + j:PAD - TAPS + 1 + j + SEQ]
                        if j == 0:
                            ins = V.tensor_scalar(xc3[:, k, :], src, col("conv_w", k), col("conv_b", k),
                                                  ALU.mult, ALU.add)
                        else:
                            ins = V.scalar_tensor_tensor(out=xc3[:, k, :], in0=src, scalar=col("conv_w", j * KC + k),
                                                         in1=xc3[:, k, :], op0=ALU.mult, op1=ALU.add)
                    if c == 1 and j == TAPS - 1:
                        step(ins, "conv_done")
                    else:
                        step(ins)

            dve.wait_ge(s["lambda_exps"], 1)
            step(V.tensor_tensor(small[:, 4:5], small[:, 3:4], small[:, 2:3], ALU.subtract))
            step(V.tensor_scalar(small[:, 5:6], small[:, 4:5], -LAM_INIT, None, ALU.add))
            e, z, z2, acc = small[:, 16:24], small[:, 100:108], small[:, 108:116], small[:, 116:124]
            step(V.tensor_scalar(z, e, 2.0, None, ALU.add))
            step(V.reciprocal(z, z))
            step(V.tensor_tensor(z, z, e, ALU.mult))
            step(V.tensor_tensor(z2, z, z, ALU.mult))
            terms = 9
            step(V.tensor_scalar(acc, z2, 2.0 / (2 * terms + 1), 2.0 / (2 * terms - 1), ALU.mult, ALU.add))
            for n in range(terms - 2, -1, -1):
                step(V.tensor_tensor(acc, acc, z2, ALU.mult))
                step(V.tensor_scalar(acc, acc, 2.0 / (2 * n + 1), None, ALU.add))
            step(V.tensor_tensor(acc, acc, z, ALU.mult))
            step(V.scalar_tensor_tensor(out=acc, in0=small[:, 24:32], scalar=0.0, in1=acc, op0=ALU.max, op1=ALU.add))
            step(V.tensor_scalar(small[:, 32:40], acc, LRU_C, None, ALU.mult))
            dve.wait_ge(s["rgate_moved"], 1)
            step(V.tensor_tensor(rg3, rg3, small[:, 32:40].unsqueeze(2).broadcast_to([P, KC, SEQ]), ALU.mult),
                 "decay_log")
            dve.wait_ge(s["tanh_made"], 1)
            dve.wait_ge(s["act_step"], 1)
            step(V.tensor_scalar(rg[:, :], lt[:, :], 1.0, None, ALU.add))
            step(V.reciprocal(rg[:, :], rg[:, :]))
            step(V.scalar_tensor_tensor(out=lt[:, :], in0=lt[:, :], scalar=0.0, in1=rg[:, :], op0=ALU.max,
                                        op1=ALU.mult), "mult_sq")
            dve.wait_ge(s["igate_moved"], 1)
            step(V.tensor_tensor(ig[:, :], ig[:, :], xc[:, :], ALU.mult))

            def attention_scores(a):
                g, t = STEPS[a]
                n = P * (t + 1)
                if a == 0:
                    dve.wait_ge(s["consts_made"], 1)
                dve.wait_ge(s["scores_full"], a + 1)
                if a:
                    dve.wait_ge(s["weights_turned"], a)
                for c in range(2):
                    ins = V.tensor_tensor(score_sbuf(t)[:, c], score_bank(t)[:, c],
                                          mask1[:, SEQ - n:SEQ].unsqueeze(1).broadcast_to([P, GRP, n]), ALU.add)
                step(ins)
                step(V.tensor_reduce(small[:, 56 + 16:56 + 24], score_sbuf(t), AX, ALU.max))
                step(V.tensor_scalar(small[:, 40:48], small[:, 72:80], -SCALE1, None, ALU.mult), "bias_made")

            def attention_weights(a):
                g, t = STEPS[a]
                n = P * (t + 1)
                dve.wait_ge(s["probs_made"], a + 1)
                step(V.reciprocal(small[:, 84:92], small[:, 48:56]))
                step(V.tensor_scalar(small[:, 88:92], small[:, 88:92], small[:, 5:6], None, ALU.mult))
                for c in range(2):
                    sc = score_sbuf(t)[:, c]
                    ins = V.tensor_tensor(sc, sc, small[:, 84 + 4 * c:88 + 4 * c].unsqueeze(2)
                                          .broadcast_to([P, GRP, n]), ALU.mult)
                step(ins)
                step(V.tensor_tensor(score_sbuf(t)[:, 0], score_sbuf(t)[:, 0], score_sbuf(t)[:, 1], ALU.add),
                     "weights_made")

            def attention_out(a):
                g, t = STEPS[a]
                dve.wait_ge(s["heads_moved"], a + 1)
                step(V.tensor_tensor(osq[:, :], oh[:, :], oh[:, :], ALU.mult))
                step(V.tensor_reduce(small[:, 60:64], osq[:, :].rearrange("p (h n) -> p h n", h=GRP), AX, ALU.add),
                     "head_sums")
                dve.wait_ge(s["head_std"], a + 1)
                step(V.reciprocal(small[:, 92:96], small[:, 64:68]))
                o3 = oh[:, :].rearrange("p (h n) -> p h n", h=GRP)
                step(V.tensor_tensor(o3, o3, small[:, 92:96].unsqueeze(2).broadcast_to([P, GRP, P]), ALU.mult))
                dve.wait_ge(s["proj_moved"], OUT_AT[f"ga{g}"] + 1)
                gate = ga3[:, t, g * HALF:(g + 1) * HALF]
                step(V.tensor_tensor(gate, gate, oh[:, :], ALU.mult), "head_gated")

            for a in range(len(STEPS)):
                attention_scores(a)
                if a == 0:
                    dve.wait_ge(s["mult_made"], 1)
                    step(V.tensor_tensor(ig[:, :], ig[:, :], lt[:, :], ALU.mult))
                    for k in range(KC):
                        ins = V.tensor_tensor_scan(xc3[:, k, :], xl[:, k * SEQ:(k + 1) * SEQ], ig3[:, k, :], 0.0,
                                                   ALU.mult, ALU.add)
                    step(ins)
                attention_weights(a)
                attention_out(a)
            dve.wait_ge(s["proj_moved"], OUT_AT["gl1"] + 1)
            step(V.tensor_tensor(gl[:, :], gl[:, :], xc[:, :], ALU.mult), "lru_done")

            dve.wait_ge(s["rows_loaded"], 16)
            for t in range(NT):
                dve.wait_ge(s["post_std"], t + 1)
                step(V.reciprocal(stat[:, 36 + t:37 + t], stat[:, 34 + t:35 + t]))
                y = vv[:, t * D:(t + 1) * D]
                step(V.scalar_tensor_tensor(out=y, in0=y, scalar=stat[:, 36 + t:37 + t], in1=post_g[:, :],
                                            op0=ALU.mult, op1=ALU.mult))
                step(V.tensor_tensor(x3[:, t, :], x3[:, t, :], y, ALU.add), "block1_done")

            def heads_rms(dst, src, sq, sums, stds, recips, made, std_made, n_made, out_name, heads, width):
                step(V.tensor_tensor(sq, src, src, ALU.mult))
                step(V.tensor_reduce(sums, sq.rearrange("p (h n) -> p h n", h=heads), AX, ALU.add), made)
                dve.wait_ge(s[std_made], n_made)
                step(V.reciprocal(recips, stds))
                d3 = dst.rearrange("p (h n) -> p h n", h=heads)
                ins = V.tensor_tensor(d3, src.rearrange("p (h n) -> p h n", h=heads),
                                      recips.unsqueeze(2).broadcast_to([recips.shape[0], heads, width]), ALU.mult)
                step(ins, out_name) if out_name else step(ins)

            for t in range(NT):
                norm(2 + t, x3[:, t, :], vv[:, t * D:(t + 1) * D], None, None)
            for t in range(NT):
                norm_out(2 + t, col("mix_g", 0, KC))
            l0, l1, mx = col("lb0", 0, 4), col("lb1", 0, 4), lbt[:, 0:4]
            step(V.tensor_tensor(mx, l0, l1, ALU.max))
            V.tensor_tensor(lbt[:, 4:8], l0, mx, ALU.subtract)
            step(V.tensor_tensor(lbt[:, 8:12], l1, mx, ALU.subtract), "lb_shifted")
            dve.wait_ge(s["lb_exp"], 1)
            step(V.tensor_tensor(lbt[:, 12:16], lbt[:, 4:8], lbt[:, 8:12], ALU.add))
            step(V.reciprocal(lbt[:, 12:16], lbt[:, 12:16]))
            step(V.tensor_tensor(lbt[:, 16:20], lbt[:, 4:8], lbt[:, 12:16], ALU.mult))
            step(V.tensor_scalar(lbt[:, 20:24], lbt[:, 16:20], -1.0, 1.0, ALU.mult, ALU.add))
            V.memset(gain8[:, 6:8], 1.0)
            V.tensor_copy(gain8[:, 4:6], col("nk_g", 1, 2))
            step(V.tensor_scalar(gain8[:, 0:4], col("nq_g").broadcast_to([P, 4]), DH ** -0.5, None, ALU.mult))

            dve.wait_ge(s["proj_moved"], OUT_AT["hf"] + 1)
            for h in range(HG_HEADS):
                f = at2.key[:, h * SEQ:(h + 1) * SEQ]
                ins = V.tensor_scalar(f, f, lbt[:, 20 + h:21 + h], lbt[:, 16 + h:17 + h], ALU.mult, ALU.add)
            step(ins, "forget_made")
            dve.wait_ge(s["log_made"], 1)
            step(V.tensor_scalar(at2.key, at2.key, -1.0, 1.0, ALU.mult, ALU.add))
            dve.wait_ge(s["scan_mask_made"], 1)
            step(V.tensor_tensor_scan(at2.cum, at2.scan_mask, at2.log_f, 0.0, ALU.mult, ALU.add))
            cum3 = at2.cum.rearrange("p (m n) -> p m n", n=CH)
            shift3 = at2.shift.rearrange("p (m n) -> p m n", n=CH)
            shape = [P, HG_HEADS * NCH, CH]
            step(V.tensor_tensor(shift3, cum3, cum3[:, :, CH // 2 - 1:CH // 2].broadcast_to(shape), ALU.subtract),
                 "shift_made")
            dve.wait_ge(s["shift_exp"], 1)
            step(V.tensor_tensor(shift3, cum3[:, :, CH - 1:CH].broadcast_to(shape), cum3, ALU.subtract), "last_made")
            dve.wait_ge(s["proj_moved"], OUT_AT["hq"] + 1)
            V.scalar_tensor_tensor(out=at2.q1, in0=at2.query, scalar=P ** -0.5, in1=at2.q1, op0=ALU.mult, op1=ALU.mult)
            V.tensor_tensor(at2.k2, at2.key, at2.k2, ALU.mult)
            V.scalar_tensor_tensor(out=at2.q3, in0=at2.query, scalar=P ** -0.5, in1=at2.q3, op0=ALU.mult, op1=ALU.mult)
            dve.wait_ge(s["last_exp"], 1)
            step(V.tensor_tensor(at2.k4, at2.key, at2.k4, ALU.mult), "recur_ready")
            dve.wait_ge(s["update_full"], 1)
            u = [pa[:, b * HALF:(b + 1) * HALF] for b in UPDATE_BANKS]
            step(V.tensor_copy(at2.states[:, 0:HALF], u[0]))
            for c in range(1, NCH - 1):
                for h in range(HG_HEADS):
                    a = h * P
                    ins = V.scalar_tensor_tensor(out=at2.states[:, c * HALF + a:c * HALF + a + P],
                                                 in0=at2.states[:, (c - 1) * HALF + a:(c - 1) * HALF + a + P],
                                                 scalar=last_exp[:, h * NCH + c:h * NCH + c + 1],
                                                 in1=u[c][:, a:a + P], op0=ALU.mult, op1=ALU.add)
                if c < NCH - 2:
                    step(ins)
            step(ins, "states_made")

            dve.wait_ge(s["proj_moved"], OUT_AT["nv"] + 1)
            for t in range(NT):
                src = nq3[:, t, 0:NORMED]
                heads_rms(src, src, sm[:, 0:NORMED], st2[:, 40 + 12 * t:52 + 12 * t],
                          st2[:, 16 + 12 * t:28 + 12 * t], small[:, 150 + 12 * t:162 + 12 * t],
                          "nsa_sums", "nsa_std", t + 1, "nsa_scaled", NORMED // DH, DH)
            dve.wait_ge(s["o_moved"], 1)
            heads_rms(at2.o, at2.o, at2.osq, st2[:, 8:16], st2[:, 0:8], small[:, 140:148], "o_sums", "o_std", 1,
                      None, NT * HG_HEADS, P)
            step(V.tensor_tensor(at2.o, at2.o, at2.gate, ALU.mult))
            for t in range(NT):
                dve.wait_ge(s["nsa_turned"], t + 1)
                ins = V.tensor_tensor(nT3[:, :, t * P:(t + 1) * P],
                                      pa[:, t * D:(t + 1) * D].rearrange("p (k n) -> p k n", k=KC),
                                      gain8.unsqueeze(2).broadcast_to([P, KC, P]), ALU.mult)
            step(ins, "nsa_normed")
            for kv in range(2):
                for n, dst in enumerate((at2.pe0, at2.pe1)):
                    ins = V.tensor_tensor(
                        dst[:, kv * SEQ:(kv + 1) * SEQ].rearrange("p (b j) -> p b j", j=CMP_STRIDE),
                        nT3[:, 6 + kv, :].rearrange("p (b j) -> p b j", j=CMP_STRIDE),
                        col("pe", kv * CMP_LEN + n * CMP_STRIDE, CMP_STRIDE).unsqueeze(1)
                        .broadcast_to([P, SEQ // CMP_STRIDE, CMP_STRIDE]), ALU.add)
            step(ins, "cmp_in")
            dve.wait_ge(s["cmp_full"], 1)
            for g in range(NKV):
                ins = V.tensor_copy(cmp_tok[0:NCMP, :].rearrange("p (v g n) -> p v g n", v=2, g=NKV)[:, :, g, :],
                                    pa[0:NCMP, (2 + g) * HALF:(2 + g) * HALF + 2 * DH]
                                    .rearrange("p (v n) -> p v n", v=2))
            step(ins)
            kc = cmp_tok[0:NCMP, 0:NKV * DH]
            heads_rms(kc, kc, at2.tmp[0:NCMP, 0:NKV * DH], st2[0:NCMP, 64:66], st2[0:NCMP, 66:68],
                      st2[0:NCMP, 68:70], "cmp_sums", "cmp_std", 1, "cmp_ready", NKV, DH)
            dve.wait_ge(s["cs_full"], 1)
            ec = e_c.rearrange("p (m n) -> p m n", n=16)[:, :, 0:NCMP]
            bc = bias_c.rearrange("p (m n) -> p m n", n=16)[:, :, 0:NCMP]
            mc = mask_c.rearrange("p (m n) -> p m n", n=16)[:, :, 0:NCMP]
            M = NT * NSA_HEADS
            for g in range(NKV):
                part = slice(g * NT * REP, (g + 1) * NT * REP)
                ins = V.tensor_tensor(ec[:, part, :], pa[:, g * HALF:g * HALF + P]
                                      .rearrange("p (m n) -> p m n", n=16)[:, :, 0:NCMP], bc[:, part, :], ALU.add)
            step(ins)
            cmax, csum = small[:, 180:196], small[:, 196:212]
            step(V.tensor_reduce(cmax, ec, AX, ALU.max))
            step(V.tensor_tensor(ec, ec, cmax.unsqueeze(2).broadcast_to([P, M, NCMP]), ALU.subtract), "cs_shifted")
            dve.wait_ge(s["cs_exp"], 1)
            step(V.tensor_tensor(ec, ec, mc, ALU.mult))
            step(V.tensor_reduce(csum, ec, AX, ALU.add), "cs_ready")
            step(V.tensor_scalar(csum, csum, 1e-30, None, ALU.max))
            step(V.reciprocal(csum, csum))
            coef = small[:, 212:228]
            gates3 = [nq3[:, t, NQW - GATES:NQW].rearrange("p (h b) -> p h b", b=3) for t in range(NT)]
            for t in range(NT):
                ins = V.tensor_tensor(coef[:, t * 8:(t + 1) * 8].rearrange("p (g r) -> p g r", g=NKV),
                                      csum.rearrange("p (g t r) -> p g t r", g=NKV, t=NT)[:, :, t, :],
                                      gates3[t][:, :, 0].rearrange("p (g r) -> p g r", g=NKV), ALU.mult)
            step(ins)
            dve.wait_ge(s["co_full"], 1)
            for t in range(NT):
                ins = V.tensor_tensor(at2.no[:, t * HALF:(t + 1) * HALF].rearrange("p (h n) -> p h n", n=DH),
                                      pa[:, t * HALF:(t + 1) * HALF].rearrange("p (h n) -> p h n", n=DH),
                                      coef[:, t * 8:(t + 1) * 8].unsqueeze(2).broadcast_to([P, NSA_HEADS, DH]),
                                      ALU.mult)
            step(ins, "co_used")
            dve.wait_ge(s["bias2_made"], 1)
            b3 = at2.bias[:, :].rearrange("p (h n) -> p h n", h=NSA_HEADS)
            for b, (t, w) in enumerate(STEPS2):
                n = P * (t + 1)
                dve.wait_ge(s["att_full"], b + 1)
                step(V.tensor_tensor(score2(at2.sc, t), score2(pa, t), b3[:, :, SEQ - n:SEQ], ALU.add))
                step(V.tensor_reduce(st2[:, 72:80], score2(at2.sc, t), AX, ALU.max))
                step(V.tensor_scalar(st2[:, 80:88], st2[:, 72:80], -1.0, None, ALU.mult), "att_bias")
                dve.wait_ge(s["att_exp"], b + 1)
                step(V.tensor_scalar(small[:, 228:236], st2[:, 88:96], 1e-30, None, ALU.max))
                step(V.reciprocal(small[:, 228:236], small[:, 228:236]))
                step(V.tensor_tensor(small[:, 228:236], small[:, 228:236], gates3[t][:, :, 1 + w], ALU.mult))
                dve.wait_ge(s["ao_full"], b + 1)
                tmp3 = at2.tmp[:, 0:HALF].rearrange("p (h n) -> p h n", n=DH)
                step(V.tensor_tensor(tmp3, pa[:, 0:HALF].rearrange("p (h n) -> p h n", n=DH),
                                     small[:, 228:236].unsqueeze(2).broadcast_to([P, NSA_HEADS, DH]), ALU.mult),
                     "ao_used")
                no = at2.no[:, t * HALF:(t + 1) * HALF]
                step(V.tensor_tensor(no, no, at2.tmp[:, 0:HALF], ALU.add))
            heads_rms(at2.no, at2.no, at2.osq, st2[:, 96:112], st2[:, 112:128], small[:, 124:140], "nsa_osums",
                      "nsa_ostd", 1, "nsa_out", NT * NSA_HEADS, DH)
            step(V.memset(small[:, 236:237], 0.0), "nsa_out")
            for t in range(NT):
                dve.wait_ge(s["mix_turned"], t + 1)
                step(V.tensor_tensor(h3[:, :, t * P:(t + 1) * P],
                                     pa[:, t * D:(t + 1) * D].rearrange("p (k n) -> p k n", k=KC),
                                     col("out2_g", 0, KC).unsqueeze(2).broadcast_to([P, KC, P]), ALU.mult),
                     "mixT_made")
            dve.wait_ge(s["proj_moved"], OUT_AT["wp1"] + 1)
            step(V.tensor_tensor(xs[:, :], xs[:, :], lt[:, :], ALU.add), "h_made")

            for t in range(NT):
                norm(4 + t, x3[:, t, :], vv[:, t * D:(t + 1) * D], None, None)
            for t in range(NT):
                norm_out(4 + t, col("ffn_g", 0, KC))
            dve.wait_ge(s["rows_loaded"], 32)
            for t in range(NT):
                xt = vv[:, t * D:(t + 1) * D]
                step(V.tensor_tensor(xt, xt, post_g[:, :], ALU.mult))
            two = [P, 2, TOPK, TOPK]

            def choose(head, odd):
                count = [0]

                def then(ins):
                    count[0] += 1
                    ins.then_inc(s["choice_step"], 1)
                    dve.wait_ge(s["choice_step"], count[0])

                def top16(rows_in, values, at, n):
                    for half in range(2):
                        where = slice(half * 8, half * 8 + 8)
                        for j in range(n):
                            ins = V.max(values[:, j, where], rows_in[:, j, :])
                        then(ins)
                        for j in range(n):
                            ins = V.max_index(at[:, j, where], values[:, j, where], rows_in[:, j, :])
                        then(ins)
                        if half == 0:
                            for j in range(n):
                                ins = V.match_replace(rows_in[:, j, :], values[:, j, where], rows_in[:, j, :], LOWEST)
                            then(ins)

                then(V.tensor_copy(halves, xc_rg[:, bass.ds(head * (2 * NKEYS), 2 * NKEYS)]))
                v3 = v16.rearrange("p (c k) -> p c k", c=2)
                top16(halves.rearrange("p (c n) -> p c n", c=2), v3, i16.rearrange("p (c k) -> p c k", c=2), 2)
                V.tensor_copy(i16f, i16)
                then(V.tensor_tensor(pairs.rearrange("p (a b) -> p a b", a=TOPK),
                                     v3[:, 0, :].unsqueeze(2).broadcast_to([P, TOPK, TOPK]),
                                     v3[:, 1, :].unsqueeze(1).broadcast_to([P, TOPK, TOPK]), ALU.add))
                top16(pairs.unsqueeze(1), best.unsqueeze(1), best_at.unsqueeze(1), 1)
                V.tensor_scalar(top_w[odd], best, best[:, 0:1], None, ALU.subtract).then_inc(s["top_shift"], 1)
                V.tensor_scalar(places_i[:, 0:TOPK], best_at, 4, None, ALU.logical_shift_right)
                then(V.tensor_scalar(places_i[:, TOPK:2 * TOPK], best_at, TOPK - 1, None, ALU.bitwise_and))
                then(V.tensor_copy(places, places_i))
                for half in range(2):
                    mine = slice(half * TOPK, (half + 1) * TOPK)
                    square = [P, TOPK, TOPK]
                    h3d = hot.rearrange("p (k j) -> p k j", k=TOPK)
                    then(V.tensor_tensor(h3d, places[:, mine].unsqueeze(2).broadcast_to(square),
                                         iota16.unsqueeze(1).broadcast_to(square), ALU.is_equal))
                    then(V.tensor_tensor(h3d, h3d, i16f[:, mine].unsqueeze(1).broadcast_to(square), ALU.mult))
                    then(V.tensor_reduce(keys_f[:, mine], h3d, AX, ALU.add))
                V.scalar_tensor_tensor(out=keys_f[:, 0:TOPK], in0=keys_f[:, 0:TOPK], scalar=float(NKEYS),
                                       in1=keys_f[:, TOPK:2 * TOPK], op0=ALU.mult, op1=ALU.add)\
                    .then_inc(s["choice_step"], 1)
                dve.wait_ge(s["choice_step"], count[0] + 1)
                dve.sem_clear(s["choice_step"])
                V.tensor_copy(all_experts[:, bass.ds(head * TOPK, TOPK)], keys_f[:, 0:TOPK]).then_inc(s["chosen"], 1)

            def head_dots(head, odd, t):
                for k in range(TOPK):
                    rows_u = u_rows[k % NBUF]
                    a = odd * TOPK + k
                    dve.wait_ge(u_here[k % NBUF], (head * 2 + k // NBUF + 1) * 16)
                    V.tensor_tensor_reduce(out=rows_u, in0=rows_u, in1=vv[:, t * D:(t + 1) * D], scale=1.0,
                                           scalar=0.0, op0=ALU.mult, op1=ALU.add,
                                           accum_out=dots[:, a:a + 1]).then_inc(s["u_free"], 1)
                mine = slice(odd * TOPK, (odd + 1) * TOPK)
                dve.wait_ge(s["top_exp"], head + 1)
                V.tensor_reduce(top_sum, top_w[odd], AX, ALU.add).then_inc(s["top_summed"], 1)
                dve.wait_ge(s["top_summed"], head * 2 + 1)
                V.reciprocal(top_sum, top_sum).then_inc(s["top_summed"], 1)
                dve.wait_ge(s["gelu_made"], head + 1)
                dve.wait_ge(s["top_summed"], head * 2 + 2)
                V.scalar_tensor_tensor(out=wk[:, mine], in0=acts[:, mine], scalar=top_sum, in1=top_w[odd],
                                       op0=ALU.mult, op1=ALU.mult).then_inc(s["w_made"], 1)

            V.memset(small[:, 237:238], 0.0).then_inc(s["u_free"], NBUF)
            V.memset(small[:, 238:239], 0.0).then_inc(s["v_free"], NBUF)
            dve.wait_ge(s["pscore_moved"], 1)
            choose(0, 0)
            dve.wait_ge(s["pscore_moved"], 2)
            with dve.Fori(0, PEER_HEADS // 2) as pair:
                for odd in range(2):
                    choose(pair * 2 + odd + 1, 1 - odd)
                    head_dots(pair * 2 + odd, odd, 0)
            with dve.Fori(PEER_HEADS // 2, PEER_HEADS - 1) as pair:
                for odd in range(2):
                    choose(pair * 2 + odd + 1, 1 - odd)
                    head_dots(pair * 2 + odd, odd, 1)
            choose(LAST_HEAD, 1)
            head_dots(LAST_HEAD - 1, 0, 1)
            head_dots(LAST_HEAD, 1, 1)

            for t in range(NT):
                dve.wait_ge(s["h2_made"], t + 1)
                norm(6 + t, x3[:, t, :], vv[:, t * D:(t + 1) * D], None, None)
            for t in range(NT):
                norm_out(6 + t, col("gate_g", 0, KC))
            dve.wait_ge(s["gate_moved"], 2)
            for t in range(NT):
                y = lt[:, t * D:(t + 1) * D]
                step(V.tensor_tensor(y, y, nq[:, t * D:(t + 1) * D], ALU.mult))
                step(V.tensor_tensor(x3[:, t, :], x3[:, t, :], y, ALU.add), "y_made")


def feature_columns(v):
    return np.asarray(v).reshape(-1, P).T


def unit_of(w, k0, c0, c1):
    w = np.asarray(w)[k0:k0 + D, c0:c1]
    out = np.zeros((P, KC, HALF), np.float32)
    out[:, :, 0:w.shape[1]] = w.reshape(KC, P, -1).transpose(1, 0, 2)
    return out.reshape(P, UNIT)


def padded(parts):
    out = np.zeros((P, UNIT), np.float32)
    at = 0
    for a in parts:
        out[:, at:at + a.shape[1]] = a
        at += a.shape[1]
    return out


def lay_out(i):
    w_in, w_out = np.asarray(i["w_in"])[0], np.asarray(i["w_out"])[0]
    at = {"q": 0, "k": D, "v": 2 * D, "ga": 3 * D, "xl": 4 * D, "gl": 5 * D}
    w2, wp = np.asarray(i["w_in_2"])[0], np.asarray(i["w_out_2"])[0]
    wq, gw = np.asarray(i["peer_wq_2"])[0], np.asarray(i["ple_gate_w_2"])[0]
    nsa, kv = 4 * HALF, 5 * HALF
    order = [np.arange(nsa, kv).reshape(NKV, REP, DH).transpose(1, 0, 2).ravel()]
    order += [np.arange(kv + n * P, kv + (n + 1) * P) for n in (2, 4, 0, 1, 3, 5)]
    order.append(np.arange(kv + 6 * P, kv + 6 * P + GATES))
    wn = w2[:, np.concatenate(order)]
    both = lambda a: np.concatenate([a, a], axis=0)
    units = []
    for name in UNITS:
        if name == "lru":
            units.append(padded([np.asarray(i[n])[0].transpose(1, 0, 2).reshape(P, D) for n in ("w_rgate", "w_igate")]))
        elif name[:3] == "wol":
            units.append(unit_of(w_out, D, int(name[3]) * HALF, (int(name[3]) + 1) * HALF))
        elif name[:3] == "woa":
            units.append(unit_of(w_out, 0, int(name[3]) * HALF, (int(name[3]) + 1) * HALF))
        elif name in ("hf", "hq", "hi", "hg"):
            a = {"hq": 0, "hf": 1, "hi": 2, "hg": 3}[name] * HALF
            units.append(unit_of(w2, 0, a, a + HALF))
        elif name in ("nq", "nk", "nv"):
            a = {"nq": 0, "nk": 1, "nv": 2}[name] * HALF
            units.append(unit_of(wn, 0, a, min(a + HALF, NQW)))
        elif name == "cmp":
            w = np.asarray(i["cmp_w1_2"])[0].reshape(2, CMP_LEN, DH, DH).transpose(2, 0, 1, 3).reshape(DH, UNIT)
            units.append(both(w))
        elif name == "keys":
            units.append(padded([np.asarray(i["peer_keys_2"])[0].reshape(2 * PEER_HEADS, NKEYS, P)
                                 .transpose(2, 0, 1).reshape(P, -1)]))
        elif name == "ple":
            w = np.asarray(i["ple_proj_2"])[0].reshape(PLE // P, P, D)
            p = np.asarray(i["p_2"])[0, 0].T.reshape(PLE // P, P, SEQ)
            units.append(padded([*w, *p]))
        elif name[:2] in ("wp", "wq", "gw"):
            c = int(name[2]) * HALF
            units.append(unit_of({"wp": wp, "wq": wq, "gw": gw}[name[:2]], 0, c, c + HALF))
        else:
            a = at[name[:-1]] + int(name[-1]) * HALF
            units.append(unit_of(w_in, 0, a, a + HALF))
    named = {
        "pre_g": feature_columns(i["pre_norm_g"]), "conv_w": feature_columns(i["conv_w"]),
        "conv_b": feature_columns(i["conv_b"]), "b_r": feature_columns(i["b_rgate"]),
        "b_i": feature_columns(i["b_igate"]), "lam": feature_columns(i["lru_lambda"]),
        "sub_g": feature_columns(i["subln_g"]),
        "mix_g": feature_columns(i["mix_norm_2"]), "ffn_g": feature_columns(i["ffn_norm_2"]),
        "gate_g": feature_columns(i["ple_gate_norm_2"]),
        "lb0": feature_columns(np.asarray(i["hg_lb_logits_2"])[0]),
        "lb1": feature_columns(np.asarray(i["hg_lb_logits_2"])[1]),
        "out2_g": np.concatenate([feature_columns(i["hg_out_norm_2"]), feature_columns(i["nsa_out_norm_2"])], axis=1),
        "nq_g": both(np.asarray(i["nsa_q_norm_2"]).T), "nk_g": both(np.asarray(i["nsa_k_norm_2"])[0].T),
        "pe": both(np.asarray(i["cmp_pe_2"])[0].reshape(2 * CMP_LEN, DH).T),
        "cmp_w2": both(np.asarray(i["cmp_w2_2"])[0].transpose(1, 0, 2).reshape(DH, 2 * DH)),
    }
    return {
        "x": np.asarray(i["x"])[0],
        "wall": np.stack(units),
        "cols": np.ascontiguousarray(np.concatenate([named[n] for n, _ in COLS], axis=1)),
        "rows": np.stack([np.asarray(i["post_norm_g"])[0], np.asarray(i["ffn_norm_2"])[0]]),
        "peer_u": np.asarray(i["peer_u_2"])[0],
        "peer_v": np.asarray(i["peer_v_2"])[0],
        "lambdas": np.concatenate([np.asarray(i[n]) for n in ("lambda_q1", "lambda_k1", "lambda_q2", "lambda_k2")], axis=1),
    }


def kernel(**inputs):
    import concourse.bacc as bacc
    from concourse.bass_utils import run_bass_kernel_spmd

    nc = bacc.Bacc("TRN2", target_bir_lowering=False, num_devices=1)
    arrays = {f"in_{n}": np.ascontiguousarray(a) for n, a in lay_out(inputs).items()}
    aps = {n[3:]: nc.dram_tensor(n, a.shape, mybir.dt.from_np(a.dtype), kind="ExternalInput").ap()
           for n, a in arrays.items()}
    out = nc.dram_tensor("out", (SEQ, D), F32, kind="ExternalOutput").ap()
    two_blocks(nc, out=out, **aps)
    r = run_bass_kernel_spmd(nc, [arrays], core_ids=[0])
    return r.results[0]["out"].reshape(1, SEQ, D)
```

```python
import math
from contextlib import ExitStack

import numpy as np

import concourse.bass as bass
from concourse import mybir

F32 = mybir.dt.float32
U32 = mybir.dt.uint32
I32 = mybir.dt.int32
ALU = mybir.AluOpType
ACT = mybir.ActivationFunctionType
AX = mybir.AxisListType.X

P = 128
SEQ = 256
D = 1024
NT = SEQ // P
KC = D // P
HALF = 512
UNIT = KC * HALF
RING = 4
EPS = 1e-6
NEG = -1e30
LOWEST = -3e38

HEADS = 8
QK = 64
SCALE1 = QK ** -0.5
LAM_INIT = 0.8 - 0.6 * math.exp(-0.3 * 0)
LRU_C = 8.0
TAPS = 4
PAD = 4
XS = SEQ + PAD
GRP = 4

HG_HEADS = 4
CH = 64
NCH = SEQ // CH
DH = 64
NKV = 2
REP = 4
NSA_HEADS = NKV * REP
CMP_LEN = 32
CMP_STRIDE = 16
NCMP = (SEQ - CMP_LEN) // CMP_STRIDE + 1
SLOPES = [2.0 ** (-8.0 * (h + 1) / NSA_HEADS) for h in range(NSA_HEADS)]
GATES = 3 * NSA_HEADS
PEER_HEADS = 8
NKEYS = 128
TOPK = 16
NSLOT = PEER_HEADS * TOPK
PLE = 256
NQW = 2 * HALF + 2 * NKV * DH + GATES
NORMED = HALF + 2 * NKV * DH

UNITS = ["xl0", "xl1", "q0", "q1", "lru", "k0", "k1", "v0", "v1", "ga0", "ga1", "gl0", "gl1",
         "wol0", "wol1", "woa0", "woa1",
         "nq", "nk", "hf", "hq", "cmp", "hi", "hg", "nv", "wp0", "wp1",
         "ple", "wq0", "wq1", "wq2", "wq3", "gw0", "gw1"]
UNIT_AT = {name: n for n, name in enumerate(UNITS)}
OUTS = ["xl0", "xl1", "q0", "q1", "k0", "k1", "v0", "v1", "ga0", "ga1", "gl0", "gl1", "wo0", "wo1",
        "nq", "nk", "hf", "hq", "hi", "hg", "nv", "wp0", "wp1", "ple0", "ple1", "wq0", "wq1", "wq2", "wq3"]
OUT_AT = {name: n for n, name in enumerate(OUTS)}

COLS = [("pre_g", KC), ("conv_w", TAPS * KC), ("conv_b", KC), ("b_r", KC), ("b_i", KC),
        ("lam", KC), ("sub_g", 1),
        ("mix_g", KC), ("ffn_g", KC), ("gate_g", KC), ("lb0", HG_HEADS), ("lb1", HG_HEADS), ("out2_g", KC),
        ("nq_g", 1), ("nk_g", 3), ("pe", 2 * CMP_LEN), ("cmp_w2", 2 * DH)]
COL_AT, NCOL = {}, 0
for _name, _width in COLS:
    COL_AT[_name] = (NCOL, NCOL + _width)
    NCOL += _width

SEMS = ["x_loaded", "cols_loaded", "rows_loaded", "lambdas_loaded", "consts_made", "identity_made", "unit_used",
        "proj_moved", "squares_summed", "std_made", "scaled", "turned", "normed", "dve_step", "act_step",
        "pool_step", "lambda_sums", "lambda_exps", "conv_done", "rgate_full", "rgate_moved", "igate_moved",
        "decay_log", "tanh_made", "mult_sq", "mult_made", "lru_done", "scores_full", "bias_made", "probs_made",
        "weights_made", "weights_turned", "turned_moved", "heads_full", "heads_moved", "head_sums", "head_std",
        "head_gated", "attn_turned", "attn_moved", "ple_full", "lb_shifted", "lb_exp", "post_std",
        "block1_done", "stored", "bias2_made", "scan_mask_made", "forget_made", "log_made", "shift_made",
        "shift_exp", "last_made", "last_exp", "recur_ready", "keys_turned", "keys_moved", "intra_full",
        "intra_moved", "intra_masked", "update_full", "states_made", "o_gated", "o_full", "o_moved", "o_sums",
        "o_std", "nsa_sums", "nsa_std", "nsa_scaled", "nsa_turned", "nsa_normed", "cmp_in", "hid_made",
        "cmp_full", "cmp_sums", "cmp_std", "cmp_ready", "group_done", "cmp_turned", "cmpT_made", "cs_full", "cs_shifted",
        "cs_exp", "cs_ready", "cs_turned", "csT_moved", "co_full", "co_used", "att_full", "att_bias", "att_exp",
        "att_turned", "att_moved", "ao_full", "ao_used", "nsa_osums", "nsa_ostd", "nsa_out", "mix_turned",
        "mixT_made", "wp_full", "wo_full", "keys_loaded", "pscore_full", "pscore_moved", "choice_step", "top_shift", "top_exp",
        "top_summed", "chosen", "cur_made", "pace", "dve_pace", "u_free", "gelu_made", "w_made", "diag_made", "v_free",
        "h2_made", "gate_full", "gate_moved", "y_made"]


UPDATE_BANKS = (0, 1, 2)
NBUF = 8
BATCH = 4
DIAGS = 4
LAST_HEAD = NT * PEER_HEADS - 1


def two_blocks(nc, x, wall, cols, rows, lambdas, sub_keys, peer_u, peer_v, out):
    with ExitStack() as ctx:
        def sb(name, words, dt=F32):
            return ctx.enter_context(nc.sbuf_tensor(name, [P, words], dt))

        s = {n: ctx.enter_context(nc.semaphore(n)) for n in SEMS}
        unit_ready = [ctx.enter_context(nc.semaphore(f"unit_ready{i}")) for i in range(RING)]

        ring = sb("ring", RING * UNIT)
        xs = sb("xs", NT * D)
        hT = sb("hT", KC * SEQ)
        colt = sb("colt", NCOL)
        post_g = sb("post_g", D)
        ident = sb("ident", P)
        mask1 = sb("mask1", SEQ)
        stat = sb("stat", 64)
        zero = sb("zero", P)

        xl = sb("xl", KC * XS)
        xc_rg = sb("xc_rg", 2 * KC * SEQ)
        xc, rg = xc_rg[:, 0:KC * SEQ], xc_rg[:, KC * SEQ:2 * KC * SEQ]
        ig = sb("ig", KC * SEQ)
        lt = sb("lt", KC * SEQ)
        gl = sb("gl", KC * SEQ)
        qT = sb("qT", KC * SEQ)
        kT = sb("kT", KC * SEQ)
        vv = sb("vv", NT * D)
        ga = sb("ga", NT * D)
        sm = sb("sm", 2 * GRP * SEQ)
        tail = sb("tail", 2 * D)
        wT = tail[:, 0:D]
        oh = tail[:, D:D + HALF]
        osq = tail[:, D + HALF:2 * D]
        junk1 = xc[:, 0:D]
        lamt = sb("lamt", 4 * QK)
        small = sb("small", 256)

        nq = sb("nq", NT * NQW)
        small2 = sb("small2", 1536)
        diag = sb("diag", DIAGS * P)

        class at2:
            key = kT[:, 0:D]
            log_f = kT[:, D:2 * D]
            cum = qT[:, 0:D]
            shift = qT[:, D:2 * D]
            q1, k2 = xc[:, 0:D], xc[:, D:2 * D]
            q3, k4 = rg[:, 0:D], rg[:, D:2 * D]
            query = ig[:, 0:D]
            scan_mask = lt[:, 0:D]
            k_tok = lt[:, D:2 * D]
            v = ga[:, 0:D]
            gate = ga[:, D:2 * D]
            intra = gl[:, 0:HALF]
            states = gl[:, HALF:4 * HALF]
            o = xl[:, 0:D]
            osq = xl[:, D:2 * D]
            nT = vv
            pe0, pe1 = sm[:, D:D + HALF], sm[:, D + HALF:2 * D]
            sc = (sm, qT)
            pT = (kT, gl)
            cT = xc
            no = ig[:, 0:D]
            tmp = ig[:, D:2 * D]
            bias = tail

        bias_c = small2[:, 0:256]
        mask_c = small2[:, 256:512]
        e_c = small2[:, 512:768]
        dist_c = small2[:, 768:800]
        dist_ci = small2[:, 800:832].bitcast(I32)
        iota16 = small2[:, 832:848]
        iota16i = small2[:, 848:864].bitcast(I32)
        gain8 = small2[:, 864:872]
        st2 = small2[:, 872:1000]
        lbt = small2[:, 1000:1032]
        hid = small2[:, 1032:1064]
        kcT = small2[:, 1064:1080]
        cmp_tok = small2[:, 1080:1336]
        last_exp = small2[:, 1336:1352]
        dots = small2[:, 1352:1384]
        acts = small2[:, 1384:1416]
        wk = small2[:, 1416:1448]
        cur = [[small2[:, 1448 + n * TOPK:1448 + (n + 1) * TOPK].bitcast(U32) for n in (2 * k, 2 * k + 1)]
               for k in range(2)]

        def choice(at, words, dt=F32):
            a = xl[:, at:at + words]
            return a if dt == F32 else a.bitcast(dt)

        halves = choice(0, 2 * NKEYS)
        pairs = choice(256, TOPK * TOPK)
        hot = choice(512, TOPK * TOPK)
        v16, i16, i16f = choice(768, 2 * TOPK), choice(800, 2 * TOPK, U32), choice(832, 2 * TOPK)
        best, best_at = choice(864, TOPK), choice(880, TOPK, U32)
        places_i, places = choice(896, 2 * TOPK, U32), choice(928, 2 * TOPK)
        keys_f = choice(960, 2 * TOPK)
        top_w = [choice(992 + n * TOPK, TOPK) for n in range(2)]
        top_sum = choice(1024, 1)
        all_experts = choice(1040, NT * NSLOT, U32)

        pp = ctx.enter_context(nc.psum_tensor("pp", [P, 2, 2, HALF], F32))
        pa = ctx.enter_context(nc.psum_tensor("pa", [P, 4 * HALF], F32))

        def col(name, n=0, k=1):
            a = COL_AT[name][0]
            return colt[:, a + n:a + n + k]

        def slot(u):
            a = (u % RING) * UNIT
            return ring[:, a:a + UNIT].rearrange("p (k n) -> p k n", k=KC)

        x3 = xs[:, :].rearrange("p (t d) -> p t d", t=NT)
        h3 = hT[:, :].rearrange("p (k n) -> p k n", k=KC)
        xl3 = xl[:, :].rearrange("p (k n) -> p k n", k=KC)
        xc3 = xc[:, :].rearrange("p (k n) -> p k n", k=KC)
        rg3 = rg[:, :].rearrange("p (k n) -> p k n", k=KC)
        ig3 = ig[:, :].rearrange("p (k n) -> p k n", k=KC)
        gl3 = gl[:, :].rearrange("p (k n) -> p k n", k=KC)
        qT3 = qT[:, :].rearrange("p (h n) -> p h n", h=HEADS)
        kT3 = kT[:, :].rearrange("p (h n) -> p h n", h=HEADS)
        v3 = vv[:, :].rearrange("p (t d) -> p t d", t=NT)
        ga3 = ga[:, :].rearrange("p (t d) -> p t d", t=NT)
        pa8 = pa[:, :].rearrange("p (k n) -> p k n", k=8)

        ring_free = [(UNIT_AT[name] % RING) * UNIT for name in ("wq2", "wq3")]
        u_rows = [b[:, n * D:(n + 1) * D] for b in (ga, gl, sm, tail) for n in range(2)]
        v_rows = [ig[:, n * D:(n + 1) * D] for n in range(2)] \
            + [ring[:, a + n * D:a + (n + 1) * D] for a in ring_free for n in range(4)][:NBUF - 2]
        u_here = [ctx.enter_context(nc.semaphore(f"u_here{i}")) for i in range(NBUF)]
        v_here = [ctx.enter_context(nc.semaphore(f"v_here{i}")) for i in range(NBUF)]

        nq3 = nq[:, :].rearrange("p (t n) -> p t n", t=NT)
        nT3 = at2.nT[:, :].rearrange("p (k n) -> p k n", k=KC)
        def peer_q(j):
            return (qT if j < PEER_HEADS else kT)[:, (j % PEER_HEADS) * SEQ:(j % PEER_HEADS + 1) * SEQ]

        pscore_psum = [pa[:, n * D:(n + 1) * D].rearrange("p (t m) -> p t m", t=NT) for n in range(2)]
        pscores = xc_rg[:, :].rearrange("p (t m) -> p t m", t=NT)

        STEPS2 = [(t, w) for t in (1, 0) for w in range(2)]
        pp_flat = pp[:, :, :, :].rearrange("p a b n -> p (a b n)")
        att_psum = (pp_flat, pa[:, :], pa[:, D:2 * D], pa[:, 0:D])
        att_shift = (st2[:, 80:88], small2[:, 1512:1520])
        att_sums = (st2[:, 88:96], small2[:, 1520:1528])

        def score2(buf, t):
            return buf[:, 0:NSA_HEADS * P * (t + 1)].rearrange("p (h n) -> p h n", h=NSA_HEADS)

        cmp_psum, hid_psum = pa[:, 3 * HALF:3 * HALF + 256], pa[:, 3 * HALF + 256:3 * HALF + 320]
        kcT_psum, cs_psum = pa[:, 3 * HALF + 320:3 * HALF + 320 + NCMP], pa[:, 2 * HALF:2 * HALF + 256]

        STEPS = [(g, t) for g in range(HEADS // GRP) for t in range(NT)]

        def score_bank(t):
            n = P * (t + 1)
            return pa[:, :].rearrange("p (c h n) -> p c h n", c=2, h=GRP)[:, :, :, 0:n]

        def score_sbuf(t):
            n = P * (t + 1)
            return sm[:, :].rearrange("p (c h n) -> p c h n", c=2, h=GRP)[:, :, :, 0:n]

        block = ctx.enter_context(nc.Block())

        @block.sync
        def _(sp):
            sp.dma_start(x3, x.rearrange("(t p) d -> p t d", p=P)).then_inc(s["x_loaded"], 16)
            sp.dma_start(colt[:, :], cols).then_inc(s["cols_loaded"], 16)
            for u in range(len(UNITS)):
                if u >= RING:
                    sp.wait_ge(s["unit_used"], u - RING + 1)
                a = (u % RING) * UNIT
                sp.dma_start(ring[:, a:a + UNIT], wall[u]).then_inc(unit_ready[u % RING], 16)
                if UNITS[u] == "wq0":
                    sp.wait_ge(s["update_full"], 1)
                    sp.dma_start(lt[:, :], sub_keys).then_inc(s["keys_loaded"], 16)
            for t in range(NT):
                for c in range(2):
                    sp.wait_ge(s["y_made"], t * 2 + c + 1)
                    mine = slice(c * HALF, (c + 1) * HALF)
                    sp.dma_start(out[t * P:(t + 1) * P, mine], x3[:, t, mine]).then_inc(s["stored"], 16)
            sp.wait_ge(s["stored"], 16 * NT * 2)

        @block.gpsimd
        def _(pool):
            def step(ins):
                step.n += 1
                ins.then_inc(s["pool_step"], 1)
                pool.wait_ge(s["pool_step"], step.n)
            step.n = 0

            pool.dma_start(lamt[:, :], lambdas.broadcast_to([P, 4 * QK])).then_inc(s["lambdas_loaded"], 16)
            pool.dma_start(post_g[:, :], rows[0:1, :].broadcast_to([P, D])).then_inc(s["rows_loaded"], 16)
            nc.gpsimd.memset(ident[:, :], 0.0)
            nc.gpsimd.memset(zero[:, :], 0.0)
            step(nc.gpsimd.memset(mask1[:, :], 0.0))
            nc.gpsimd.affine_select(out=ident[:, :], in_=ident[:, :], compare_op=ALU.not_equal, fill=1.0,
                                    base=0, pattern=[[-1, P]], channel_multiplier=1).then_inc(s["identity_made"], 1)
            nc.gpsimd.affine_select(out=mask1[:, :], in_=mask1[:, :], compare_op=ALU.is_ge, fill=NEG,
                                    base=P, pattern=[[-1, SEQ]], channel_multiplier=1).then_inc(s["consts_made"], 1)
            nc.gpsimd.iota(dist_ci.rearrange("p (t n) -> p t n", t=NT), pattern=[[P, NT], [-CMP_STRIDE, 16]],
                           base=1 - CMP_LEN, channel_multiplier=1)
            step(nc.gpsimd.iota(iota16i, pattern=[[1, 16]], base=0, channel_multiplier=0))
            nc.gpsimd.tensor_copy(iota16, iota16i)
            step(nc.gpsimd.tensor_copy(dist_c, dist_ci))
            bc = bias_c.rearrange("p (g t r n) -> p g t r n", g=NKV, t=NT, r=REP)
            mc = mask_c.rearrange("p (g t r n) -> p g t r n", g=NKV, t=NT, r=REP)
            dc = dist_c.rearrange("p (t n) -> p t n", t=NT)
            for h in range(NSA_HEADS):
                ins = nc.gpsimd.tensor_scalar(mc[:, h // REP, :, h % REP, :], dc, 0.0, None, ALU.is_ge)
            step(ins)
            step(nc.gpsimd.affine_select(out=dist_c, in_=dist_c, compare_op=ALU.is_ge, fill=-NEG, base=1 - CMP_LEN,
                                         pattern=[[P, NT], [-CMP_STRIDE, 16]], channel_multiplier=1))
            for h in range(NSA_HEADS):
                ins = nc.gpsimd.tensor_scalar(bc[:, h // REP, :, h % REP, :], dc, -SLOPES[h], None, ALU.mult)
            step(ins)
            pool.wait_ge(s["block1_done"], 1)
            b3 = at2.bias[:, :].rearrange("p (h n) -> p h n", h=NSA_HEADS)
            step(nc.gpsimd.iota(b3[:, 7, :].bitcast(I32), pattern=[[-1, SEQ]], base=P, channel_multiplier=1))
            step(nc.gpsimd.tensor_copy(mask1[:, :], b3[:, 7, :].bitcast(I32)))
            step(nc.gpsimd.affine_select(out=mask1[:, :], in_=mask1[:, :], compare_op=ALU.is_ge, fill=-NEG,
                                         base=P, pattern=[[-1, SEQ]], channel_multiplier=1))
            step(nc.gpsimd.memset(at2.scan_mask, 1.0))
            nc.gpsimd.memset(at2.scan_mask.rearrange("p (c n) -> p c n", n=CH)[:, :, 0:1], 0.0)\
                .then_inc(s["scan_mask_made"], 1)
            for h in range(NSA_HEADS):
                ins = nc.gpsimd.tensor_scalar(b3[:, h, :], mask1[:, :], -SLOPES[h], None, ALU.mult)
            ins.then_inc(s["bias2_made"], 1)
            pool.wait_ge(s["block1_done"], NT)
            pool.dma_start(post_g[:, :], rows[1:2, :].broadcast_to([P, D])).then_inc(s["rows_loaded"], 16)
            pool.wait_ge(s["bias2_made"], 1)
            pool.wait_ge(s["intra_moved"], 1)
            for half in range(2):
                if half:
                    pool.wait_ge(s["intra_masked"], 1)
                a = at2.intra[half * CH:(half + 1) * CH, :].rearrange("p (c n) -> p c n", n=CH)
                nc.gpsimd.affine_select(out=a, in_=a, compare_op=ALU.is_ge, fill=0.0, base=0,
                                        pattern=[[0, HG_HEADS * NT], [1, CH]], channel_multiplier=-1)\
                    .then_inc(s["intra_masked"], 1)

            pool.wait_ge(s["intra_masked"], 2)
            def indices(kind, parity, head):
                pool.wait_ge(s["chosen"], head + 1)
                pool.sem_inc(s["pace"], 1)
                nc.gpsimd.tensor_copy(cur[kind][parity], all_experts[:, bass.ds(head * TOPK, TOPK)])\
                    .then_inc(s["cur_made"], 1)

            def gather(kind, parity, head, k):
                table, rows_to, here, free = ((peer_u, u_rows, u_here, "u_free"),
                                              (peer_v, v_rows, v_here, "v_free"))[kind]
                if kind == 1 and k == 2:
                    pool.wait_ge(s["unit_used"], UNIT_AT["wq3"] + 1)
                if k % BATCH == 0:
                    pool.wait_ge(s[free], head * TOPK + k + BATCH)
                    pool.sem_inc(s["pace"], 1)
                nc.gpsimd.indirect_dma_start(out=rows_to[k % NBUF], out_offset=None, in_=table,
                                             in_offset=bass.IndirectOffsetOnAxis(ap=cur[kind][parity][:, k:k + 1], axis=0))\
                    .then_inc(here[k % NBUF], 16)

            def gather_step(n, parity):
                indices(0, parity, n + 1)
                indices(1, parity, n)
                pool.wait_ge(s["cur_made"], 2 * n + 3)
                for k in range(TOPK):
                    gather(0, parity, n + 1, k)
                    gather(1, parity, n, k)

            pool.wait_ge(s["unit_used"], UNIT_AT["wp1"] + 1)
            indices(0, 1, 0)
            pool.wait_ge(s["cur_made"], 1)
            for k in range(TOPK):
                gather(0, 1, 0, k)
            last = LAST_HEAD
            with pool.Fori(0, last // 2) as pair:
                for parity in range(2):
                    gather_step(pair * 2 + parity, parity)
            gather_step(last - 1, 0)
            indices(1, 1, last)
            pool.wait_ge(s["cur_made"], 2 * last + 2)
            for k in range(TOPK):
                gather(1, 1, last, k)

        @block.tensor
        def _(pe):
            outs = [0]

            def begin_output():
                if outs[0] >= 2:
                    pe.wait_ge(s["proj_moved"], outs[0] - 1)
                buf = pp[:, outs[0] % 2]
                outs[0] += 1
                return buf

            def take_unit(name):
                u = UNIT_AT[name]
                pe.wait_ge(unit_ready[u % RING], 16 * (u // RING + 1))
                return slot(u)

            def turn_norm(m, src, t):
                pe.wait_ge(s["scaled"], m + 1)
                for k in range(KC):
                    ins = nc.tensor.transpose(pa[:, t * D + k * P:t * D + (k + 1) * P],
                                              src[:, k * P:(k + 1) * P], ident[:, :])
                ins.then_inc(s["turned"], 1)

            def feature_major(name):
                w = take_unit(name)
                buf = begin_output().rearrange("p a (b n) -> p (a b) n", b=2)
                for c in range(4):
                    for k in range(KC):
                        ins = nc.tensor.matmul(buf[:, c, :], w[:, k, c * P:(c + 1) * P], h3[:, k, :],
                                               start=(k == 0), stop=(k == KC - 1))
                return ins

            def token_major(name, width=HALF):
                w = take_unit(name)
                buf = begin_output()
                for t in range(NT):
                    for k in range(KC):
                        ins = nc.tensor.matmul(buf[:, t, 0:width], h3[:, k, t * P:(t + 1) * P], w[:, k, 0:width],
                                               start=(k == 0), stop=(k == KC - 1))
                return ins

            def done(ins, name):
                ins.then_inc(s["unit_used"], 1)

            def scores(a):
                g, t = STEPS[a]
                if a == 0:
                    pe.wait_ge(s["igate_moved"], 1)
                    pe.wait_ge(s["proj_moved"], OUT_AT["k1"] + 1)
                else:
                    pe.wait_ge(s["turned_moved"], a)
                    pe.wait_ge(s["heads_moved"], a)
                n = P * (t + 1)
                for c in range(2):
                    for h in range(GRP):
                        ins = nc.tensor.matmul(score_bank(t)[:, c, h, :],
                                               qT3[c * QK:(c + 1) * QK, g * GRP + h, t * P:(t + 1) * P],
                                               kT3[c * QK:(c + 1) * QK, g * GRP + h, 0:n], start=True, stop=True)
                ins.then_inc(s["scores_full"], 1)

            def turn_weights(a):
                g, t = STEPS[a]
                pe.wait_ge(s["weights_made"], a + 1)
                for h in range(GRP):
                    for kb in range(t + 1):
                        n = h * (t + 1) + kb
                        ins = nc.tensor.transpose(pa[:, n * P:(n + 1) * P],
                                                  score_sbuf(t)[:, 0, h, kb * P:(kb + 1) * P], ident[:, :])
                ins.then_inc(s["weights_turned"], 1)

            def values(a):
                g, t = STEPS[a]
                pe.wait_ge(s["turned_moved"], a + 1)
                pe.wait_ge(s["proj_moved"], OUT_AT["v1"] + 1)
                for h in range(GRP):
                    for kb in range(t + 1):
                        n = h * (t + 1) + kb
                        ins = nc.tensor.matmul(pa[:, 2 * HALF + h * P:2 * HALF + (h + 1) * P],
                                               wT[:, n * P:(n + 1) * P],
                                               v3[:, kb, (g * GRP + h) * P:(g * GRP + h + 1) * P],
                                               start=(kb == 0), stop=(kb == t))
                ins.then_inc(s["heads_full"], 1)

            pe.wait_ge(s["identity_made"], 1)
            for t in range(NT):
                turn_norm(t, vv[:, t * D:(t + 1) * D], t)
            pe.wait_ge(s["normed"], NT)
            for name in ("xl0", "xl1", "q0", "q1"):
                done(feature_major(name), name)
            w = take_unit("lru").rearrange("p k n -> p (k n)")
            pe.wait_ge(s["conv_done"], 1)
            for n in range(KC):
                ins = nc.tensor.matmul(pa8[:, n, :], w[:, n * P:(n + 1) * P], xc3[:, n, :], start=True, stop=True)
            ins.then_inc(s["rgate_full"], 1)
            pe.wait_ge(s["rgate_moved"], 1)
            for n in range(KC):
                ins = nc.tensor.matmul(pa8[:, n, :], w[:, D + n * P:D + (n + 1) * P], xc3[:, n, :],
                                       start=True, stop=True)
            ins.then_inc(s["unit_used"], 1)
            for name in ("k0", "k1"):
                done(feature_major(name), name)
            for name in ("v0", "v1"):
                done(token_major(name), name)
            for a, name in enumerate(("ga0", "ga1", "gl0", "gl1")):
                scores(a)
                done(token_major(name) if name[:2] == "ga" else feature_major(name), name)
                turn_weights(a)
                values(a)
            bufs = [begin_output(), begin_output()]
            pe.wait_ge(s["lru_done"], 1)
            for c in range(2):
                w = take_unit(f"wol{c}")
                for t in range(NT):
                    for k in range(KC):
                        ins = nc.tensor.matmul(bufs[c][:, t, :], gl3[:, k, t * P:(t + 1) * P], w[:, k, :],
                                               start=(k == 0), stop=False)
                ins.then_inc(s["unit_used"], 1)
            for t in range(NT):
                pe.wait_ge(s["head_gated"], NT + 1 + t)
                if t == 0:
                    pe.wait_ge(s["heads_moved"], len(STEPS))
                for k in range(KC):
                    ins = nc.tensor.transpose(pa[:, t * D + k * P:t * D + (k + 1) * P],
                                              ga3[:, t, k * P:(k + 1) * P], ident[:, :])
                ins.then_inc(s["attn_turned"], 1)
            wo = [take_unit(f"woa{c}") for c in range(2)]
            for t in range(NT):
                pe.wait_ge(s["attn_moved"], t + 1)
                for c in range(2):
                    for k in range(KC):
                        ins = nc.tensor.matmul(bufs[c][:, t, :], h3[:, k, t * P:(t + 1) * P], wo[c][:, k, :],
                                               start=False, stop=(k == KC - 1))
                    if t == NT - 1:
                        ins.then_inc(s["unit_used"], 1)
                if t == 0:
                    ins.then_inc(s["wo_full"], 1)

            turn_norm(2, vv[:, 0:D], 0)
            w = take_unit("nq")
            buf = begin_output()
            for t in range(NT):
                if t:
                    turn_norm(3, vv[:, D:2 * D], 1)
                pe.wait_ge(s["normed"], NT + t + 1)
                for k in range(KC):
                    ins = nc.tensor.matmul(buf[:, t, :], h3[:, k, t * P:(t + 1) * P], w[:, k, :],
                                           start=(k == 0), stop=(k == KC - 1))
            done(ins, "nq")
            done(token_major("nk"), "nk")
            done(feature_major("hf"), "hf")
            for t in range(NT):
                pe.wait_ge(s["nsa_scaled"], t + 1)
                for k in range(KC):
                    ins = nc.tensor.transpose(pa[:, t * D + k * P:t * D + (k + 1) * P],
                                              nq3[:, t, k * P:(k + 1) * P], ident[:, :])
                ins.then_inc(s["nsa_turned"], 1)
            done(feature_major("hq"), "hq")
            w = take_unit("cmp").rearrange("p k n -> p (k n)")
            pe.wait_ge(s["cmp_in"], 1)
            for g in range(NKV):
                half = slice(g * DH, (g + 1) * DH)
                for kv in range(2):
                    for j in range(CMP_LEN):
                        src = (at2.pe0 if j < CMP_STRIDE else at2.pe1)[half, kv * SEQ:(kv + 1) * SEQ]
                        n = (kv * CMP_LEN + j) * DH
                        ins = nc.tensor.matmul(hid_psum[half, kv * 16:kv * 16 + NCMP],
                                               w[half, n:n + DH],
                                               src[:, j:j + CMP_STRIDE * (NCMP - 1) + 1:CMP_STRIDE],
                                               start=(j == 0), stop=(j == CMP_LEN - 1))
            ins.then_inc(s["unit_used"], 1)
            done(token_major("hi"), "hi")
            pe.wait_ge(s["recur_ready"], 1)
            for h in range(HG_HEADS):
                for t in range(NT):
                    n = h * NT + t
                    ins = nc.tensor.transpose(pa[:, n * P:(n + 1) * P],
                                              at2.k4[:, h * SEQ + t * P:h * SEQ + (t + 1) * P], ident[:, :])
            ins.then_inc(s["keys_turned"], 1)
            for h in range(HG_HEADS):
                for c in range(NCH):
                    a = h * SEQ + c * CH
                    o = 2 * HALF + (h * NT + c // 2) * CH
                    half = slice((c % 2) * CH, (c % 2 + 1) * CH)
                    ins = nc.tensor.matmul(pa[half, o:o + CH], at2.k2[:, a:a + CH], at2.q1[:, a:a + CH],
                                           start=True, stop=True)
            ins.then_inc(s["intra_full"], 1)
            done(token_major("hg"), "hg")
            pe.wait_ge(s["hid_made"], 1)
            for g in range(NKV):
                half = slice(g * DH, (g + 1) * DH)
                for kv in range(2):
                    ins = nc.tensor.matmul(cmp_psum[0:NCMP, (g * 2 + kv) * DH:(g * 2 + kv + 1) * DH],
                                           hid[half, kv * 16:kv * 16 + NCMP], col("cmp_w2", kv * DH, DH)[half, :],
                                           start=True, stop=True)
                if g == 0:
                    ins.then_inc(s["group_done"], 1)
                    pe.wait_ge(s["group_done"], 1)
            ins.then_inc(s["cmp_full"], 1)
            pe.wait_ge(s["keys_moved"], 1)
            pe.wait_ge(s["proj_moved"], OUT_AT["hi"] + 1)
            pe.wait_ge(s["intra_moved"], 1)
            for c, bank in enumerate(UPDATE_BANKS):
                half = slice((c % 2) * CH, (c % 2 + 1) * CH)
                for h in range(HG_HEADS):
                    n = h * NT + c // 2
                    ins = nc.tensor.matmul(pa[:, bank * HALF + h * P:bank * HALF + (h + 1) * P],
                                           at2.k_tok[half, n * P:(n + 1) * P],
                                           at2.v[half, (c // 2) * HALF + h * P:(c // 2) * HALF + (h + 1) * P],
                                           start=True, stop=True)
            ins.then_inc(s["update_full"], 1)
            done(token_major("nv", NQW - 2 * HALF), "nv")

            pe.wait_ge(s["cmp_ready"], 1)
            nc.tensor.transpose(kcT_psum, cmp_tok[0:NCMP, 0:P], ident[0:NCMP, 0:NCMP])\
                .then_inc(s["cmp_turned"], 1)
            pe.wait_ge(s["states_made"], 1)
            pe.wait_ge(s["cmpT_made"], 1)
            for g in range(NKV):
                half = slice(g * DH, (g + 1) * DH)
                for t in range(NT):
                    for r in range(REP):
                        a = g * P + (t * REP + r) * 16
                        ins = nc.tensor.matmul(cs_psum[:, a:a + NCMP], nT3[half, r, t * P:(t + 1) * P],
                                               kcT[half, 0:NCMP], start=True, stop=True)
                if g == 0:
                    ins.then_inc(s["group_done"], 1)
                    pe.wait_ge(s["group_done"], 2)
            ins.then_inc(s["cs_full"], 1)
            pe.wait_ge(s["intra_masked"], 2)
            for c in range(NCH):
                half = slice((c % 2) * CH, (c % 2 + 1) * CH)
                for h in range(HG_HEADS):
                    o = pa[half, (c // 2) * HALF + h * P:(c // 2) * HALF + (h + 1) * P]
                    n = (h * NT + c // 2) * CH
                    ins = nc.tensor.matmul(o, at2.intra[half, n:n + CH],
                                           at2.v[half, (c // 2) * HALF + h * P:(c // 2) * HALF + (h + 1) * P],
                                           start=True, stop=(c == 0))
                    if c:
                        a = h * SEQ + c * CH
                        ins = nc.tensor.matmul(o, at2.q3[:, a:a + CH],
                                               at2.states[:, (c - 1) * HALF + h * P:(c - 1) * HALF + (h + 1) * P],
                                               start=False, stop=True)
            ins.then_inc(s["o_full"], 1)

            def att_scores(b):
                t, w = STEPS2[b]
                for h in range(NSA_HEADS):
                    half = slice(h // REP * DH, (h // REP + 1) * DH)
                    ins = nc.tensor.matmul(score2(att_psum[b], t)[:, h, :], nT3[half, h % REP, t * P:(t + 1) * P],
                                           nT3[half, 4 + w, 0:(t + 1) * P], start=True, stop=True)
                ins.then_inc(s["att_full"], 1)

            def att_turn(b):
                t, w = STEPS2[b]
                pe.wait_ge(s["att_exp"], b + 1)
                for h in range(NSA_HEADS):
                    for kb in range(t + 1):
                        n = h * (t + 1) + kb
                        ins = nc.tensor.transpose(att_psum[b][:, n * P:(n + 1) * P],
                                                  score2(at2.sc[b % 2], t)[:, h, kb * P:(kb + 1) * P], ident[:, :])
                ins.then_inc(s["att_turned"], 1)

            def att_values(b):
                t, w = STEPS2[b]
                pe.wait_ge(s["att_moved"], b + 1)
                for h in range(NSA_HEADS):
                    for kb in range(t + 1):
                        n = h * (t + 1) + kb
                        a = D + w * P + h // REP * DH
                        ins = nc.tensor.matmul(att_psum[b][:, h * DH:(h + 1) * DH],
                                               at2.pT[b % 2][:, n * P:(n + 1) * P],
                                               nq3[:, kb, a:a + DH], start=(kb == 0), stop=(kb == t))
                ins.then_inc(s["ao_full"], 1)

            pe.wait_ge(s["proj_moved"], OUT_AT["nv"] + 1)
            att_scores(0)
            pe.wait_ge(s["o_moved"], 1)
            pe.wait_ge(s["cs_ready"], 1)
            for n in range(NT * NSA_HEADS):
                ins = nc.tensor.transpose(pa[0:NCMP, n * P:(n + 1) * P], e_c[:, n * 16:n * 16 + NCMP], ident[:, :])
            ins.then_inc(s["cs_turned"], 1)
            pe.wait_ge(s["csT_moved"], 1)
            for t in range(NT):
                for h in range(NSA_HEADS):
                    n = (h // REP * NT + t) * REP + h % REP
                    a = D + t * HALF + h * DH
                    ins = nc.tensor.matmul(pa[:, a:a + DH], at2.cT[0:NCMP, n * P:(n + 1) * P],
                                           cmp_tok[0:NCMP, P + h // REP * DH:P + (h // REP + 1) * DH],
                                           start=True, stop=True)
            ins.then_inc(s["co_full"], 1)
            att_turn(0)
            pe.wait_ge(s["co_used"], 1)
            att_scores(1)
            att_values(0)

            pe.wait_ge(s["ao_used"], 1)
            pe.wait_ge(s["o_gated"], 1)
            for k in range(4):
                for t in range(NT):
                    ins = nc.tensor.transpose(pp_flat[:, k * SEQ + t * P:k * SEQ + (t + 1) * P],
                                              at2.o[:, t * HALF + k * P:t * HALF + (k + 1) * P], ident[:, :])
            ins.then_inc(s["mix_turned"], 1)
            att_turn(1)
            att_values(1)
            att_scores(2)
            pe.wait_ge(s["ao_used"], 2)
            att_scores(3)

            wp = [take_unit(f"wp{c}") for c in range(2)]

            def mixed(t, ks):
                for c in range(2):
                    for k in ks:
                        ins = nc.tensor.matmul(pp[:, c, t, :], h3[:, k, t * P:(t + 1) * P], wp[c][:, k, :],
                                               start=(k == 0), stop=(k == KC - 1))
                    if (t, ks[-1]) == (0, KC - 1):
                        ins.then_inc(s["unit_used"], 1)
                return ins

            def turn_sparse(t, to):
                pe.wait_ge(s["nsa_out"], NT - t)
                for k in range(4):
                    ins = nc.tensor.transpose(to[:, k * P:(k + 1) * P],
                                              at2.no[:, t * HALF + k * P:t * HALF + (k + 1) * P], ident[:, :])
                ins.then_inc(s["mix_turned"], 1)

            pe.wait_ge(s["mixT_made"], 1)
            for t in range(NT):
                mixed(t, range(4))
            outs[0] += 2
            att_turn(2)
            att_values(2)
            turn_sparse(1, pa[:, 3 * HALF:4 * HALF])
            att_turn(3)
            att_values(3)
            pe.wait_ge(s["mixT_made"], 2)
            mixed(1, range(4, KC)).then_inc(s["wp_full"], 1)
            turn_sparse(0, pa[:, HALF:2 * HALF])
            pe.wait_ge(s["mixT_made"], 3)
            mixed(0, range(4, KC))

            turn_norm(4, vv[:, D:2 * D], 1)
            w = take_unit("ple").rearrange("p k n -> p (k n)")
            for c in range(2):
                buf = begin_output()
                for t in range(NT):
                    for k in range(PLE // P):
                        ins = nc.tensor.matmul(buf[:, t, :], w[:, 2 * D + k * SEQ + t * P:2 * D + k * SEQ + (t + 1) * P],
                                               w[:, k * D + c * HALF:k * D + (c + 1) * HALF],
                                               start=(k == 0), stop=(k == PLE // P - 1))
                if c == 0:
                    ins.then_inc(s["ple_full"], 1)
                    turn_norm(5, vv[:, 0:D], 0)
            ins.then_inc(s["unit_used"], 1)
            pe.wait_ge(s["normed"], 3 * NT)
            keys = lt[:, :]
            for c in range(4):
                if c == 0:
                    pe.wait_ge(s["keys_loaded"], 16)
                done(feature_major(f"wq{c}"), f"wq{c}")
                pe.wait_ge(s["proj_moved"], OUT_AT[f"wq{c}"] + 1)
                if c >= 2:
                    pe.wait_ge(s["pscore_moved"], c - 1)
                for t in range(NT):
                    for n in range(4):
                        j = 4 * c + n
                        ins = nc.tensor.matmul(pscore_psum[c % 2][:, t, n * P:(n + 1) * P],
                                               peer_q(j)[:, t * P:(t + 1) * P],
                                               keys[:, j * NKEYS:(j + 1) * NKEYS], start=True, stop=True)
                ins.then_inc(s["pscore_full"], 1)
            for t in range(NT):
                for c in range(2):
                    nc.tensor.matmul(pp[:, t, c, :], ident[:, :], x3[:, t, c * HALF:(c + 1) * HALF],
                                     start=True, stop=True)

            def expert_sums(t, head):
                for k in range(TOPK):
                    pe.wait_ge(s["diag_made"], head * TOPK + k + 1)
                    pe.wait_ge(v_here[k % NBUF], (head * 2 + k // NBUF + 1) * 16)
                    n = k % DIAGS
                    for c in range(2):
                        ins = nc.tensor.matmul(pp[:, t, c, :], diag[:, n * P:(n + 1) * P],
                                               v_rows[k % NBUF][:, c * HALF:(c + 1) * HALF],
                                               start=False, stop=True, skip_group_check=True)
                    ins.then_inc(s["v_free"], 1)

            def embedding_gate(t, c):
                w = take_unit(f"gw{c}")
                for k in range(KC):
                    ins = nc.tensor.matmul(pp[:, t, c, :], h3[:, k, t * P:(t + 1) * P], w[:, k, :],
                                           start=(k == 0), stop=(k == KC - 1))
                ins.then_inc(s["gate_full"], 1)

            with pe.Fori(0, PEER_HEADS // 2) as pair:
                for odd in range(2):
                    expert_sums(0, pair * 2 + odd)
            expert_sums(1, PEER_HEADS)
            turn_norm(6, vv[:, 0:D], 0)
            pe.wait_ge(s["normed"], 3 * NT + 1)
            embedding_gate(0, 0)
            expert_sums(1, PEER_HEADS + 1)
            embedding_gate(0, 1)
            with pe.Fori(PEER_HEADS // 2 + 1, PEER_HEADS) as pair:
                for odd in range(2):
                    expert_sums(1, pair * 2 + odd)
            turn_norm(7, vv[:, D:2 * D], 1)
            pe.wait_ge(s["normed"], 4 * NT)
            for c in range(2):
                embedding_gate(1, c)

        @block.scalar
        def _(act):
            def full(name):
                unit = {"wo0": "woa0", "wo1": "woa1"}.get(name, name)
                act.wait_ge(s["unit_used"], UNIT_AT[unit] + 1)
                return pp[:, OUT_AT[name] % 2]

            def step(ins):
                step.n += 1
                ins.then_inc(s["act_step"], 1)
                act.wait_ge(s["act_step"], step.n)
            step.n = 0

            def move(name, dst, func=ACT.Copy, width=HALF):
                nc.scalar.activation(dst, full(name)[:, :, 0:width], func).then_inc(s["proj_moved"], 1)

            def norm_std(m):
                act.wait_ge(s["squares_summed"], m + 1)
                nc.scalar.activation(stat[:, 16 + m:17 + m], stat[:, m:m + 1], ACT.Sqrt, bias=eps_col, scale=1.0 / D)\
                    .then_inc(s["std_made"], 1)

            eps_col = small[:, 250:251]
            for t in range(NT):
                norm_std(t)
            for c in range(2):
                nc.scalar.activation(xl3[:, 4 * c:4 * c + 4, PAD:XS],
                                     full(f"xl{c}").rearrange("p a (b n) -> p (a b) n", b=2), ACT.Copy)\
                    .then_inc(s["proj_moved"], 1)
            act.wait_ge(s["lambda_sums"], 1)
            nc.scalar.activation(small[:, 2:4], small[:, 0:2], ACT.Exp)
            nc.scalar.activation(small[:, 16:24], small[:, 8:16], ACT.Exp, scale=-1.0).then_inc(s["lambda_exps"], 1)
            for c in range(2):
                move(f"q{c}", qT[:, c * D:(c + 1) * D].rearrange("p (a n) -> p a n", a=2))
            act.wait_ge(s["rgate_full"], 1)
            for n in range(KC):
                ins = nc.scalar.activation(rg3[:, n, :], pa8[:, n, :], ACT.Sigmoid, bias=col("b_r", n))
            ins.then_inc(s["rgate_moved"], 1)
            act.wait_ge(s["unit_used"], UNIT_AT["lru"] + 1)
            for n in range(KC):
                ins = nc.scalar.activation(ig3[:, n, :], pa8[:, n, :], ACT.Sigmoid, bias=col("b_i", n))
            ins.then_inc(s["igate_moved"], 1)
            act.wait_ge(s["decay_log"], 1)
            nc.scalar.activation(lt[:, :], rg[:, :], ACT.Tanh).then_inc(s["tanh_made"], 1)
            step(nc.scalar.activation(xl[:, 0:KC * SEQ], rg[:, :], ACT.Exp, scale=-1.0))
            for c in range(2):
                move(f"k{c}", kT[:, c * D:(c + 1) * D].rearrange("p (a n) -> p a n", a=2))
            act.wait_ge(s["mult_sq"], 1)
            nc.scalar.activation(lt[:, :], lt[:, :], ACT.Sqrt, scale=2.0).then_inc(s["mult_made"], 1)
            for c in range(2):
                move(f"v{c}", v3[:, :, c * HALF:(c + 1) * HALF])
            for a, name in enumerate(("ga0", "ga1", "gl0", "gl1")):
                g, t = STEPS[a]
                act.wait_ge(s["bias_made"], a + 1)
                for n in range(2 * GRP):
                    src = score_sbuf(t)[:, n // GRP, n % GRP, :]
                    ins = nc.scalar.activation(src, src, ACT.Exp, bias=small[:, 40 + n:41 + n], scale=SCALE1,
                                               accum_out=small[:, 48 + n:49 + n])
                ins.then_inc(s["probs_made"], 1)
                if name[:2] == "ga":
                    move(name, ga3[:, :, (a % 2) * HALF:(a % 2 + 1) * HALF], ACT.Silu)
                else:
                    c = a % 2
                    move(name, gl[:, c * D:(c + 1) * D].rearrange("p (a n) -> p a n", a=2), ACT.Silu)
                act.wait_ge(s["weights_turned"], a + 1)
                n = GRP * (t + 1) * P
                nc.scalar.activation(wT[:, 0:n], pa[:, 0:n], ACT.Copy).then_inc(s["turned_moved"], 1)
                act.wait_ge(s["heads_full"], a + 1)
                if a:
                    act.wait_ge(s["head_gated"], a)
                nc.scalar.activation(oh[:, :], pa[:, 2 * HALF:3 * HALF], ACT.Copy).then_inc(s["heads_moved"], 1)
                act.wait_ge(s["head_sums"], a + 1)
                nc.scalar.activation(small[:, 64:68], small[:, 60:64], ACT.Sqrt, bias=eps_col, scale=1.0 / P)\
                    .then_inc(s["head_std"], 1)
            for t in range(NT):
                act.wait_ge(s["attn_turned"], t + 1)
                nc.scalar.activation(h3[:, :, t * P:(t + 1) * P],
                                     pa[:, t * D:(t + 1) * D].rearrange("p (k n) -> p k n", k=KC),
                                     ACT.Copy, scale=small[:, 80:81]).then_inc(s["attn_moved"], 1)
            for t in range(NT):
                if t == 0:
                    act.wait_ge(s["wo_full"], 1)
                else:
                    act.wait_ge(s["unit_used"], UNIT_AT["woa1"] + 1)
                for c in range(2):
                    ins = nc.scalar.activation(junk1[:, c * HALF:(c + 1) * HALF], pp[:, c, t, :], ACT.Square,
                                               accum_out=stat[:, 32 + 2 * c + t:33 + 2 * c + t])
                step(ins)
                step(nc.scalar.activation(stat[:, 36 + t:37 + t], stat[:, 32 + t:33 + t], ACT.Identity,
                                          bias=stat[:, 34 + t:35 + t]))
                nc.scalar.activation(stat[:, 38 + t:39 + t], stat[:, 36 + t:37 + t], ACT.Sqrt, bias=eps_col,
                                     scale=1.0 / D).then_inc(s["post_std"], 1)
                norm_std(2 + t)

            act.wait_ge(s["lb_shifted"], 1)
            nc.scalar.activation(lbt[:, 4:12], lbt[:, 4:12], ACT.Exp).then_inc(s["lb_exp"], 1)
            move("nq", nq3[:, :, 0:HALF])
            move("nk", nq3[:, :, HALF:2 * HALF])
            for t in range(NT):
                act.wait_ge(s["nsa_sums"], t + 1)
                nc.scalar.activation(st2[:, 16 + 12 * t:28 + 12 * t], st2[:, 40 + 12 * t:52 + 12 * t], ACT.Sqrt,
                                     bias=eps_col, scale=1.0 / DH).then_inc(s["nsa_std"], 1)
            nc.scalar.activation(at2.key.rearrange("p (a n) -> p a n", a=2), full("hf"), ACT.Sigmoid)\
                .then_inc(s["proj_moved"], 1)
            move("hq", at2.query.rearrange("p (a n) -> p a n", a=2), ACT.Silu)
            act.wait_ge(s["forget_made"], 1)
            nc.scalar.activation(at2.log_f, at2.key, ACT.Ln).then_inc(s["log_made"], 1)
            act.wait_ge(s["shift_made"], 1)
            nc.scalar.activation(at2.q1, at2.shift, ACT.Exp)
            nc.scalar.activation(at2.k2, at2.shift, ACT.Exp, scale=-1.0)
            nc.scalar.activation(at2.q3, at2.cum, ACT.Exp)
            nc.scalar.activation(last_exp, at2.cum[:, CH - 1::CH], ACT.Exp).then_inc(s["shift_exp"], 1)
            act.wait_ge(s["last_made"], 1)
            nc.scalar.activation(at2.k4, at2.shift, ACT.Exp).then_inc(s["last_exp"], 1)
            act.wait_ge(s["unit_used"], UNIT_AT["cmp"] + 1)
            nc.scalar.activation(hid.rearrange("p (v n) -> p v n", v=2)[:, :, 0:NCMP],
                                 hid_psum[:, 0:32].rearrange("p (v n) -> p v n", v=2)[:, :, 0:NCMP],
                                 ACT.Gelu_apprx_tanh).then_inc(s["hid_made"], 1)
            move("hi", at2.v.rearrange("p (a n) -> p a n", a=2))
            act.wait_ge(s["keys_turned"], 1)
            nc.scalar.activation(at2.k_tok, pa[:, 0:D], ACT.Copy).then_inc(s["keys_moved"], 1)
            act.wait_ge(s["intra_full"], 1)
            nc.scalar.activation(at2.intra, pa[:, 2 * HALF:3 * HALF], ACT.Copy).then_inc(s["intra_moved"], 1)
            move("hg", at2.gate.rearrange("p (a n) -> p a n", a=2), ACT.Silu)
            act.wait_ge(s["cmp_sums"], 1)
            nc.scalar.activation(st2[0:NCMP, 66:68], st2[0:NCMP, 64:66], ACT.Sqrt, bias=eps_col[0:NCMP, :],
                                 scale=1.0 / DH).then_inc(s["cmp_std"], 1)
            buf = full("nv")
            nc.scalar.activation(nq3[:, :, NQW - GATES:NQW], buf[:, :, 2 * NKV * DH:2 * NKV * DH + GATES], ACT.Sigmoid)
            nc.scalar.activation(nq3[:, :, D:NQW - GATES], buf[:, :, 0:2 * NKV * DH], ACT.Copy)\
                .then_inc(s["proj_moved"], 1)
            act.wait_ge(s["cmp_turned"], 1)
            nc.scalar.activation(kcT[:, 0:NCMP], kcT_psum, ACT.Copy, scale=col("nk_g", 0))\
                .then_inc(s["cmpT_made"], 1)
            act.wait_ge(s["cs_shifted"], 1)
            ec = e_c.rearrange("p (m n) -> p m n", n=16)[:, :, 0:NCMP]
            nc.scalar.activation(ec, ec, ACT.Exp).then_inc(s["cs_exp"], 1)
            act.wait_ge(s["o_full"], 1)
            nc.scalar.activation(at2.o, pa[:, 0:D], ACT.Copy).then_inc(s["o_moved"], 1)
            act.wait_ge(s["cs_turned"], 1)
            nc.scalar.activation(at2.cT[0:NCMP, :], pa[0:NCMP, :], ACT.Copy).then_inc(s["csT_moved"], 1)

            def att_exps(b):
                t, w = STEPS2[b]
                act.wait_ge(s["att_bias"], b + 1)
                for h in range(NSA_HEADS):
                    src = score2(at2.sc[b % 2], t)[:, h, :]
                    ins = nc.scalar.activation(src, src, ACT.Exp, bias=att_shift[b % 2][:, h:h + 1],
                                               accum_out=att_sums[b % 2][:, h:h + 1])
                ins.then_inc(s["att_exp"], 1)

            def att_move(b):
                t, w = STEPS2[b]
                act.wait_ge(s["att_turned"], b + 1)
                n = NSA_HEADS * (t + 1) * P
                nc.scalar.activation(at2.pT[b % 2][:, 0:n], att_psum[b][:, 0:n], ACT.Copy).then_inc(s["att_moved"], 1)

            def sparse_std(t):
                act.wait_ge(s["nsa_osums"], NT - t)
                nc.scalar.activation(st2[:, 112 + 8 * t:120 + 8 * t], st2[:, 96 + 8 * t:104 + 8 * t], ACT.Sqrt,
                                     bias=eps_col, scale=1.0 / DH).then_inc(s["nsa_ostd"], 1)

            att_exps(0)
            att_move(0)
            att_exps(1)
            act.wait_ge(s["o_sums"], 1)
            nc.scalar.activation(st2[:, 0:8], st2[:, 8:16], ACT.Sqrt, bias=eps_col, scale=1.0 / P)\
                .then_inc(s["o_std"], 1)
            att_move(1)
            att_exps(2)
            att_exps(3)
            sparse_std(1)
            att_move(2)
            att_move(3)
            sparse_std(0)

            for t in range(NT):
                norm_std(4 + t)
            for c in range(2):
                if c == 0:
                    act.wait_ge(s["ple_full"], 1)
                else:
                    act.wait_ge(s["unit_used"], UNIT_AT["ple"] + 1)
                nc.scalar.activation(nq[:, 0:2 * D].rearrange("p (t d) -> p t d", t=NT)
                                     [:, :, c * HALF:(c + 1) * HALF], pp[:, OUT_AT[f"ple{c}"] % 2], ACT.Copy)\
                    .then_inc(s["proj_moved"], 1)
            for c in range(4):
                b = (qT if c < 2 else kT)[:, (c % 2) * D:(c % 2 + 1) * D]
                move(f"wq{c}", b.rearrange("p (a n) -> p a n", a=2))
                act.wait_ge(s["pscore_full"], c + 1)
                nc.scalar.activation(pscores[:, :, c * HALF:(c + 1) * HALF], pscore_psum[c % 2], ACT.Copy)\
                    .then_inc(s["pscore_moved"], 2 if c == 3 else 1)
            def top_exp(head, odd):
                act.wait_ge(s["top_shift"], head + 1)
                nc.scalar.activation(top_w[odd], top_w[odd], ACT.Exp).then_inc(s["top_exp"], 1)

            def head_gelus(head, odd):
                act.wait_ge(s["u_free"], head * TOPK + NBUF + TOPK)
                mine = slice(odd * TOPK, (odd + 1) * TOPK)
                nc.scalar.activation(acts[:, mine], dots[:, mine], ACT.Gelu_apprx_tanh).then_inc(s["gelu_made"], 1)

            def head_diags(head, odd):
                act.wait_ge(s["w_made"], head + 1)
                for k in range(TOPK):
                    act.wait_ge(s["v_free"], head * TOPK + k + 1 + NBUF - DIAGS)
                    n = k % DIAGS
                    a = odd * TOPK + k
                    nc.scalar.activation(diag[:, n * P:(n + 1) * P], ident[:, :], ACT.Copy, scale=wk[:, a:a + 1])\
                        .then_inc(s["diag_made"], 1)

            def tile_sums(t):
                act.wait_ge(s["v_free"], NBUF + (t + 1) * NSLOT)
                nc.scalar.activation(x3[:, t, :].rearrange("p (c n) -> p c n", c=2), pp[:, t, :, :], ACT.Copy)\
                    .then_inc(s["h2_made"], 1)

            def gate_moves(t):
                for c in range(2):
                    act.wait_ge(s["gate_full"], t * 2 + c + 1)
                    nc.scalar.activation(lt[:, t * D + c * HALF:t * D + (c + 1) * HALF], pp[:, t, c, :], ACT.Sigmoid)\
                        .then_inc(s["gate_moved"], 1)

            top_exp(0, 0)
            with act.Fori(0, PEER_HEADS // 2) as pair:
                for odd in range(2):
                    top_exp(pair * 2 + odd + 1, 1 - odd)
                    head_gelus(pair * 2 + odd, odd)
                    head_diags(pair * 2 + odd, odd)
            tile_sums(0)
            top_exp(PEER_HEADS + 1, 1)
            head_gelus(PEER_HEADS, 0)
            norm_std(6)
            head_diags(PEER_HEADS, 0)
            top_exp(PEER_HEADS + 2, 0)
            head_gelus(PEER_HEADS + 1, 1)
            head_diags(PEER_HEADS + 1, 1)
            with act.Fori(PEER_HEADS // 2 + 1, PEER_HEADS - 1) as pair:
                for odd in range(2):
                    top_exp(pair * 2 + odd + 1, 1 - odd)
                    head_gelus(pair * 2 + odd, odd)
                    head_diags(pair * 2 + odd, odd)
            top_exp(LAST_HEAD, 1)
            head_gelus(LAST_HEAD - 1, 0)
            head_diags(LAST_HEAD - 1, 0)
            head_gelus(LAST_HEAD, 1)
            gate_moves(0)
            head_diags(LAST_HEAD, 1)
            tile_sums(1)
            norm_std(7)
            gate_moves(1)

        @block.vector
        def _(dve):
            counts = {}

            def step(ins, name="dve_step"):
                counts[name] = counts.get(name, 0) + 1
                ins.then_inc(s[name], 1)
                dve.wait_ge(s[name], counts[name])

            V = nc.vector
            eps_col = small[:, 250:251]

            def norm(m, src, junk):
                step(V.tensor_tensor_reduce(out=junk, in0=src, in1=src, scale=1.0, scalar=0.0, op0=ALU.mult,
                                            op1=ALU.add, accum_out=stat[:, m:m + 1]), "squares_summed")
                dve.wait_ge(s["std_made"], m + 1)
                step(V.reciprocal(stat[:, 24 + m:25 + m], stat[:, 16 + m:17 + m]))
                step(V.tensor_scalar(junk, src, stat[:, 24 + m:25 + m], None, ALU.mult), "scaled")

            def norm_out(m, gain, t):
                dve.wait_ge(s["turned"], m + 1)
                step(V.tensor_tensor(h3[:, :, t * P:(t + 1) * P],
                                     pa[:, t * D:(t + 1) * D].rearrange("p (k n) -> p k n", k=KC),
                                     gain.unsqueeze(2).broadcast_to([P, KC, P]), ALU.mult), "normed")

            step(V.memset(eps_col, EPS))
            dve.wait_ge(s["x_loaded"], 16)
            for t in range(NT):
                norm(t, x3[:, t, :], vv[:, t * D:(t + 1) * D])
            step(V.memset(xl3[:, :, 0:PAD], 0.0))
            dve.wait_ge(s["cols_loaded"], 16)
            for t in range(NT):
                norm_out(t, col("pre_g", 0, KC), t)

            dve.wait_ge(s["lambdas_loaded"], 16)
            for j in range(2):
                V.tensor_tensor_reduce(out=lamt[:, 2 * j * QK:(2 * j + 1) * QK],
                                       in0=lamt[:, 2 * j * QK:(2 * j + 1) * QK],
                                       in1=lamt[:, (2 * j + 1) * QK:(2 * j + 2) * QK], scale=1.0, scalar=0.0,
                                       op0=ALU.mult, op1=ALU.add, accum_out=small[:, j:j + 1])
            step(V.tensor_scalar(small[:, 24:32], col("lam", 0, KC), -1.0, None, ALU.mult))
            step(V.tensor_tensor(small[:, 8:16], small[:, 24:32], col("lam", 0, KC), ALU.max), "lambda_sums")
            V.tensor_scalar(small[:, 80:81], col("sub_g"), 1.0 - LAM_INIT, None, ALU.mult)

            for c in range(2):
                dve.wait_ge(s["proj_moved"], OUT_AT[f"xl{c}"] + 1)
                for j in range(TAPS):
                    for k in range(4 * c, 4 * c + 4):
                        src = xl3[:, k, PAD - TAPS + 1 + j:PAD - TAPS + 1 + j + SEQ]
                        if j == 0:
                            ins = V.tensor_scalar(xc3[:, k, :], src, col("conv_w", k), col("conv_b", k),
                                                  ALU.mult, ALU.add)
                        else:
                            ins = V.scalar_tensor_tensor(out=xc3[:, k, :], in0=src, scalar=col("conv_w", j * KC + k),
                                                         in1=xc3[:, k, :], op0=ALU.mult, op1=ALU.add)
                    if c == 1 and j == TAPS - 1:
                        step(ins, "conv_done")
                    else:
                        step(ins)

            dve.wait_ge(s["lambda_exps"], 1)
            step(V.tensor_tensor(small[:, 4:5], small[:, 3:4], small[:, 2:3], ALU.subtract))
            step(V.tensor_scalar(small[:, 5:6], small[:, 4:5], -LAM_INIT, None, ALU.add))
            e, z, z2, acc = small[:, 16:24], small[:, 100:108], small[:, 108:116], small[:, 116:124]
            step(V.tensor_scalar(z, e, 2.0, None, ALU.add))
            step(V.reciprocal(z, z))
            step(V.tensor_tensor(z, z, e, ALU.mult))
            step(V.tensor_tensor(z2, z, z, ALU.mult))
            terms = 9
            step(V.tensor_scalar(acc, z2, 2.0 / (2 * terms + 1), 2.0 / (2 * terms - 1), ALU.mult, ALU.add))
            for n in range(terms - 2, -1, -1):
                step(V.tensor_tensor(acc, acc, z2, ALU.mult))
                step(V.tensor_scalar(acc, acc, 2.0 / (2 * n + 1), None, ALU.add))
            step(V.tensor_tensor(acc, acc, z, ALU.mult))
            step(V.scalar_tensor_tensor(out=acc, in0=small[:, 24:32], scalar=0.0, in1=acc, op0=ALU.max, op1=ALU.add))
            step(V.tensor_scalar(small[:, 32:40], acc, LRU_C, None, ALU.mult))
            dve.wait_ge(s["rgate_moved"], 1)
            step(V.tensor_tensor(rg3, rg3, small[:, 32:40].unsqueeze(2).broadcast_to([P, KC, SEQ]), ALU.mult),
                 "decay_log")
            dve.wait_ge(s["tanh_made"], 1)
            dve.wait_ge(s["act_step"], 1)
            step(V.tensor_scalar(rg[:, :], lt[:, :], 1.0, None, ALU.add))
            step(V.reciprocal(rg[:, :], rg[:, :]))
            step(V.scalar_tensor_tensor(out=lt[:, :], in0=lt[:, :], scalar=0.0, in1=rg[:, :], op0=ALU.max,
                                        op1=ALU.mult), "mult_sq")
            dve.wait_ge(s["igate_moved"], 1)
            step(V.tensor_tensor(ig[:, :], ig[:, :], xc[:, :], ALU.mult))

            def attention_scores(a):
                g, t = STEPS[a]
                n = P * (t + 1)
                if a == 0:
                    dve.wait_ge(s["consts_made"], 1)
                dve.wait_ge(s["scores_full"], a + 1)
                if a:
                    dve.wait_ge(s["weights_turned"], a)
                for c in range(2):
                    ins = V.tensor_tensor(score_sbuf(t)[:, c], score_bank(t)[:, c],
                                          mask1[:, SEQ - n:SEQ].unsqueeze(1).broadcast_to([P, GRP, n]), ALU.add)
                step(ins)
                step(V.tensor_reduce(small[:, 56 + 16:56 + 24], score_sbuf(t), AX, ALU.max))
                step(V.tensor_scalar(small[:, 40:48], small[:, 72:80], -SCALE1, None, ALU.mult), "bias_made")

            def attention_weights(a):
                g, t = STEPS[a]
                n = P * (t + 1)
                dve.wait_ge(s["probs_made"], a + 1)
                step(V.reciprocal(small[:, 84:92], small[:, 48:56]))
                step(V.tensor_scalar(small[:, 88:92], small[:, 88:92], small[:, 5:6], None, ALU.mult))
                for c in range(2):
                    sc = score_sbuf(t)[:, c]
                    ins = V.tensor_tensor(sc, sc, small[:, 84 + 4 * c:88 + 4 * c].unsqueeze(2)
                                          .broadcast_to([P, GRP, n]), ALU.mult)
                step(ins)
                step(V.tensor_tensor(score_sbuf(t)[:, 0], score_sbuf(t)[:, 0], score_sbuf(t)[:, 1], ALU.add),
                     "weights_made")

            def attention_out(a):
                g, t = STEPS[a]
                dve.wait_ge(s["heads_moved"], a + 1)
                step(V.tensor_tensor(osq[:, :], oh[:, :], oh[:, :], ALU.mult))
                step(V.tensor_reduce(small[:, 60:64], osq[:, :].rearrange("p (h n) -> p h n", h=GRP), AX, ALU.add),
                     "head_sums")
                dve.wait_ge(s["head_std"], a + 1)
                step(V.reciprocal(small[:, 92:96], small[:, 64:68]))
                o3 = oh[:, :].rearrange("p (h n) -> p h n", h=GRP)
                step(V.tensor_tensor(o3, o3, small[:, 92:96].unsqueeze(2).broadcast_to([P, GRP, P]), ALU.mult))
                dve.wait_ge(s["proj_moved"], OUT_AT[f"ga{g}"] + 1)
                gate = ga3[:, t, g * HALF:(g + 1) * HALF]
                step(V.tensor_tensor(gate, gate, oh[:, :], ALU.mult), "head_gated")

            for a in range(len(STEPS)):
                attention_scores(a)
                if a == 0:
                    dve.wait_ge(s["mult_made"], 1)
                    step(V.tensor_tensor(ig[:, :], ig[:, :], lt[:, :], ALU.mult))
                    for k in range(KC):
                        ins = V.tensor_tensor_scan(xc3[:, k, :], xl[:, k * SEQ:(k + 1) * SEQ], ig3[:, k, :], 0.0,
                                                   ALU.mult, ALU.add)
                    step(ins)
                attention_weights(a)
                attention_out(a)
            dve.wait_ge(s["proj_moved"], OUT_AT["gl1"] + 1)
            step(V.tensor_tensor(gl[:, :], gl[:, :], xc[:, :], ALU.mult), "lru_done")

            dve.wait_ge(s["rows_loaded"], 16)
            for t in range(NT):
                dve.wait_ge(s["post_std"], t + 1)
                step(V.reciprocal(stat[:, 40 + t:41 + t], stat[:, 38 + t:39 + t]))
                y = vv[:, t * D:(t + 1) * D]
                for c in range(2):
                    mine = slice(c * HALF, (c + 1) * HALF)
                    ins = V.scalar_tensor_tensor(out=y[:, mine], in0=pp[:, c, t, :], scalar=stat[:, 40 + t:41 + t],
                                                 in1=post_g[:, mine], op0=ALU.mult, op1=ALU.mult)
                if t == NT - 1:
                    ins.then_inc(s["proj_moved"], 2)
                    dve.wait_ge(s["proj_moved"], OUT_AT["wo1"] + 1)
                else:
                    step(ins)
                step(V.tensor_tensor(x3[:, t, :], x3[:, t, :], y, ALU.add), "block1_done")
                norm(2 + t, x3[:, t, :], y)
                norm_out(2 + t, col("mix_g", 0, KC), t)

            def heads_rms(dst, src, sq, sums, stds, recips, made, std_made, n_made, out_name, heads, width):
                step(V.tensor_tensor(sq, src, src, ALU.mult))
                step(V.tensor_reduce(sums, sq.rearrange("p (h n) -> p h n", h=heads), AX, ALU.add), made)
                dve.wait_ge(s[std_made], n_made)
                step(V.reciprocal(recips, stds))
                d3 = dst.rearrange("p (h n) -> p h n", h=heads)
                ins = V.tensor_tensor(d3, src.rearrange("p (h n) -> p h n", h=heads),
                                      recips.unsqueeze(2).broadcast_to([recips.shape[0], heads, width]), ALU.mult)
                step(ins, out_name) if out_name else step(ins)

            l0, l1, mx = col("lb0", 0, 4), col("lb1", 0, 4), lbt[:, 0:4]
            step(V.tensor_tensor(mx, l0, l1, ALU.max))
            V.tensor_tensor(lbt[:, 4:8], l0, mx, ALU.subtract)
            step(V.tensor_tensor(lbt[:, 8:12], l1, mx, ALU.subtract), "lb_shifted")
            dve.wait_ge(s["lb_exp"], 1)
            step(V.tensor_tensor(lbt[:, 12:16], lbt[:, 4:8], lbt[:, 8:12], ALU.add))
            step(V.reciprocal(lbt[:, 12:16], lbt[:, 12:16]))
            step(V.tensor_tensor(lbt[:, 16:20], lbt[:, 4:8], lbt[:, 12:16], ALU.mult))
            step(V.tensor_scalar(lbt[:, 20:24], lbt[:, 16:20], -1.0, 1.0, ALU.mult, ALU.add))
            V.memset(gain8[:, 6:8], 1.0)
            V.tensor_copy(gain8[:, 4:6], col("nk_g", 1, 2))
            step(V.tensor_scalar(gain8[:, 0:4], col("nq_g").broadcast_to([P, 4]), DH ** -0.5, None, ALU.mult))

            dve.wait_ge(s["proj_moved"], OUT_AT["nk"] + 1)
            for t in range(NT):
                src = nq3[:, t, 0:NORMED]
                heads_rms(src, src, sm[:, 0:NORMED], st2[:, 40 + 12 * t:52 + 12 * t],
                          st2[:, 16 + 12 * t:28 + 12 * t], small[:, 150 + 12 * t:162 + 12 * t],
                          "nsa_sums", "nsa_std", t + 1, "nsa_scaled", NORMED // DH, DH)
            dve.wait_ge(s["proj_moved"], OUT_AT["hf"] + 1)
            for h in range(HG_HEADS):
                f = at2.key[:, h * SEQ:(h + 1) * SEQ]
                ins = V.tensor_scalar(f, f, lbt[:, 20 + h:21 + h], lbt[:, 16 + h:17 + h], ALU.mult, ALU.add)
            step(ins, "forget_made")
            for t in range(NT):
                dve.wait_ge(s["nsa_turned"], t + 1)
                step(V.tensor_tensor(nT3[:, :, t * P:(t + 1) * P],
                                     pa[:, t * D:(t + 1) * D].rearrange("p (k n) -> p k n", k=KC),
                                     gain8.unsqueeze(2).broadcast_to([P, KC, P]), ALU.mult), "nsa_normed")
            for kv in range(2):
                for n, dst in enumerate((at2.pe0, at2.pe1)):
                    ins = V.tensor_tensor(
                        dst[:, kv * SEQ:(kv + 1) * SEQ].rearrange("p (b j) -> p b j", j=CMP_STRIDE),
                        nT3[:, 6 + kv, :].rearrange("p (b j) -> p b j", j=CMP_STRIDE),
                        col("pe", kv * CMP_LEN + n * CMP_STRIDE, CMP_STRIDE).unsqueeze(1)
                        .broadcast_to([P, SEQ // CMP_STRIDE, CMP_STRIDE]), ALU.add)
            step(ins, "cmp_in")
            dve.wait_ge(s["log_made"], 1)
            step(V.tensor_scalar(at2.key, at2.key, -1.0, 1.0, ALU.mult, ALU.add))
            dve.wait_ge(s["scan_mask_made"], 1)
            step(V.tensor_tensor_scan(at2.cum, at2.scan_mask, at2.log_f, 0.0, ALU.mult, ALU.add))
            cum3 = at2.cum.rearrange("p (m n) -> p m n", n=CH)
            shift3 = at2.shift.rearrange("p (m n) -> p m n", n=CH)
            shape = [P, HG_HEADS * NCH, CH]
            step(V.tensor_tensor(shift3, cum3, cum3[:, :, CH // 2 - 1:CH // 2].broadcast_to(shape), ALU.subtract),
                 "shift_made")
            dve.wait_ge(s["shift_exp"], 1)
            step(V.tensor_tensor(shift3, cum3[:, :, CH - 1:CH].broadcast_to(shape), cum3, ALU.subtract), "last_made")
            dve.wait_ge(s["proj_moved"], OUT_AT["hq"] + 1)
            V.scalar_tensor_tensor(out=at2.q1, in0=at2.query, scalar=P ** -0.5, in1=at2.q1, op0=ALU.mult, op1=ALU.mult)
            V.tensor_tensor(at2.k2, at2.key, at2.k2, ALU.mult)
            V.scalar_tensor_tensor(out=at2.q3, in0=at2.query, scalar=P ** -0.5, in1=at2.q3, op0=ALU.mult, op1=ALU.mult)
            dve.wait_ge(s["last_exp"], 1)
            step(V.tensor_tensor(at2.k4, at2.key, at2.k4, ALU.mult), "recur_ready")

            dve.wait_ge(s["cmp_full"], 1)
            step(V.tensor_copy(cmp_tok[0:NCMP, :].rearrange("p (v g n) -> p v g n", v=2, g=NKV),
                               cmp_psum[0:NCMP, :].rearrange("p (g v n) -> p v g n", v=2, g=NKV)))
            kc = cmp_tok[0:NCMP, 0:NKV * DH]
            heads_rms(kc, kc, at2.tmp[0:NCMP, 0:NKV * DH], st2[0:NCMP, 64:66], st2[0:NCMP, 66:68],
                      st2[0:NCMP, 68:70], "cmp_sums", "cmp_std", 1, "cmp_ready", NKV, DH)

            dve.wait_ge(s["update_full"], 1)
            u = [pa[:, b * HALF:(b + 1) * HALF] for b in UPDATE_BANKS]
            step(V.tensor_copy(at2.states[:, 0:HALF], u[0]))
            for c in range(1, NCH - 1):
                for h in range(HG_HEADS):
                    a = h * P
                    ins = V.scalar_tensor_tensor(out=at2.states[:, c * HALF + a:c * HALF + a + P],
                                                 in0=at2.states[:, (c - 1) * HALF + a:(c - 1) * HALF + a + P],
                                                 scalar=last_exp[:, h * NCH + c:h * NCH + c + 1],
                                                 in1=u[c][:, a:a + P], op0=ALU.mult, op1=ALU.add)
                if c < NCH - 2:
                    step(ins)
            step(ins, "states_made")

            dve.wait_ge(s["cs_full"], 1)
            ec = e_c.rearrange("p (m n) -> p m n", n=16)[:, :, 0:NCMP]
            bc = bias_c.rearrange("p (m n) -> p m n", n=16)[:, :, 0:NCMP]
            mc = mask_c.rearrange("p (m n) -> p m n", n=16)[:, :, 0:NCMP]
            M = NT * NSA_HEADS
            step(V.tensor_tensor(ec, cs_psum.rearrange("p (m n) -> p m n", n=16)[:, :, 0:NCMP], bc, ALU.add))
            cmax, csum = small[:, 180:196], small[:, 196:212]
            step(V.tensor_reduce(cmax, ec, AX, ALU.max))
            step(V.tensor_tensor(ec, ec, cmax.unsqueeze(2).broadcast_to([P, M, NCMP]), ALU.subtract), "cs_shifted")
            dve.wait_ge(s["cs_exp"], 1)
            step(V.tensor_tensor(ec, ec, mc, ALU.mult))
            step(V.tensor_reduce(csum, ec, AX, ALU.add), "cs_ready")

            gates3 = [nq3[:, t, NQW - GATES:NQW].rearrange("p (h b) -> p h b", b=3) for t in range(NT)]
            b3 = at2.bias[:, :].rearrange("p (h n) -> p h n", h=NSA_HEADS)

            def att_biased(b):
                t, w = STEPS2[b]
                n = P * (t + 1)
                sc = score2(at2.sc[b % 2], t)
                dve.wait_ge(s["att_full"], b + 1)
                step(V.tensor_tensor(sc, score2(att_psum[b], t), b3[:, :, SEQ - n:SEQ], ALU.add))
                step(V.tensor_reduce(st2[:, 72:80], sc, AX, ALU.max))
                step(V.tensor_scalar(att_shift[b % 2], st2[:, 72:80], -1.0, None, ALU.mult), "att_bias")

            def att_out(b):
                t, w = STEPS2[b]
                over = small[:, 228:236]
                dve.wait_ge(s["att_exp"], b + 1)
                step(V.tensor_scalar(over, att_sums[b % 2], 1e-30, None, ALU.max))
                step(V.reciprocal(over, over))
                step(V.tensor_tensor(over, over, gates3[t][:, :, 1 + w], ALU.mult))
                dve.wait_ge(s["ao_full"], b + 1)
                tmp3 = at2.tmp[:, 0:HALF].rearrange("p (h n) -> p h n", n=DH)
                step(V.tensor_tensor(tmp3, att_psum[b][:, 0:HALF].rearrange("p (h n) -> p h n", n=DH),
                                     over.unsqueeze(2).broadcast_to([P, NSA_HEADS, DH]), ALU.mult), "ao_used")
                no = at2.no[:, t * HALF:(t + 1) * HALF]
                step(V.tensor_tensor(no, no, at2.tmp[:, 0:HALF], ALU.add))

            def sparse_sums(t):
                no = at2.no[:, t * HALF:(t + 1) * HALF]
                step(V.tensor_tensor(at2.osq[:, 0:HALF], no, no, ALU.mult))
                step(V.tensor_reduce(st2[:, 96 + 8 * t:104 + 8 * t],
                                     at2.osq[:, 0:HALF].rearrange("p (h n) -> p h n", n=DH), AX, ALU.add), "nsa_osums")

            def sparse_scaled(t):
                dve.wait_ge(s["nsa_ostd"], NT - t)
                recips = small[:, 124 + 8 * t:132 + 8 * t]
                step(V.reciprocal(recips, st2[:, 112 + 8 * t:120 + 8 * t]))
                no = at2.no[:, t * HALF:(t + 1) * HALF].rearrange("p (h n) -> p h n", n=DH)
                step(V.tensor_tensor(no, no, recips.unsqueeze(2).broadcast_to([P, NSA_HEADS, DH]), ALU.mult), "nsa_out")

            def mixed_gained(n, dst, src, chunks, width):
                dve.wait_ge(s["mix_turned"], n)
                step(V.tensor_tensor(dst, src.rearrange("p (k n) -> p k n", k=4),
                                     col("out2_g", chunks, 4).unsqueeze(2).broadcast_to([P, 4, width]), ALU.mult),
                     "mixT_made")

            dve.wait_ge(s["bias2_made"], 1)
            att_biased(0)
            step(V.tensor_scalar(csum, csum, 1e-30, None, ALU.max))
            step(V.reciprocal(csum, csum))
            coef = small[:, 212:228]
            for t in range(NT):
                ins = V.tensor_tensor(coef[:, t * 8:(t + 1) * 8].rearrange("p (g r) -> p g r", g=NKV),
                                      csum.rearrange("p (g t r) -> p g t r", g=NKV, t=NT)[:, :, t, :],
                                      gates3[t][:, :, 0].rearrange("p (g r) -> p g r", g=NKV), ALU.mult)
            step(ins)
            dve.wait_ge(s["co_full"], 1)
            step(V.tensor_tensor(at2.no.rearrange("p (m n) -> p m n", n=DH),
                                 pa[:, D:2 * D].rearrange("p (m n) -> p m n", n=DH),
                                 coef.unsqueeze(2).broadcast_to([P, M, DH]), ALU.mult), "co_used")
            dve.wait_ge(s["o_moved"], 1)
            step(V.tensor_tensor(at2.osq, at2.o, at2.o, ALU.mult))
            step(V.tensor_reduce(st2[:, 8:16], at2.osq.rearrange("p (h n) -> p h n", n=P), AX, ALU.add), "o_sums")
            att_biased(1)
            att_out(0)
            dve.wait_ge(s["o_std"], 1)
            step(V.reciprocal(small[:, 140:148], st2[:, 0:8]))
            o3 = at2.o.rearrange("p (h n) -> p h n", n=P)
            step(V.tensor_tensor(o3, o3, small[:, 140:148].unsqueeze(2).broadcast_to([P, NT * HG_HEADS, P]), ALU.mult))
            step(V.tensor_tensor(at2.o, at2.o, at2.gate, ALU.mult), "o_gated")
            mixed_gained(1, h3[:, 0:4, :], pp_flat[:, 0:D], 0, SEQ)
            att_out(1)
            sparse_sums(1)
            att_biased(2)
            att_biased(3)
            sparse_scaled(1)
            att_out(2)
            mixed_gained(2, h3[:, 4:KC, P:2 * P], pa[:, 3 * HALF:4 * HALF], 4, P)
            att_out(3)
            sparse_sums(0)
            sparse_scaled(0)
            mixed_gained(3, h3[:, 4:KC, 0:P], pa[:, HALF:2 * HALF], 4, P)

            def joined(t):
                for c in range(2):
                    rows_x = x3[:, t, c * HALF:(c + 1) * HALF]
                    ins = V.tensor_tensor(rows_x, rows_x, pp[:, c, t, :], ALU.add)
                return ins

            dve.wait_ge(s["wp_full"], 1)
            step(joined(1))
            norm(4, x3[:, 1, :], vv[:, D:2 * D])
            dve.wait_ge(s["unit_used"], UNIT_AT["wp1"] + 1)
            joined(0).then_inc(s["proj_moved"], 2)
            dve.wait_ge(s["proj_moved"], OUT_AT["wp1"] + 1)
            norm(5, x3[:, 0, :], vv[:, 0:D])
            norm_out(4, col("ffn_g", 0, KC), 1)
            norm_out(5, col("ffn_g", 0, KC), 0)
            dve.wait_ge(s["rows_loaded"], 32)
            for t in range(NT):
                xt = vv[:, t * D:(t + 1) * D]
                step(V.tensor_tensor(xt, xt, post_g[:, :], ALU.mult))
            two = [P, 2, TOPK, TOPK]

            def choose(head, odd):
                count = [0]

                def then(ins):
                    count[0] += 1
                    ins.then_inc(s["choice_step"], 1)
                    dve.wait_ge(s["choice_step"], count[0])

                def top16(rows_in, values, at, n):
                    for half in range(2):
                        where = slice(half * 8, half * 8 + 8)
                        for j in range(n):
                            ins = V.max(values[:, j, where], rows_in[:, j, :])
                        then(ins)
                        for j in range(n):
                            ins = V.max_index(at[:, j, where], values[:, j, where], rows_in[:, j, :])
                        then(ins)
                        if half == 0:
                            for j in range(n):
                                ins = V.match_replace(rows_in[:, j, :], values[:, j, where], rows_in[:, j, :], LOWEST)
                            then(ins)

                then(V.tensor_copy(halves, xc_rg[:, bass.ds(head * (2 * NKEYS), 2 * NKEYS)]))
                v3 = v16.rearrange("p (c k) -> p c k", c=2)
                top16(halves.rearrange("p (c n) -> p c n", c=2), v3, i16.rearrange("p (c k) -> p c k", c=2), 2)
                V.tensor_copy(i16f, i16)
                then(V.tensor_tensor(pairs.rearrange("p (a b) -> p a b", a=TOPK),
                                     v3[:, 0, :].unsqueeze(2).broadcast_to([P, TOPK, TOPK]),
                                     v3[:, 1, :].unsqueeze(1).broadcast_to([P, TOPK, TOPK]), ALU.add))
                top16(pairs.unsqueeze(1), best.unsqueeze(1), best_at.unsqueeze(1), 1)
                V.tensor_scalar(top_w[odd], best, best[:, 0:1], None, ALU.subtract).then_inc(s["top_shift"], 1)
                V.tensor_scalar(places_i[:, 0:TOPK], best_at, 4, None, ALU.logical_shift_right)
                then(V.tensor_scalar(places_i[:, TOPK:2 * TOPK], best_at, TOPK - 1, None, ALU.bitwise_and))
                then(V.tensor_copy(places, places_i))
                for half in range(2):
                    mine = slice(half * TOPK, (half + 1) * TOPK)
                    square = [P, TOPK, TOPK]
                    h3d = hot.rearrange("p (k j) -> p k j", k=TOPK)
                    then(V.tensor_tensor(h3d, places[:, mine].unsqueeze(2).broadcast_to(square),
                                         iota16.unsqueeze(1).broadcast_to(square), ALU.is_equal))
                    then(V.tensor_tensor(h3d, h3d, i16f[:, mine].unsqueeze(1).broadcast_to(square), ALU.mult))
                    then(V.tensor_reduce(keys_f[:, mine], h3d, AX, ALU.add))
                V.scalar_tensor_tensor(out=keys_f[:, 0:TOPK], in0=keys_f[:, 0:TOPK], scalar=float(NKEYS),
                                       in1=keys_f[:, TOPK:2 * TOPK], op0=ALU.mult, op1=ALU.add)\
                    .then_inc(s["choice_step"], 1)
                dve.wait_ge(s["choice_step"], count[0] + 1)
                dve.sem_clear(s["choice_step"])
                V.tensor_copy(all_experts[:, bass.ds(head * TOPK, TOPK)], keys_f[:, 0:TOPK]).then_inc(s["chosen"], 1)

            def head_dots(head, odd, t):
                for k in range(TOPK):
                    rows_u = u_rows[k % NBUF]
                    a = odd * TOPK + k
                    dve.wait_ge(u_here[k % NBUF], (head * 2 + k // NBUF + 1) * 16)
                    V.tensor_tensor_reduce(out=rows_u, in0=rows_u, in1=vv[:, t * D:(t + 1) * D], scale=1.0,
                                           scalar=0.0, op0=ALU.mult, op1=ALU.add,
                                           accum_out=dots[:, a:a + 1]).then_inc(s["u_free"], 1)
                mine = slice(odd * TOPK, (odd + 1) * TOPK)
                dve.wait_ge(s["top_exp"], head + 1)
                V.tensor_reduce(top_sum, top_w[odd], AX, ALU.add).then_inc(s["top_summed"], 1)
                dve.wait_ge(s["top_summed"], head * 2 + 1)
                V.reciprocal(top_sum, top_sum).then_inc(s["top_summed"], 1)
                dve.wait_ge(s["gelu_made"], head + 1)
                dve.wait_ge(s["top_summed"], head * 2 + 2)
                V.scalar_tensor_tensor(out=wk[:, mine], in0=acts[:, mine], scalar=top_sum, in1=top_w[odd],
                                       op0=ALU.mult, op1=ALU.mult).then_inc(s["w_made"], 1)

            V.memset(small[:, 237:238], 0.0).then_inc(s["u_free"], NBUF)
            V.memset(small[:, 238:239], 0.0).then_inc(s["v_free"], NBUF)
            dve.wait_ge(s["pscore_moved"], 1)
            choose(0, 0)
            with dve.Fori(0, PEER_HEADS // 2) as pair:
                for odd in range(2):
                    dve.wait_ge(s["pscore_moved"], pair + odd + 1)
                    dve.sem_inc(s["dve_pace"], 1)
                    choose(pair * 2 + odd + 1, 1 - odd)
                    head_dots(pair * 2 + odd, odd, 0)
            def gate_input(t):
                dve.wait_ge(s["h2_made"], t + 1)
                norm(6 + t, x3[:, t, :], vv[:, t * D:(t + 1) * D])

            def gated(t):
                for c in range(2):
                    dve.wait_ge(s["gate_moved"], t * 2 + c + 1)
                    mine = slice(t * D + c * HALF, t * D + (c + 1) * HALF)
                    step(V.tensor_tensor(lt[:, mine], lt[:, mine], nq[:, mine], ALU.mult))
                    step(V.tensor_tensor(xs[:, mine], xs[:, mine], lt[:, mine], ALU.add), "y_made")

            choose(PEER_HEADS + 1, 1)
            head_dots(PEER_HEADS, 0, 1)
            gate_input(0)
            choose(PEER_HEADS + 2, 0)
            head_dots(PEER_HEADS + 1, 1, 1)
            norm_out(6, col("gate_g", 0, KC), 0)
            with dve.Fori(PEER_HEADS // 2 + 1, PEER_HEADS - 1) as pair:
                for odd in range(2):
                    choose(pair * 2 + odd + 1, 1 - odd)
                    head_dots(pair * 2 + odd, odd, 1)
            choose(LAST_HEAD, 1)
            head_dots(LAST_HEAD - 1, 0, 1)
            head_dots(LAST_HEAD, 1, 1)
            gated(0)
            gate_input(1)
            norm_out(7, col("gate_g", 0, KC), 1)
            gated(1)


def feature_columns(v):
    return np.asarray(v).reshape(-1, P).T


def unit_of(w, k0, c0, c1):
    w = np.asarray(w)[k0:k0 + D, c0:c1]
    out = np.zeros((P, KC, HALF), np.float32)
    out[:, :, 0:w.shape[1]] = w.reshape(KC, P, -1).transpose(1, 0, 2)
    return out.reshape(P, UNIT)


def padded(parts):
    out = np.zeros((P, UNIT), np.float32)
    at = 0
    for a in parts:
        out[:, at:at + a.shape[1]] = a
        at += a.shape[1]
    return out


def lay_out(i):
    w_in, w_out = np.asarray(i["w_in"])[0], np.asarray(i["w_out"])[0]
    at = {"q": 0, "k": D, "v": 2 * D, "ga": 3 * D, "xl": 4 * D, "gl": 5 * D}
    w2, wp = np.asarray(i["w_in_2"])[0], np.asarray(i["w_out_2"])[0]
    wq, gw = np.asarray(i["peer_wq_2"])[0], np.asarray(i["ple_gate_w_2"])[0]
    nsa, kv = 4 * HALF, 5 * HALF
    order = [np.arange(nsa, kv).reshape(NKV, REP, DH).transpose(1, 0, 2).ravel()]
    order += [np.arange(kv + n * P, kv + (n + 1) * P) for n in (2, 4, 0, 1, 3, 5)]
    order.append(np.arange(kv + 6 * P, kv + 6 * P + GATES))
    wn = w2[:, np.concatenate(order)]
    both = lambda a: np.concatenate([a, a], axis=0)
    units = []
    for name in UNITS:
        if name == "lru":
            units.append(padded([np.asarray(i[n])[0].transpose(1, 0, 2).reshape(P, D) for n in ("w_rgate", "w_igate")]))
        elif name[:3] == "wol":
            units.append(unit_of(w_out, D, int(name[3]) * HALF, (int(name[3]) + 1) * HALF))
        elif name[:3] == "woa":
            units.append(unit_of(w_out, 0, int(name[3]) * HALF, (int(name[3]) + 1) * HALF))
        elif name in ("hf", "hq", "hi", "hg"):
            a = {"hq": 0, "hf": 1, "hi": 2, "hg": 3}[name] * HALF
            units.append(unit_of(w2, 0, a, a + HALF))
        elif name in ("nq", "nk", "nv"):
            a = {"nq": 0, "nk": 1, "nv": 2}[name] * HALF
            units.append(unit_of(wn, 0, a, min(a + HALF, NQW)))
        elif name == "cmp":
            w = np.asarray(i["cmp_w1_2"])[0].reshape(2, CMP_LEN, DH, DH).transpose(2, 0, 1, 3).reshape(DH, UNIT)
            units.append(both(w))
        elif name == "ple":
            w = np.asarray(i["ple_proj_2"])[0].reshape(PLE // P, P, D)
            p = np.asarray(i["p_2"])[0, 0].T.reshape(PLE // P, P, SEQ)
            units.append(padded([*w, *p]))
        elif name[:2] in ("wp", "wq", "gw"):
            c = int(name[2]) * HALF
            units.append(unit_of({"wp": wp, "wq": wq, "gw": gw}[name[:2]], 0, c, c + HALF))
        else:
            a = at[name[:-1]] + int(name[-1]) * HALF
            units.append(unit_of(w_in, 0, a, a + HALF))
    named = {
        "pre_g": feature_columns(i["pre_norm_g"]), "conv_w": feature_columns(i["conv_w"]),
        "conv_b": feature_columns(i["conv_b"]), "b_r": feature_columns(i["b_rgate"]),
        "b_i": feature_columns(i["b_igate"]), "lam": feature_columns(i["lru_lambda"]),
        "sub_g": feature_columns(i["subln_g"]),
        "mix_g": feature_columns(i["mix_norm_2"]), "ffn_g": feature_columns(i["ffn_norm_2"]),
        "gate_g": feature_columns(i["ple_gate_norm_2"]),
        "lb0": feature_columns(np.asarray(i["hg_lb_logits_2"])[0]),
        "lb1": feature_columns(np.asarray(i["hg_lb_logits_2"])[1]),
        "out2_g": np.concatenate([feature_columns(i["hg_out_norm_2"]), feature_columns(i["nsa_out_norm_2"])], axis=1),
        "nq_g": both(np.asarray(i["nsa_q_norm_2"]).T), "nk_g": both(np.asarray(i["nsa_k_norm_2"])[0].T),
        "pe": both(np.asarray(i["cmp_pe_2"])[0].reshape(2 * CMP_LEN, DH).T),
        "cmp_w2": both(np.asarray(i["cmp_w2_2"])[0].transpose(1, 0, 2).reshape(DH, 2 * DH)),
    }
    return {
        "x": np.asarray(i["x"])[0],
        "wall": np.stack(units),
        "cols": np.ascontiguousarray(np.concatenate([named[n] for n, _ in COLS], axis=1)),
        "rows": np.stack([np.asarray(i["post_norm_g"])[0], np.asarray(i["ffn_norm_2"])[0]]),
        "sub_keys": np.ascontiguousarray(np.asarray(i["peer_keys_2"])[0].reshape(2 * PEER_HEADS, NKEYS, P)
                                         .transpose(2, 0, 1).reshape(P, -1)),
        "peer_u": np.asarray(i["peer_u_2"])[0],
        "peer_v": np.asarray(i["peer_v_2"])[0],
        "lambdas": np.concatenate([np.asarray(i[n]) for n in ("lambda_q1", "lambda_k1", "lambda_q2", "lambda_k2")], axis=1),
    }


def kernel(**inputs):
    import concourse.bacc as bacc
    from concourse.bass_utils import run_bass_kernel_spmd

    nc = bacc.Bacc("TRN2", target_bir_lowering=False, num_devices=1)
    arrays = {f"in_{n}": np.ascontiguousarray(a) for n, a in lay_out(inputs).items()}
    aps = {n[3:]: nc.dram_tensor(n, a.shape, mybir.dt.from_np(a.dtype), kind="ExternalInput").ap()
           for n, a in arrays.items()}
    out = nc.dram_tensor("out", (SEQ, D), F32, kind="ExternalOutput").ap()
    two_blocks(nc, out=out, **aps)
    r = run_bass_kernel_spmd(nc, [arrays], core_ids=[0])
    return r.results[0]["out"].reshape(1, SEQ, D)
```

```python
import math
from contextlib import ExitStack

import numpy as np

import concourse.bass as bass
from concourse import mybir

F32 = mybir.dt.float32
U32 = mybir.dt.uint32
I32 = mybir.dt.int32
ALU = mybir.AluOpType
ACT = mybir.ActivationFunctionType
AX = mybir.AxisListType.X

P = 128
SEQ = 256
D = 1024
NT = SEQ // P
KC = D // P
HALF = 512
UNIT = KC * HALF
RING = 4
EPS = 1e-6
NEG = -1e30
LOWEST = -3e38

HEADS = 8
QK = 64
SCALE1 = QK ** -0.5
LAM_INIT = 0.8 - 0.6 * math.exp(-0.3 * 0)
LRU_C = 8.0
TAPS = 4
PAD = 4
XS = SEQ + PAD
GRP = 4

HG_HEADS = 4
CH = 64
NCH = SEQ // CH
DH = 64
NKV = 2
REP = 4
NSA_HEADS = NKV * REP
CMP_LEN = 32
CMP_STRIDE = 16
NCMP = (SEQ - CMP_LEN) // CMP_STRIDE + 1
SLOPES = [2.0 ** (-8.0 * (h + 1) / NSA_HEADS) for h in range(NSA_HEADS)]
GATES = 3 * NSA_HEADS
PEER_HEADS = 8
NKEYS = 128
TOPK = 16
NSLOT = PEER_HEADS * TOPK
PLE = 256
NQW = 2 * HALF + 2 * NKV * DH + GATES
NORMED = HALF + 2 * NKV * DH

UNITS = ["xl0", "xl1", "q0", "q1", "k0", "lru", "k1", "v0", "v1", "ga0", "ga1", "gl0", "gl1",
         "wol0", "wol1", "woa0", "woa1",
         "nq", "nk", "hf", "hq", "cmp", "hi", "hg", "nv", "wp0", "wp1",
         "ple", "wq0", "wq1", "wq2", "wq3", "gw0", "gw1"]
UNIT_AT = {name: n for n, name in enumerate(UNITS)}
OUTS = ["xl0", "xl1", "q0", "q1", "k0", "k1", "v0", "v1", "ga0", "ga1", "gl0", "gl1", "wo0", "wo1",
        "nq", "nk", "hf", "hq", "hi", "hg", "nv", "wp0", "wp1", "ple0", "ple1", "wq0", "wq1", "wq2", "wq3"]
OUT_AT = {name: n for n, name in enumerate(OUTS)}

COLS = [("pre_g", KC), ("conv_w", TAPS * KC), ("conv_b", KC), ("b_r", KC), ("b_i", KC),
        ("lam", KC), ("sub_g", 1),
        ("mix_g", KC), ("ffn_g", KC), ("gate_g", KC), ("lb0", HG_HEADS), ("lb1", HG_HEADS), ("out2_g", KC),
        ("nq_g", 1), ("nk_g", 3), ("pe", 2 * CMP_LEN), ("cmp_w2", 2 * DH)]
COL_AT, NCOL = {}, 0
for _name, _width in COLS:
    COL_AT[_name] = (NCOL, NCOL + _width)
    NCOL += _width

SEMS = ["x_loaded0", "x_loaded1", "cols_loaded", "rows_loaded", "lambdas_loaded", "consts_made", "identity_made", "unit_used",
        "proj_moved", "squares_summed", "std_made", "scaled", "turned", "normed", "dve_step", "act_step",
        "pool_step", "lambda_sums", "lambda_exps", "conv_done", "rgate_full", "rgate_moved", "igate_moved",
        "decay_log", "tanh_made", "mult_sq", "mult_made", "lru_done", "scores_full", "bias_made", "probs_made",
        "weights_made", "weights_turned", "turned_moved", "heads_full", "heads_moved", "head_sums", "head_std",
        "head_gated", "attn_turned", "attn_moved", "ple_full", "lb_shifted", "lb_exp", "post_std",
        "block1_done", "stored", "bias2_made", "scan_mask_made", "forget_made", "log_made", "shift_made",
        "shift_exp", "last_made", "last_exp", "recur_ready", "keys_turned", "keys_moved", "intra_full",
        "intra_moved", "intra_masked", "update_full", "states_made", "o_gated", "o_full", "o_moved", "o_sums",
        "o_std", "nsa_sums", "nsa_std", "nsa_scaled", "nsa_turned", "nsa_normed", "cmp_in", "hid_made",
        "cmp_full", "cmp_sums", "cmp_std", "cmp_ready", "v_blocks_made", "cmp_turned", "cmpT_made", "cs_full", "cs_shifted",
        "cs_exp", "cs_ready", "cs_turned", "csT_moved", "co_full", "co_used", "att_full", "att_bias", "att_exp",
        "att_turned", "att_moved", "ao_full", "ao_used", "nsa_osums", "nsa_ostd", "nsa_out", "mix_turned",
        "mixT_made", "wp_full", "wo_full", "keys_loaded", "first_query", "first_moved", "first_scores", "first_taken", "pscore_full", "pscore_moved", "choice_step", "top_shift", "top_exp",
        "top_summed", "chosen", "cur_made", "pace", "dve_pace", "u_free", "gelu_made", "w_made", "diag_made", "v_free",
        "h2_made", "gate_full", "gate_moved", "y_made"]


UPDATE_BANKS = (0, 1, 2)
NBUF = 8
BATCH = 2
DIAGS = 4
LAST_HEAD = NT * PEER_HEADS - 1


def two_blocks(nc, x, wall, cols, rows, lambdas, sub_keys, peer_u, peer_v, out):
    with ExitStack() as ctx:
        def sb(name, words, dt=F32):
            return ctx.enter_context(nc.sbuf_tensor(name, [P, words], dt))

        s = {n: ctx.enter_context(nc.semaphore(n)) for n in SEMS}
        unit_ready = [ctx.enter_context(nc.semaphore(f"unit_ready{i}")) for i in range(RING)]

        ring = sb("ring", RING * UNIT)
        xs = sb("xs", NT * D)
        hT = sb("hT", KC * SEQ)
        colt = sb("colt", NCOL)
        post_g = sb("post_g", D)
        ident = sb("ident", P)
        mask1 = sb("mask1", SEQ)
        stat = sb("stat", 64)
        zero = sb("zero", P)

        xl = sb("xl", KC * XS)
        xc_rg = sb("xc_rg", 2 * KC * SEQ)
        xc, rg = xc_rg[:, 0:KC * SEQ], xc_rg[:, KC * SEQ:2 * KC * SEQ]
        ig = sb("ig", KC * SEQ)
        lt = sb("lt", KC * SEQ)
        gl = sb("gl", KC * SEQ)
        qT = sb("qT", KC * SEQ)
        kT = sb("kT", KC * SEQ)
        vv = sb("vv", NT * D)
        ga = sb("ga", NT * D)
        sm = sb("sm", 2 * GRP * SEQ)
        tail = sb("tail", 2 * D)
        wT = tail[:, 0:D]
        oh = tail[:, D:D + HALF]
        osq = tail[:, D + HALF:2 * D]
        junk1 = xc[:, 0:D]
        lamt = sb("lamt", 4 * QK)
        small = sb("small", 256)

        nq = sb("nq", NT * NQW)
        small2 = sb("small2", 1536)
        diag = sb("diag", DIAGS * P)

        class at2:
            key = kT[:, 0:D]
            log_f = kT[:, D:2 * D]
            cum = qT[:, 0:D]
            shift = qT[:, D:2 * D]
            q1, k2 = xc[:, 0:D], xc[:, D:2 * D]
            q3, k4 = rg[:, 0:D], rg[:, D:2 * D]
            query = ig[:, 0:D]
            scan_mask = lt[:, 0:D]
            k_tok = lt[:, D:2 * D]
            v = ga[:, 0:D]
            gate = ga[:, D:2 * D]
            intra = gl[:, 0:HALF]
            states = gl[:, HALF:4 * HALF]
            o = xl[:, 0:D]
            osq = xl[:, D:2 * D]
            nT = vv
            pe0, pe1 = sm[:, D:D + HALF], sm[:, D + HALF:2 * D]
            sc = [b[:, n * D:(n + 1) * D] for b in (sm, qT) for n in range(2)]
            pT = [b[:, n * D:(n + 1) * D] for b in (kT, gl) for n in range(2)]
            cT = xc
            no = ig[:, 0:D]
            tmp = ig[:, D:D + HALF]
            v_blocks = ig[:, D + HALF:2 * D]
            kc = small2[0:2 * 16, 512:640]
            bias = tail

        bias_c = small2[:, 0:256]
        mask_c = small2[:, 256:512]
        e_c = small2[:, 512:768]
        dist_c = small2[:, 768:800]
        dist_ci = small2[:, 800:832].bitcast(I32)
        iota16 = small2[:, 832:848]
        iota16i = small2[:, 848:864].bitcast(I32)
        gain8 = small2[:, 864:872]
        st2 = small2[:, 872:1000]
        lbt = small2[:, 1000:1032]
        kcT = small2[:, 1032:1064]
        hid_k = small2[:, 1064:1096]
        hid_v = small2[:, 1096:1224]
        last_exp = small2[:, 1336:1352]
        head_mask = small2[:, 1512:1520]
        group_mask = small2[0:2 * 16, 1520:1522]
        dots = small2[:, 1352:1384]
        acts = small2[:, 1384:1416]
        wk = small2[:, 1416:1448]
        cur = [[small2[:, 1448 + n * TOPK:1448 + (n + 1) * TOPK].bitcast(U32) for n in (2 * k, 2 * k + 1)]
               for k in range(2)]

        def choice(at, words, dt=F32):
            a = xl[:, at:at + words]
            return a if dt == F32 else a.bitcast(dt)

        halves = choice(0, 2 * NKEYS)
        pairs = choice(256, TOPK * TOPK)
        hot = choice(512, TOPK * TOPK)
        v16, i16, i16f = choice(768, 2 * TOPK), choice(800, 2 * TOPK, U32), choice(832, 2 * TOPK)
        best, best_at = choice(864, TOPK), choice(880, TOPK, U32)
        places_i, places = choice(896, 2 * TOPK, U32), choice(928, 2 * TOPK)
        keys_f = choice(960, 2 * TOPK)
        top_w = [choice(992 + n * TOPK, TOPK) for n in range(2)]
        top_sum = choice(1024, 1)
        all_experts = choice(1040, NT * NSLOT, U32)

        pp = ctx.enter_context(nc.psum_tensor("pp", [P, 2, 2, HALF], F32))
        pa = ctx.enter_context(nc.psum_tensor("pa", [P, 4 * HALF], F32))

        def col(name, n=0, k=1):
            a = COL_AT[name][0]
            return colt[:, a + n:a + n + k]

        def slot(u):
            a = (u % RING) * UNIT
            return ring[:, a:a + UNIT].rearrange("p (k n) -> p k n", k=KC)

        x3 = xs[:, :].rearrange("p (t d) -> p t d", t=NT)
        h3 = hT[:, :].rearrange("p (k n) -> p k n", k=KC)
        xl3 = xl[:, :].rearrange("p (k n) -> p k n", k=KC)
        xc3 = xc[:, :].rearrange("p (k n) -> p k n", k=KC)
        rg3 = rg[:, :].rearrange("p (k n) -> p k n", k=KC)
        ig3 = ig[:, :].rearrange("p (k n) -> p k n", k=KC)
        gl3 = gl[:, :].rearrange("p (k n) -> p k n", k=KC)
        qT3 = qT[:, :].rearrange("p (h n) -> p h n", h=HEADS)
        kT3 = kT[:, :].rearrange("p (h n) -> p h n", h=HEADS)
        v3 = vv[:, :].rearrange("p (t d) -> p t d", t=NT)
        ga3 = ga[:, :].rearrange("p (t d) -> p t d", t=NT)
        pa8 = pa[:, :].rearrange("p (k n) -> p k n", k=8)

        ring_free = [(UNIT_AT[name] % RING) * UNIT for name in ("wq2", "wq3")]
        u_rows = [b[:, n * D:(n + 1) * D] for b in (ga, gl, sm, tail) for n in range(2)]
        v_rows = [ig[:, n * D:(n + 1) * D] for n in range(2)] \
            + [ring[:, a + n * D:a + (n + 1) * D] for a in ring_free for n in range(4)][:NBUF - 2]
        u_here = [ctx.enter_context(nc.semaphore(f"u_here{i}")) for i in range(NBUF)]
        v_here = [ctx.enter_context(nc.semaphore(f"v_here{i}")) for i in range(NBUF)]

        nq3 = nq[:, :].rearrange("p (t n) -> p t n", t=NT)
        nT3 = at2.nT[:, :].rearrange("p (k n) -> p k n", k=KC)
        def peer_q(j):
            return (qT if j < PEER_HEADS else kT)[:, (j % PEER_HEADS) * SEQ:(j % PEER_HEADS + 1) * SEQ]

        pscore_psum = [pa[:, n * D:(n + 1) * D].rearrange("p (t m) -> p t m", t=NT) for n in range(2)]
        pscores = xc_rg[:, :].rearrange("p (t m) -> p t m", t=NT)

        STEPS2 = [(1, w, range(g * REP, (g + 1) * REP)) for w in range(2) for g in range(NKV)] \
            + [(0, w, range(NSA_HEADS)) for w in range(2)]
        pp_flat = pp[:, :, :, :].rearrange("p a b n -> p (a b n)")
        att_psum = (pp_flat[:, D:2 * D], pp_flat[:, 0:D]) + 2 * (pa[:, 0:D], pa[:, D:2 * D])
        att_shift = [lamt[:, b * 16:b * 16 + 8] for b in range(len(STEPS2))]
        att_sums = [lamt[:, b * 16 + 8:b * 16 + 16] for b in range(len(STEPS2))]

        def score2(buf, b):
            return buf.rearrange("p (h n) -> p h n", h=len(STEPS2[b][2]))

        in_bank3 = pa[:, 3 * HALF:4 * HALF]
        hid_psum, kc_psum, vc_psum = in_bank3[:, 256:320], in_bank3[0:2 * 16, 0:DH], in_bank3[:, DH:2 * DH]
        kcT_psum, csT_psum = in_bank3[:, 320:352], in_bank3[:, 0:256]
        cs_psum, co_psum = pa[:, 2 * HALF:2 * HALF + 256], pa[:, D:2 * D]

        STEPS = [(g, t) for g in range(HEADS // GRP) for t in range(NT)]

        def score_bank(t):
            n = P * (t + 1)
            return pa[:, :].rearrange("p (c h n) -> p c h n", c=2, h=GRP)[:, :, :, 0:n]

        def score_sbuf(t):
            n = P * (t + 1)
            return sm[:, :].rearrange("p (c h n) -> p c h n", c=2, h=GRP)[:, :, :, 0:n]

        block = ctx.enter_context(nc.Block())

        @block.sync
        def _(sp):
            for t in range(NT):
                sp.dma_start(x3[:, t, :], x[t * P:(t + 1) * P, :]).then_inc(s[f"x_loaded{t}"], 16)
            sp.dma_start(colt[:, :], cols).then_inc(s["cols_loaded"], 16)
            for u in range(len(UNITS)):
                if u >= RING:
                    sp.wait_ge(s["unit_used"], u - RING + 1)
                a = (u % RING) * UNIT
                sp.dma_start(ring[:, a:a + UNIT], wall[u]).then_inc(unit_ready[u % RING], 16)
                if UNITS[u] == "wq0":
                    sp.wait_ge(s["update_full"], 1)
                    sp.dma_start(lt[:, :], sub_keys).then_inc(s["keys_loaded"], 16)
            for t in range(NT):
                for c in range(2):
                    sp.wait_ge(s["y_made"], t * 2 + c + 1)
                    mine = slice(c * HALF, (c + 1) * HALF)
                    sp.dma_start(out[t * P:(t + 1) * P, mine], x3[:, t, mine]).then_inc(s["stored"], 16)
            sp.wait_ge(s["stored"], 16 * NT * 2)

        @block.gpsimd
        def _(pool):
            def step(ins):
                step.n += 1
                ins.then_inc(s["pool_step"], 1)
                pool.wait_ge(s["pool_step"], step.n)
            step.n = 0

            pool.dma_start(lamt[:, :], lambdas.broadcast_to([P, 4 * QK])).then_inc(s["lambdas_loaded"], 16)
            pool.dma_start(post_g[:, :], rows[0:1, :].broadcast_to([P, D])).then_inc(s["rows_loaded"], 16)
            nc.gpsimd.memset(ident[:, :], 0.0)
            nc.gpsimd.memset(zero[:, :], 0.0)
            step(nc.gpsimd.memset(mask1[:, :], 0.0))
            nc.gpsimd.affine_select(out=ident[:, :], in_=ident[:, :], compare_op=ALU.not_equal, fill=1.0,
                                    base=0, pattern=[[-1, P]], channel_multiplier=1).then_inc(s["identity_made"], 1)
            nc.gpsimd.affine_select(out=mask1[:, :], in_=mask1[:, :], compare_op=ALU.is_ge, fill=NEG,
                                    base=P, pattern=[[-1, SEQ]], channel_multiplier=1).then_inc(s["consts_made"], 1)
            nc.gpsimd.iota(dist_ci.rearrange("p (t n) -> p t n", t=NT), pattern=[[P, NT], [-CMP_STRIDE, 16]],
                           base=1 - CMP_LEN, channel_multiplier=1)
            step(nc.gpsimd.iota(iota16i, pattern=[[1, 16]], base=0, channel_multiplier=0))
            nc.gpsimd.tensor_copy(iota16, iota16i)
            step(nc.gpsimd.tensor_copy(dist_c, dist_ci))
            bc = bias_c.rearrange("p (t r g n) -> p t r g n", g=NKV, t=NT, r=REP)
            mc = mask_c.rearrange("p (t r g n) -> p t r g n", g=NKV, t=NT, r=REP)
            nc.gpsimd.memset(group_mask, 1.0)
            step(nc.gpsimd.memset(head_mask, 1.0))
            hm = head_mask.rearrange("p (g r) -> p g r", g=NKV)
            for sign, base in ((1, 0), (-1, 15)):
                nc.gpsimd.affine_select(out=group_mask, in_=group_mask, compare_op=ALU.is_ge, fill=0.0, base=base,
                                        pattern=[[-16 * sign, NKV]], channel_multiplier=sign)
                step(nc.gpsimd.affine_select(out=hm, in_=hm, compare_op=ALU.is_ge, fill=0.0, base=base,
                                             pattern=[[-16 * sign, NKV], [-32 * sign, REP]], channel_multiplier=sign))
            dc = dist_c.rearrange("p (t n) -> p t n", t=NT)
            for h in range(NSA_HEADS):
                ins = nc.gpsimd.tensor_scalar(mc[:, :, h % REP, h // REP, :], dc, 0.0, None, ALU.is_ge)
            step(ins)
            step(nc.gpsimd.affine_select(out=dist_c, in_=dist_c, compare_op=ALU.is_ge, fill=-NEG, base=1 - CMP_LEN,
                                         pattern=[[P, NT], [-CMP_STRIDE, 16]], channel_multiplier=1))
            for h in range(NSA_HEADS):
                ins = nc.gpsimd.tensor_scalar(bc[:, :, h % REP, h // REP, :], dc, -SLOPES[h], None, ALU.mult)
            step(ins)
            pool.wait_ge(s["block1_done"], 1)
            b3 = at2.bias[:, :].rearrange("p (h n) -> p h n", h=NSA_HEADS)
            step(nc.gpsimd.iota(b3[:, 7, :].bitcast(I32), pattern=[[-1, SEQ]], base=P, channel_multiplier=1))
            step(nc.gpsimd.tensor_copy(mask1[:, :], b3[:, 7, :].bitcast(I32)))
            step(nc.gpsimd.affine_select(out=mask1[:, :], in_=mask1[:, :], compare_op=ALU.is_ge, fill=-NEG,
                                         base=P, pattern=[[-1, SEQ]], channel_multiplier=1))
            step(nc.gpsimd.memset(at2.scan_mask, 1.0))
            nc.gpsimd.memset(at2.scan_mask.rearrange("p (c n) -> p c n", n=CH)[:, :, 0:1], 0.0)\
                .then_inc(s["scan_mask_made"], 1)
            for h in range(NSA_HEADS):
                ins = nc.gpsimd.tensor_scalar(b3[:, h, :], mask1[:, :], -SLOPES[h], None, ALU.mult)
            ins.then_inc(s["bias2_made"], 1)
            pool.wait_ge(s["block1_done"], NT)
            pool.dma_start(post_g[:, :], rows[1:2, :].broadcast_to([P, D])).then_inc(s["rows_loaded"], 16)
            pool.wait_ge(s["bias2_made"], 1)
            pool.wait_ge(s["intra_moved"], 1)
            for half in range(2):
                if half:
                    pool.wait_ge(s["intra_masked"], 1)
                a = at2.intra[half * CH:(half + 1) * CH, :].rearrange("p (c n) -> p c n", n=CH)
                nc.gpsimd.affine_select(out=a, in_=a, compare_op=ALU.is_ge, fill=0.0, base=0,
                                        pattern=[[0, HG_HEADS * NT], [1, CH]], channel_multiplier=-1)\
                    .then_inc(s["intra_masked"], 1)

            pool.wait_ge(s["intra_masked"], 2)
            def indices(kind, parity, head):
                pool.wait_ge(s["chosen"], head + 1)
                pool.sem_inc(s["pace"], 1)
                nc.gpsimd.tensor_copy(cur[kind][parity], all_experts[:, bass.ds(head * TOPK, TOPK)])\
                    .then_inc(s["cur_made"], 1)

            def gather(kind, parity, head, k):
                table, rows_to, here, free = ((peer_u, u_rows, u_here, "u_free"),
                                              (peer_v, v_rows, v_here, "v_free"))[kind]
                if kind == 1 and k in (2, 6):
                    pool.wait_ge(s["unit_used"], UNIT_AT["wq2" if k == 2 else "wq3"] + 1)
                if k % BATCH == 0:
                    pool.wait_ge(s[free], head * TOPK + k + BATCH)
                    pool.sem_inc(s["pace"], 1)
                nc.gpsimd.indirect_dma_start(out=rows_to[k % NBUF], out_offset=None, in_=table,
                                             in_offset=bass.IndirectOffsetOnAxis(ap=cur[kind][parity][:, k:k + 1], axis=0))\
                    .then_inc(here[k % NBUF], 16)

            def gather_step(n, parity):
                indices(0, parity, n + 1)
                indices(1, parity, n)
                pool.wait_ge(s["cur_made"], 2 * n + 3)
                for k in range(TOPK):
                    gather(0, parity, n + 1, k)
                    gather(1, parity, n, k)

            pool.wait_ge(s["unit_used"], UNIT_AT["wp1"] + 1)
            indices(0, 1, 0)
            pool.wait_ge(s["cur_made"], 1)
            for k in range(TOPK):
                gather(0, 1, 0, k)
            last = LAST_HEAD
            with pool.Fori(0, last // 2) as pair:
                for parity in range(2):
                    gather_step(pair * 2 + parity, parity)
            gather_step(last - 1, 0)
            indices(1, 1, last)
            pool.wait_ge(s["cur_made"], 2 * last + 2)
            for k in range(TOPK):
                gather(1, 1, last, k)

        @block.tensor
        def _(pe):
            outs = [0]

            def begin_output():
                if outs[0] >= 2:
                    pe.wait_ge(s["proj_moved"], outs[0] - 1)
                buf = pp[:, outs[0] % 2]
                outs[0] += 1
                return buf

            def take_unit(name):
                u = UNIT_AT[name]
                pe.wait_ge(unit_ready[u % RING], 16 * (u // RING + 1))
                return slot(u)

            def turn_norm(m, src, t):
                pe.wait_ge(s["scaled"], m + 1)
                for k in range(KC):
                    ins = nc.tensor.transpose(pa[:, t * D + k * P:t * D + (k + 1) * P],
                                              src[:, k * P:(k + 1) * P], ident[:, :])
                ins.then_inc(s["turned"], 1)

            def feature_major(name):
                w = take_unit(name)
                buf = begin_output().rearrange("p a (b n) -> p (a b) n", b=2)
                for c in range(4):
                    for k in range(KC):
                        ins = nc.tensor.matmul(buf[:, c, :], w[:, k, c * P:(c + 1) * P], h3[:, k, :],
                                               start=(k == 0), stop=(k == KC - 1))
                return ins

            def token_major(name, width=HALF):
                w = take_unit(name)
                buf = begin_output()
                for t in range(NT):
                    for k in range(KC):
                        ins = nc.tensor.matmul(buf[:, t, 0:width], h3[:, k, t * P:(t + 1) * P], w[:, k, 0:width],
                                               start=(k == 0), stop=(k == KC - 1))
                return ins

            def project(name, between):
                w, buf = take_unit(name), begin_output()
                flat = buf.rearrange("p a (b n) -> p (a b) n", b=2)
                for part in range(8):
                    if part in between:
                        between[part]()
                    for i in range(2 if name[:2] == "ga" else 4):
                        if name[:2] == "ga":
                            t, k = part // 4, part % 4 * 2 + i
                            ins = nc.tensor.matmul(buf[:, t, :], h3[:, k, t * P:(t + 1) * P], w[:, k, :],
                                                   start=(k == 0), stop=(k == KC - 1))
                        else:
                            c, k = part // 2, part % 2 * 4 + i
                            ins = nc.tensor.matmul(flat[:, c, :], w[:, k, c * P:(c + 1) * P], h3[:, k, :],
                                                   start=(k == 0), stop=(k == KC - 1))
                ins.then_inc(s["unit_used"], 1)

            def done(ins, name):
                ins.then_inc(s["unit_used"], 1)

            def scores(a):
                g, t = STEPS[a]
                if a == 0:
                    pe.wait_ge(s["igate_moved"], 1)
                    pe.wait_ge(s["proj_moved"], OUT_AT["k1"] + 1)
                else:
                    pe.wait_ge(s["turned_moved"], a)
                    pe.wait_ge(s["heads_moved"], a)
                n = P * (t + 1)
                for c in range(2):
                    for h in range(GRP):
                        ins = nc.tensor.matmul(score_bank(t)[:, c, h, :],
                                               qT3[c * QK:(c + 1) * QK, g * GRP + h, t * P:(t + 1) * P],
                                               kT3[c * QK:(c + 1) * QK, g * GRP + h, 0:n], start=True, stop=True)
                ins.then_inc(s["scores_full"], 1)

            def turn_weights(a):
                g, t = STEPS[a]
                pe.wait_ge(s["weights_made"], a + 1)
                for h in range(GRP):
                    for kb in range(t + 1):
                        n = h * (t + 1) + kb
                        ins = nc.tensor.transpose(pa[:, n * P:(n + 1) * P],
                                                  score_sbuf(t)[:, 0, h, kb * P:(kb + 1) * P], ident[:, :])
                ins.then_inc(s["weights_turned"], 1)

            def values(a):
                g, t = STEPS[a]
                pe.wait_ge(s["turned_moved"], a + 1)
                pe.wait_ge(s["proj_moved"], OUT_AT["v1"] + 1)
                for h in range(GRP):
                    for kb in range(t + 1):
                        n = h * (t + 1) + kb
                        ins = nc.tensor.matmul(pa[:, 2 * HALF + h * P:2 * HALF + (h + 1) * P],
                                               wT[:, n * P:(n + 1) * P],
                                               v3[:, kb, (g * GRP + h) * P:(g * GRP + h + 1) * P],
                                               start=(kb == 0), stop=(kb == t))
                ins.then_inc(s["heads_full"], 1)

            pe.wait_ge(s["identity_made"], 1)
            for t in range(NT):
                turn_norm(t, vv[:, t * D:(t + 1) * D], t)
            pe.wait_ge(s["normed"], NT)
            for name in ("xl0", "xl1", "q0", "q1"):
                done(feature_major(name), name)
            w = take_unit("lru").rearrange("p k n -> p (k n)")
            pe.wait_ge(s["conv_done"], 1)
            for n in range(KC):
                ins = nc.tensor.matmul(pa8[:, n, :], w[:, n * P:(n + 1) * P], xc3[:, n, :], start=True, stop=True)
            ins.then_inc(s["rgate_full"], 1)
            done(feature_major("k0"), "k0")
            pe.wait_ge(s["rgate_moved"], 1)
            for n in range(KC):
                ins = nc.tensor.matmul(pa8[:, n, :], w[:, D + n * P:D + (n + 1) * P], xc3[:, n, :],
                                       start=True, stop=True)
            ins.then_inc(s["unit_used"], 1)
            done(feature_major("k1"), "k1")
            for name in ("v0", "v1"):
                done(token_major(name), name)
            project("ga0", {0: lambda: scores(0), 5: lambda: turn_weights(0), 6: lambda: values(0)})
            project("ga1", {0: lambda: scores(1)})
            project("gl0", {0: lambda: turn_weights(1), 1: lambda: values(1), 2: lambda: scores(2),
                            7: lambda: turn_weights(2)})
            project("gl1", {0: lambda: values(2), 1: lambda: scores(3)})
            bufs = []
            wo = [take_unit(f"wol{c}") for c in range(2)]
            for half in range(2):
                pe.wait_ge(s["lru_done"], half + 1)
                for c in range(2):
                    if half == 0:
                        bufs.append(begin_output())
                    for t in range(NT):
                        if (half, c) == (0, 1):
                            (turn_weights, values)[t](3)
                        for k in range(4 * half, 4 * half + 4):
                            ins = nc.tensor.matmul(bufs[c][:, t, :], gl3[:, k, t * P:(t + 1) * P], wo[c][:, k, :],
                                                   start=(k == 0), stop=False)
                    if half:
                        ins.then_inc(s["unit_used"], 1)
            for t in range(NT):
                pe.wait_ge(s["head_gated"], NT + 1 + t)
                if t == 0:
                    pe.wait_ge(s["heads_moved"], len(STEPS))
                for k in range(KC):
                    ins = nc.tensor.transpose(pa[:, t * D + k * P:t * D + (k + 1) * P],
                                              ga3[:, t, k * P:(k + 1) * P], ident[:, :])
                ins.then_inc(s["attn_turned"], 1)
            wo = [take_unit(f"woa{c}") for c in range(2)]
            for t in range(NT):
                pe.wait_ge(s["attn_moved"], t + 1)
                for c in range(2):
                    for k in range(KC):
                        if (t, c, k) == (1, 1, 4):
                            turn_norm(2, vv[:, 0:D], 0)
                        ins = nc.tensor.matmul(bufs[c][:, t, :], h3[:, k, t * P:(t + 1) * P], wo[c][:, k, :],
                                               start=False, stop=(k == KC - 1))
                    if t == NT - 1:
                        ins.then_inc(s["unit_used"], 1)
                if t == 0:
                    ins.then_inc(s["wo_full"], 1)

            pe.wait_ge(s["normed"], NT + 1)
            for t in range(NT):
                if t:
                    pe.wait_ge(s["proj_moved"], OUT_AT["wo1"] + 1)
                    pe.wait_ge(s["normed"], NT + 2)
                for n, name in enumerate(("nq", "nk")):
                    w = take_unit(name)
                    for k in range(KC):
                        if (t, n, k) == (0, 1, 2):
                            turn_norm(3, vv[:, D:2 * D], 1)
                        ins = nc.tensor.matmul(pp[:, OUT_AT[name] % 2, t, :], h3[:, k, t * P:(t + 1) * P], w[:, k, :],
                                               start=(k == 0), stop=(k == KC - 1))
                    if t:
                        done(ins, name)
            outs[0] += 2
            done(feature_major("hf"), "hf")
            for t in range(NT):
                pe.wait_ge(s["nsa_scaled"], t + 1)
                for k in range(KC):
                    ins = nc.tensor.transpose(pa[:, t * D + k * P:t * D + (k + 1) * P],
                                              nq3[:, t, k * P:(k + 1) * P], ident[:, :])
                ins.then_inc(s["nsa_turned"], 1)
            done(feature_major("hq"), "hq")
            w = take_unit("cmp").rearrange("p k n -> p (k n)")
            pe.wait_ge(s["cmp_in"], 1)
            for g in range(NKV):
                half = slice(g * DH, (g + 1) * DH)
                for kv in range(2):
                    for j in range(CMP_LEN):
                        src = (at2.pe0 if j < CMP_STRIDE else at2.pe1)[half, kv * SEQ:(kv + 1) * SEQ]
                        n = (kv * CMP_LEN + j) * DH
                        ins = nc.tensor.matmul(hid_psum[half, kv * 16:kv * 16 + NCMP],
                                               w[half, n:n + DH],
                                               src[:, j:j + CMP_STRIDE * (NCMP - 1) + 1:CMP_STRIDE],
                                               start=(j == 0), stop=(j == CMP_LEN - 1))
            ins.then_inc(s["unit_used"], 1)
            done(token_major("hi"), "hi")
            pe.wait_ge(s["recur_ready"], 1)
            for h in range(HG_HEADS):
                for t in range(NT):
                    n = h * NT + t
                    ins = nc.tensor.transpose(pa[:, n * P:(n + 1) * P],
                                              at2.k4[:, h * SEQ + t * P:h * SEQ + (t + 1) * P], ident[:, :])
            ins.then_inc(s["keys_turned"], 1)
            for h in range(HG_HEADS):
                for c in range(NCH):
                    a = h * SEQ + c * CH
                    o = 2 * HALF + (h * NT + c // 2) * CH
                    half = slice((c % 2) * CH, (c % 2 + 1) * CH)
                    ins = nc.tensor.matmul(pa[half, o:o + CH], at2.k2[:, a:a + CH], at2.q1[:, a:a + CH],
                                           start=True, stop=True)
            ins.then_inc(s["intra_full"], 1)
            done(token_major("hg"), "hg")
            pe.wait_ge(s["hid_made"], 1)
            nc.tensor.matmul(kc_psum, hid_k, col("cmp_w2", 0, DH), start=True, stop=True)
            nc.tensor.matmul(vc_psum, hid_v, col("cmp_w2", DH, DH), start=True, stop=True).then_inc(s["cmp_full"], 1)
            pe.wait_ge(s["keys_moved"], 1)
            pe.wait_ge(s["proj_moved"], OUT_AT["hi"] + 1)
            pe.wait_ge(s["intra_moved"], 1)
            for c, bank in enumerate(UPDATE_BANKS):
                half = slice((c % 2) * CH, (c % 2 + 1) * CH)
                for h in range(HG_HEADS):
                    n = h * NT + c // 2
                    ins = nc.tensor.matmul(pa[:, bank * HALF + h * P:bank * HALF + (h + 1) * P],
                                           at2.k_tok[half, n * P:(n + 1) * P],
                                           at2.v[half, (c // 2) * HALF + h * P:(c // 2) * HALF + (h + 1) * P],
                                           start=True, stop=True)
            ins.then_inc(s["update_full"], 1)
            done(token_major("nv", NQW - 2 * HALF), "nv")

            pe.wait_ge(s["cmp_ready"], 1)
            nc.tensor.transpose(kcT_psum, at2.kc, ident[0:2 * 16, 0:2 * 16]).then_inc(s["cmp_turned"], 1)
            def att_scores(b):
                t, w, heads = STEPS2[b]
                for i, h in enumerate(heads):
                    half = slice(h // REP * DH, (h // REP + 1) * DH)
                    ins = nc.tensor.matmul(score2(att_psum[b], b)[:, i, :], nT3[half, h % REP, t * P:(t + 1) * P],
                                           nT3[half, 4 + w, 0:(t + 1) * P], start=True, stop=True)
                ins.then_inc(s["att_full"], 1)

            def att_turn(b):
                t, w, heads = STEPS2[b]
                pe.wait_ge(s["att_exp"], b + 1)
                for n in range(KC):
                    ins = nc.tensor.transpose(att_psum[b][:, n * P:(n + 1) * P],
                                              at2.sc[b % 4][:, n * P:(n + 1) * P], ident[:, :])
                ins.then_inc(s["att_turned"], 1)

            def att_values(b):
                t, w, heads = STEPS2[b]
                pe.wait_ge(s["att_moved"], b + 1)
                for i, h in enumerate(heads):
                    for kb in range(t + 1):
                        n = i * (t + 1) + kb
                        a = D + w * P + h // REP * DH
                        ins = nc.tensor.matmul(att_psum[b][:, i * DH:(i + 1) * DH],
                                               at2.pT[b % 4][:, n * P:(n + 1) * P],
                                               nq3[:, kb, a:a + DH], start=(kb == 0), stop=(kb == t))
                ins.then_inc(s["ao_full"], 1)

            pe.wait_ge(s["proj_moved"], OUT_AT["hg"] + 1)
            att_scores(0)
            pe.wait_ge(s["intra_masked"], 2)
            pe.wait_ge(s["states_made"], 1)
            for c in range(NCH):
                half = slice((c % 2) * CH, (c % 2 + 1) * CH)
                for h in range(HG_HEADS):
                    o = pa[half, (c // 2) * HALF + h * P:(c // 2) * HALF + (h + 1) * P]
                    n = (h * NT + c // 2) * CH
                    ins = nc.tensor.matmul(o, at2.intra[half, n:n + CH],
                                           at2.v[half, (c // 2) * HALF + h * P:(c // 2) * HALF + (h + 1) * P],
                                           start=True, stop=(c == 0))
                    if c:
                        a = h * SEQ + c * CH
                        ins = nc.tensor.matmul(o, at2.q3[:, a:a + CH],
                                               at2.states[:, (c - 1) * HALF + h * P:(c - 1) * HALF + (h + 1) * P],
                                               start=False, stop=True)
            ins.then_inc(s["o_full"], 1)

            pe.wait_ge(s["cmpT_made"], 1)
            for t in range(NT):
                for r in range(REP):
                    a = (t * REP + r) * 32
                    ins = nc.tensor.matmul(cs_psum[:, a:a + 32], nT3[:, r, t * P:(t + 1) * P], kcT,
                                           start=True, stop=True)
            ins.then_inc(s["cs_full"], 1)
            pe.wait_ge(s["proj_moved"], OUT_AT["nv"] + 1)
            att_scores(1)
            att_turn(0)
            pe.wait_ge(s["cs_ready"], 1)
            for t in range(NT):
                ins = nc.tensor.transpose(csT_psum[:, t * P:(t + 1) * P], e_c[:, t * P:(t + 1) * P], ident[:, :])
            ins.then_inc(s["cs_turned"], 1)
            att_turn(1)
            pe.wait_ge(s["csT_moved"], 1)
            pe.wait_ge(s["v_blocks_made"], 1)
            for t in range(NT):
                ins = nc.tensor.matmul(co_psum[:, t * HALF:(t + 1) * HALF], at2.cT[:, t * P:(t + 1) * P], at2.v_blocks,
                                       start=True, stop=True)
            ins.then_inc(s["co_full"], 1)
            pe.wait_ge(s["o_moved"], 1)
            pe.wait_ge(s["co_used"], 1)
            att_scores(2)
            att_scores(3)
            att_values(0)
            att_values(1)
            att_turn(2)
            att_turn(3)
            pe.wait_ge(s["ao_used"], 2)
            pe.wait_ge(s["o_gated"], 1)
            for k in range(4):
                for t in range(NT):
                    ins = nc.tensor.transpose(pp_flat[:, k * SEQ + t * P:k * SEQ + (t + 1) * P],
                                              at2.o[:, t * HALF + k * P:t * HALF + (k + 1) * P], ident[:, :])
            ins.then_inc(s["mix_turned"], 1)
            att_values(2)
            att_values(3)

            wp = [take_unit(f"wp{c}") for c in range(2)]

            def mixed(t, ks):
                for c in range(2):
                    for k in ks:
                        ins = nc.tensor.matmul(pp[:, c, t, :], h3[:, k, t * P:(t + 1) * P], wp[c][:, k, :],
                                               start=(k == 0), stop=(k == KC - 1))
                    if (t, ks[-1]) == (0, KC - 1):
                        ins.then_inc(s["unit_used"], 1)
                return ins

            def turn_sparse(t, to):
                pe.wait_ge(s["nsa_out"], NT - t)
                for k in range(4):
                    ins = nc.tensor.transpose(to[:, k * P:(k + 1) * P],
                                              at2.no[:, t * HALF + k * P:t * HALF + (k + 1) * P], ident[:, :])
                ins.then_inc(s["mix_turned"], 1)

            pe.wait_ge(s["mixT_made"], 1)
            outs[0] += 2
            mixed(1, range(4))
            for b in (4, 5):
                pe.wait_ge(s["ao_used"], b - 1)
                att_scores(b)
            mixed(0, range(4))
            att_turn(4)
            att_turn(5)
            att_values(4)
            turn_sparse(1, pa[:, HALF:2 * HALF])
            att_values(5)
            pe.wait_ge(s["mixT_made"], 2)
            mixed(1, range(4, KC)).then_inc(s["wp_full"], 1)
            turn_sparse(0, pa[:, 3 * HALF:4 * HALF])
            pe.wait_ge(s["mixT_made"], 3)
            mixed(0, range(4, KC))

            turn_norm(4, vv[:, D:2 * D], 1)
            w = take_unit("ple").rearrange("p k n -> p (k n)")
            for c in range(2):
                buf = begin_output()
                for t in range(NT):
                    for k in range(PLE // P):
                        ins = nc.tensor.matmul(buf[:, t, :], w[:, 2 * D + k * SEQ + t * P:2 * D + k * SEQ + (t + 1) * P],
                                               w[:, k * D + c * HALF:k * D + (c + 1) * HALF],
                                               start=(k == 0), stop=(k == PLE // P - 1))
                if c == 0:
                    ins.then_inc(s["ple_full"], 1)
                    turn_norm(5, vv[:, 0:D], 0)
            ins.then_inc(s["unit_used"], 1)
            pe.wait_ge(s["normed"], 3 * NT)
            keys = lt[:, :]
            pe.wait_ge(s["keys_loaded"], 16)

            def key_scores(c, tiles, halves):
                for t in tiles:
                    for n in halves:
                        j = 4 * c + n
                        ins = nc.tensor.matmul(pscore_psum[c % 2][:, t, n * P:(n + 1) * P],
                                               peer_q(j)[:, t * P:(t + 1) * P],
                                               keys[:, j * NKEYS:(j + 1) * NKEYS], start=True, stop=True)
                return ins

            def seed(t):
                for c in range(2):
                    nc.tensor.matmul(pp[:, t, c, :], ident[:, :], x3[:, t, c * HALF:(c + 1) * HALF],
                                     start=True, stop=True)

            for c in range(4):
                w = take_unit(f"wq{c}")
                buf = begin_output().rearrange("p a (b n) -> p (a b) n", b=2)
                for m in range(4):
                    if (c, m) == (0, 3):
                        pe.wait_ge(s["first_moved"], 1)
                        key_scores(0, (0,), (0, 1)).then_inc(s["first_scores"], 1)
                    if c >= 2 and m == 1:
                        pe.wait_ge(s["proj_moved"], OUT_AT[f"wq{c - 1}"] + 1)
                        if c == 3:
                            pe.wait_ge(s["pscore_moved"], 1)
                        key_scores(c - 1, range(NT), range(4)).then_inc(s["pscore_full"], 1)
                    for k in range(KC):
                        ins = nc.tensor.matmul(buf[:, m, :], w[:, k, m * P:(m + 1) * P], h3[:, k, :],
                                               start=(k == 0), stop=(k == KC - 1))
                    if (c, m) == (0, 1):
                        ins.then_inc(s["first_query"], 1)
                ins.then_inc(s["unit_used"], 1)
                if c == 0:
                    pe.wait_ge(s["first_taken"], 1)
                    pe.wait_ge(s["proj_moved"], OUT_AT["wq0"] + 1)
                    key_scores(0, (0,), (2, 3))
                    key_scores(0, (1,), range(4)).then_inc(s["pscore_full"], 1)
            seed(1)
            pe.wait_ge(s["proj_moved"], OUT_AT["wq3"] + 1)
            pe.wait_ge(s["pscore_moved"], 2)
            key_scores(3, range(NT), range(4)).then_inc(s["pscore_full"], 1)
            seed(0)
            def expert_sums(t, head):
                for k in range(TOPK):
                    pe.wait_ge(s["diag_made"], head * TOPK + k + 1)
                    pe.wait_ge(v_here[k % NBUF], (head * 2 + k // NBUF + 1) * 16)
                    n = k % DIAGS
                    for c in range(2):
                        ins = nc.tensor.matmul(pp[:, t, c, :], diag[:, n * P:(n + 1) * P],
                                               v_rows[k % NBUF][:, c * HALF:(c + 1) * HALF],
                                               start=False, stop=True, skip_group_check=True)
                    ins.then_inc(s["v_free"], 1)

            def turn_sums(t):
                pe.wait_ge(s["h2_made"], t + 1)
                for k in range(KC):
                    ins = nc.tensor.transpose(pa[:, t * D + k * P:t * D + (k + 1) * P],
                                              x3[:, t, k * P:(k + 1) * P], ident[:, :])
                ins.then_inc(s["turned"], 1)

            def embedding_gate(t, c):
                w = take_unit(f"gw{c}")
                for k in range(KC):
                    ins = nc.tensor.matmul(pp[:, t, c, :], h3[:, k, t * P:(t + 1) * P], w[:, k, :],
                                           start=(k == 0), stop=(k == KC - 1))
                ins.then_inc(s["gate_full"], 1)

            with pe.Fori(0, PEER_HEADS // 2) as pair:
                for odd in range(2):
                    expert_sums(0, pair * 2 + odd)
            expert_sums(1, PEER_HEADS)
            turn_sums(0)
            pe.wait_ge(s["normed"], 3 * NT + 1)
            embedding_gate(0, 0)
            expert_sums(1, PEER_HEADS + 1)
            embedding_gate(0, 1)
            with pe.Fori(PEER_HEADS // 2 + 1, PEER_HEADS) as pair:
                for odd in range(2):
                    expert_sums(1, pair * 2 + odd)
            turn_sums(1)
            pe.wait_ge(s["normed"], 4 * NT)
            for c in range(2):
                embedding_gate(1, c)

        @block.scalar
        def _(act):
            def full(name):
                unit = {"wo0": "woa0", "wo1": "woa1"}.get(name, name)
                act.wait_ge(s["unit_used"], UNIT_AT[unit] + 1)
                return pp[:, OUT_AT[name] % 2]

            def step(ins):
                step.n += 1
                ins.then_inc(s["act_step"], 1)
                act.wait_ge(s["act_step"], step.n)
            step.n = 0

            def move(name, dst, func=ACT.Copy, width=HALF):
                nc.scalar.activation(dst, full(name)[:, :, 0:width], func).then_inc(s["proj_moved"], 1)

            def norm_std(m):
                act.wait_ge(s["squares_summed"], m + 1)
                nc.scalar.activation(stat[:, 16 + m:17 + m], stat[:, m:m + 1], ACT.Sqrt, bias=eps_col, scale=1.0 / D)\
                    .then_inc(s["std_made"], 1)

            eps_col = small[:, 250:251]
            for t in range(NT):
                norm_std(t)
            for c in range(2):
                nc.scalar.activation(xl3[:, 4 * c:4 * c + 4, PAD:XS],
                                     full(f"xl{c}").rearrange("p a (b n) -> p (a b) n", b=2), ACT.Copy)\
                    .then_inc(s["proj_moved"], 1)
            act.wait_ge(s["lambda_sums"], 1)
            nc.scalar.activation(small[:, 2:4], small[:, 0:2], ACT.Exp)
            nc.scalar.activation(small[:, 16:24], small[:, 8:16], ACT.Exp, scale=-1.0).then_inc(s["lambda_exps"], 1)
            for c in range(2):
                move(f"q{c}", qT[:, c * D:(c + 1) * D].rearrange("p (a n) -> p a n", a=2))
            act.wait_ge(s["rgate_full"], 1)
            for n in range(KC):
                ins = nc.scalar.activation(rg3[:, n, :], pa8[:, n, :], ACT.Sigmoid, bias=col("b_r", n))
            ins.then_inc(s["rgate_moved"], 1)
            act.wait_ge(s["decay_log"], 1)
            nc.scalar.activation(lt[:, :], rg[:, :], ACT.Tanh).then_inc(s["tanh_made"], 1)
            step(nc.scalar.activation(xl[:, 0:KC * SEQ], rg[:, :], ACT.Exp, scale=-1.0))
            move("k0", kT[:, 0:D].rearrange("p (a n) -> p a n", a=2))
            act.wait_ge(s["unit_used"], UNIT_AT["lru"] + 1)
            for n in range(KC):
                ins = nc.scalar.activation(ig3[:, n, :], pa8[:, n, :], ACT.Sigmoid, bias=col("b_i", n))
            ins.then_inc(s["igate_moved"], 1)
            move("k1", kT[:, D:2 * D].rearrange("p (a n) -> p a n", a=2))
            act.wait_ge(s["mult_sq"], 1)
            nc.scalar.activation(lt[:, :], lt[:, :], ACT.Sqrt, scale=2.0).then_inc(s["mult_made"], 1)
            for c in range(2):
                move(f"v{c}", v3[:, :, c * HALF:(c + 1) * HALF])

            def exps(a):
                g, t = STEPS[a]
                act.wait_ge(s["bias_made"], a + 1)
                for n in range(2 * GRP):
                    src = score_sbuf(t)[:, n // GRP, n % GRP, :]
                    ins = nc.scalar.activation(src, src, ACT.Exp, bias=small[:, 40 + n:41 + n], scale=SCALE1,
                                               accum_out=small[:, 48 + n:49 + n])
                ins.then_inc(s["probs_made"], 1)

            def gate(name):
                c = int(name[2])
                if name[:2] == "ga":
                    move(name, ga3[:, :, c * HALF:(c + 1) * HALF], ACT.Silu)
                else:
                    move(name, gl[:, c * D:(c + 1) * D].rearrange("p (a n) -> p a n", a=2), ACT.Silu)

            def move_weights(a):
                act.wait_ge(s["weights_turned"], a + 1)
                n = GRP * (STEPS[a][1] + 1) * P
                nc.scalar.activation(wT[:, 0:n], pa[:, 0:n], ACT.Copy).then_inc(s["turned_moved"], 1)

            def move_heads(a):
                act.wait_ge(s["heads_full"], a + 1)
                if a:
                    act.wait_ge(s["head_gated"], a)
                nc.scalar.activation(oh[:, :], pa[:, 2 * HALF:3 * HALF], ACT.Copy).then_inc(s["heads_moved"], 1)

            def head_std(a):
                act.wait_ge(s["head_sums"], a + 1)
                nc.scalar.activation(small[:, 64:68], small[:, 60:64], ACT.Sqrt, bias=eps_col, scale=1.0 / P)\
                    .then_inc(s["head_std"], 1)

            exps(0)
            move_weights(0)
            move_heads(0)
            gate("ga0")
            exps(1)
            head_std(0)
            gate("ga1")
            move_weights(1)
            move_heads(1)
            exps(2)
            head_std(1)
            move_weights(2)
            gate("gl0")
            move_heads(2)
            exps(3)
            head_std(2)
            gate("gl1")
            move_weights(3)
            move_heads(3)
            head_std(3)
            for t in range(NT):
                act.wait_ge(s["attn_turned"], t + 1)
                nc.scalar.activation(h3[:, :, t * P:(t + 1) * P],
                                     pa[:, t * D:(t + 1) * D].rearrange("p (k n) -> p k n", k=KC),
                                     ACT.Copy, scale=small[:, 80:81]).then_inc(s["attn_moved"], 1)
            for t in range(NT):
                if t == 0:
                    act.wait_ge(s["wo_full"], 1)
                else:
                    act.wait_ge(s["unit_used"], UNIT_AT["woa1"] + 1)
                for c in range(2):
                    ins = nc.scalar.activation(junk1[:, c * HALF:(c + 1) * HALF], pp[:, c, t, :], ACT.Square,
                                               accum_out=stat[:, 32 + 2 * c + t:33 + 2 * c + t])
                step(ins)
                step(nc.scalar.activation(stat[:, 36 + t:37 + t], stat[:, 32 + t:33 + t], ACT.Identity,
                                          bias=stat[:, 34 + t:35 + t]))
                nc.scalar.activation(stat[:, 38 + t:39 + t], stat[:, 36 + t:37 + t], ACT.Sqrt, bias=eps_col,
                                     scale=1.0 / D).then_inc(s["post_std"], 1)
                norm_std(2 + t)

            act.wait_ge(s["lb_shifted"], 1)
            nc.scalar.activation(lbt[:, 4:12], lbt[:, 4:12], ACT.Exp).then_inc(s["lb_exp"], 1)
            move("nq", nq3[:, :, 0:HALF])
            move("nk", nq3[:, :, HALF:2 * HALF])
            for t in range(NT):
                act.wait_ge(s["nsa_sums"], t + 1)
                nc.scalar.activation(st2[:, 16 + 12 * t:28 + 12 * t], st2[:, 40 + 12 * t:52 + 12 * t], ACT.Sqrt,
                                     bias=eps_col, scale=1.0 / DH).then_inc(s["nsa_std"], 1)
            nc.scalar.activation(at2.key.rearrange("p (a n) -> p a n", a=2), full("hf"), ACT.Sigmoid)\
                .then_inc(s["proj_moved"], 1)
            move("hq", at2.query.rearrange("p (a n) -> p a n", a=2), ACT.Silu)
            act.wait_ge(s["forget_made"], 1)
            nc.scalar.activation(at2.log_f, at2.key, ACT.Ln).then_inc(s["log_made"], 1)
            act.wait_ge(s["shift_made"], 1)
            nc.scalar.activation(at2.q1, at2.shift, ACT.Exp)
            nc.scalar.activation(at2.k2, at2.shift, ACT.Exp, scale=-1.0)
            nc.scalar.activation(at2.q3, at2.cum, ACT.Exp)
            nc.scalar.activation(last_exp, at2.cum[:, CH - 1::CH], ACT.Exp).then_inc(s["shift_exp"], 1)
            act.wait_ge(s["last_made"], 1)
            nc.scalar.activation(at2.k4, at2.shift, ACT.Exp).then_inc(s["last_exp"], 1)
            act.wait_ge(s["unit_used"], UNIT_AT["cmp"] + 1)
            for g in range(NKV):
                half = slice(g * DH, (g + 1) * DH)
                nc.scalar.activation(hid_k[half, g * 16:g * 16 + NCMP], hid_psum[half, 0:NCMP], ACT.Gelu_apprx_tanh)
                ins = nc.scalar.activation(hid_v[half, :].rearrange("p (r m) -> p r m", r=REP)
                                           [:, :, g * 16:g * 16 + NCMP],
                                           hid_psum[half, 16:16 + NCMP].unsqueeze(1).broadcast_to([DH, REP, NCMP]),
                                           ACT.Gelu_apprx_tanh)
            ins.then_inc(s["hid_made"], 1)
            move("hi", at2.v.rearrange("p (a n) -> p a n", a=2))
            act.wait_ge(s["keys_turned"], 1)
            nc.scalar.activation(at2.k_tok, pa[:, 0:D], ACT.Copy).then_inc(s["keys_moved"], 1)
            act.wait_ge(s["intra_full"], 1)
            nc.scalar.activation(at2.intra, pa[:, 2 * HALF:3 * HALF], ACT.Copy).then_inc(s["intra_moved"], 1)
            move("hg", at2.gate.rearrange("p (a n) -> p a n", a=2), ACT.Silu)
            act.wait_ge(s["cmp_sums"], 1)
            nc.scalar.activation(st2[0:32, 65:66], st2[0:32, 64:65], ACT.Sqrt, bias=eps_col[0:32, :],
                                 scale=1.0 / DH).then_inc(s["cmp_std"], 1)
            buf = full("nv")
            nc.scalar.activation(nq3[:, :, NQW - GATES:NQW], buf[:, :, 2 * NKV * DH:2 * NKV * DH + GATES], ACT.Sigmoid)
            nc.scalar.activation(nq3[:, :, D:NQW - GATES], buf[:, :, 0:2 * NKV * DH], ACT.Copy)\
                .then_inc(s["proj_moved"], 1)
            act.wait_ge(s["cmp_turned"], 1)
            nc.scalar.activation(kcT, kcT_psum, ACT.Copy, scale=col("nk_g", 0)).then_inc(s["cmpT_made"], 1)

            def att_exps(b):
                act.wait_ge(s["att_bias"], b + 1)
                for i in range(len(STEPS2[b][2])):
                    src = score2(at2.sc[b % 4], b)[:, i, :]
                    ins = nc.scalar.activation(src, src, ACT.Exp, bias=att_shift[b][:, i:i + 1],
                                               accum_out=att_sums[b][:, i:i + 1])
                ins.then_inc(s["att_exp"], 1)

            def att_move(b):
                act.wait_ge(s["att_turned"], b + 1)
                nc.scalar.activation(at2.pT[b % 4], att_psum[b], ACT.Copy).then_inc(s["att_moved"], 1)

            def sparse_std(t):
                act.wait_ge(s["nsa_osums"], NT - t)
                nc.scalar.activation(st2[:, 112 + 8 * t:120 + 8 * t], st2[:, 96 + 8 * t:104 + 8 * t], ACT.Sqrt,
                                     bias=eps_col, scale=1.0 / DH).then_inc(s["nsa_ostd"], 1)

            att_exps(0)
            act.wait_ge(s["cs_shifted"], 1)
            nc.scalar.activation(e_c, e_c, ACT.Exp).then_inc(s["cs_exp"], 1)
            act.wait_ge(s["o_full"], 1)
            nc.scalar.activation(at2.o, pa[:, 0:D], ACT.Copy).then_inc(s["o_moved"], 1)
            att_exps(1)
            att_move(0)
            act.wait_ge(s["cs_turned"], 1)
            nc.scalar.activation(at2.cT[:, 0:SEQ], csT_psum, ACT.Copy).then_inc(s["csT_moved"], 1)
            att_move(1)
            for b in (2, 3):
                att_exps(b)
            act.wait_ge(s["o_sums"], 1)
            nc.scalar.activation(st2[:, 0:8], st2[:, 8:16], ACT.Sqrt, bias=eps_col, scale=1.0 / P)\
                .then_inc(s["o_std"], 1)
            for b in (2, 3):
                att_move(b)
            for b in (4, 5):
                att_exps(b)
            sparse_std(1)
            for b in (4, 5):
                att_move(b)
            sparse_std(0)

            for t in range(NT):
                norm_std(4 + t)
            for c in range(2):
                if c == 0:
                    act.wait_ge(s["ple_full"], 1)
                else:
                    act.wait_ge(s["unit_used"], UNIT_AT["ple"] + 1)
                nc.scalar.activation(nq[:, 0:2 * D].rearrange("p (t d) -> p t d", t=NT)
                                     [:, :, c * HALF:(c + 1) * HALF], pp[:, OUT_AT[f"ple{c}"] % 2], ACT.Copy)\
                    .then_inc(s["proj_moved"], 1)
            def scores_moved(c):
                act.wait_ge(s["pscore_full"], c + 1)
                if c == 0:
                    nc.scalar.activation(pscores[:, 0, 2 * P:HALF], pscore_psum[0][:, 0, 2 * P:HALF], ACT.Copy)
                    ins = nc.scalar.activation(pscores[:, 1, 0:HALF], pscore_psum[0][:, 1, :], ACT.Copy)
                else:
                    ins = nc.scalar.activation(pscores[:, :, c * HALF:(c + 1) * HALF], pscore_psum[c % 2], ACT.Copy)
                ins.then_inc(s["pscore_moved"], 2 if c == 3 else 1)

            def queries_moved(c):
                b = (qT if c < 2 else kT)[:, (c % 2) * D:(c % 2 + 1) * D].rearrange("p (a n) -> p a n", a=2)
                move(f"wq{c}", b)

            act.wait_ge(s["first_query"], 1)
            first = pp[:, OUT_AT["wq0"] % 2]
            nc.scalar.activation(qT[:, 0:HALF], first[:, 0, :], ACT.Copy).then_inc(s["first_moved"], 1)
            act.wait_ge(s["first_scores"], 1)
            nc.scalar.activation(pscores[:, 0, 0:2 * P], pscore_psum[0][:, 0, 0:2 * P], ACT.Copy)\
                .then_inc(s["first_taken"], 1)
            act.wait_ge(s["unit_used"], UNIT_AT["wq0"] + 1)
            nc.scalar.activation(qT[:, HALF:D], first[:, 1, :], ACT.Copy).then_inc(s["proj_moved"], 1)
            scores_moved(0)
            queries_moved(1)
            scores_moved(1)
            queries_moved(2)

            def top_exp(head, odd):
                act.wait_ge(s["top_shift"], head + 1)
                nc.scalar.activation(top_w[odd], top_w[odd], ACT.Exp).then_inc(s["top_exp"], 1)

            def head_gelus(head, odd):
                act.wait_ge(s["u_free"], head * TOPK + NBUF + TOPK)
                mine = slice(odd * TOPK, (odd + 1) * TOPK)
                nc.scalar.activation(acts[:, mine], dots[:, mine], ACT.Gelu_apprx_tanh).then_inc(s["gelu_made"], 1)

            def head_diags(head, odd):
                act.wait_ge(s["w_made"], head + 1)
                for k in range(TOPK):
                    act.wait_ge(s["v_free"], head * TOPK + k + 1 + NBUF - DIAGS)
                    n = k % DIAGS
                    a = odd * TOPK + k
                    nc.scalar.activation(diag[:, n * P:(n + 1) * P], ident[:, :], ACT.Copy, scale=wk[:, a:a + 1])\
                        .then_inc(s["diag_made"], 1)

            def tile_sums(t):
                act.wait_ge(s["v_free"], NBUF + (t + 1) * NSLOT)
                nc.scalar.activation(x3[:, t, :].rearrange("p (c n) -> p c n", c=2), pp[:, t, :, :], ACT.Copy)\
                    .then_inc(s["h2_made"], 1)

            def gate_moves(t):
                for c in range(2):
                    act.wait_ge(s["gate_full"], t * 2 + c + 1)
                    if c == 0:
                        act.wait_ge(s["scaled"], 3 * NT + t + 1)
                    nc.scalar.activation(lt[:, t * D + c * HALF:t * D + (c + 1) * HALF], pp[:, t, c, :], ACT.Sigmoid,
                                         scale=stat[:, 30 + t:31 + t])\
                        .then_inc(s["gate_moved"], 1)

            top_exp(0, 0)
            scores_moved(2)
            top_exp(1, 1)
            head_gelus(0, 0)
            queries_moved(3)
            head_diags(0, 0)
            scores_moved(3)
            top_exp(2, 0)
            head_gelus(1, 1)
            head_diags(1, 1)
            with act.Fori(1, PEER_HEADS // 2) as pair:
                for odd in range(2):
                    top_exp(pair * 2 + odd + 1, 1 - odd)
                    head_gelus(pair * 2 + odd, odd)
                    head_diags(pair * 2 + odd, odd)
            tile_sums(0)
            top_exp(PEER_HEADS + 1, 1)
            head_gelus(PEER_HEADS, 0)
            norm_std(6)
            head_diags(PEER_HEADS, 0)
            top_exp(PEER_HEADS + 2, 0)
            head_gelus(PEER_HEADS + 1, 1)
            head_diags(PEER_HEADS + 1, 1)
            with act.Fori(PEER_HEADS // 2 + 1, PEER_HEADS - 1) as pair:
                for odd in range(2):
                    top_exp(pair * 2 + odd + 1, 1 - odd)
                    head_gelus(pair * 2 + odd, odd)
                    head_diags(pair * 2 + odd, odd)
            top_exp(LAST_HEAD, 1)
            head_gelus(LAST_HEAD - 1, 0)
            head_diags(LAST_HEAD - 1, 0)
            head_gelus(LAST_HEAD, 1)
            gate_moves(0)
            head_diags(LAST_HEAD, 1)
            tile_sums(1)
            norm_std(7)
            gate_moves(1)

        @block.vector
        def _(dve):
            counts = {}

            def step(ins, name="dve_step"):
                counts[name] = counts.get(name, 0) + 1
                ins.then_inc(s[name], 1)
                dve.wait_ge(s[name], counts[name])

            V = nc.vector
            eps_col = small[:, 250:251]

            def norm(m, src, junk):
                step(V.tensor_tensor_reduce(out=junk, in0=src, in1=src, scale=1.0, scalar=0.0, op0=ALU.mult,
                                            op1=ALU.add, accum_out=stat[:, m:m + 1]), "squares_summed")
                dve.wait_ge(s["std_made"], m + 1)
                step(V.reciprocal(stat[:, 24 + m:25 + m], stat[:, 16 + m:17 + m]))
                step(V.tensor_scalar(junk, src, stat[:, 24 + m:25 + m], None, ALU.mult), "scaled")

            def norm_out(m, gain, t):
                dve.wait_ge(s["turned"], m + 1)
                step(V.tensor_tensor(h3[:, :, t * P:(t + 1) * P],
                                     pa[:, t * D:(t + 1) * D].rearrange("p (k n) -> p k n", k=KC),
                                     gain.unsqueeze(2).broadcast_to([P, KC, P]), ALU.mult), "normed")

            step(V.memset(eps_col, EPS))
            for t in range(NT):
                dve.wait_ge(s[f"x_loaded{t}"], 16)
                norm(t, x3[:, t, :], vv[:, t * D:(t + 1) * D])
            step(V.memset(xl3[:, :, 0:PAD], 0.0))
            dve.wait_ge(s["cols_loaded"], 16)
            for t in range(NT):
                norm_out(t, col("pre_g", 0, KC), t)

            dve.wait_ge(s["lambdas_loaded"], 16)
            for j in range(2):
                V.tensor_tensor_reduce(out=lamt[:, 2 * j * QK:(2 * j + 1) * QK],
                                       in0=lamt[:, 2 * j * QK:(2 * j + 1) * QK],
                                       in1=lamt[:, (2 * j + 1) * QK:(2 * j + 2) * QK], scale=1.0, scalar=0.0,
                                       op0=ALU.mult, op1=ALU.add, accum_out=small[:, j:j + 1])
            step(V.tensor_scalar(small[:, 24:32], col("lam", 0, KC), -1.0, None, ALU.mult))
            step(V.tensor_tensor(small[:, 8:16], small[:, 24:32], col("lam", 0, KC), ALU.max), "lambda_sums")
            V.tensor_scalar(small[:, 80:81], col("sub_g"), 1.0 - LAM_INIT, None, ALU.mult)

            for c in range(2):
                dve.wait_ge(s["proj_moved"], OUT_AT[f"xl{c}"] + 1)
                for j in range(TAPS):
                    for k in range(4 * c, 4 * c + 4):
                        src = xl3[:, k, PAD - TAPS + 1 + j:PAD - TAPS + 1 + j + SEQ]
                        if j == 0:
                            ins = V.tensor_scalar(xc3[:, k, :], src, col("conv_w", k), col("conv_b", k),
                                                  ALU.mult, ALU.add)
                        else:
                            ins = V.scalar_tensor_tensor(out=xc3[:, k, :], in0=src, scalar=col("conv_w", j * KC + k),
                                                         in1=xc3[:, k, :], op0=ALU.mult, op1=ALU.add)
                    if c == 1 and j == TAPS - 1:
                        step(ins, "conv_done")
                    else:
                        step(ins)

            dve.wait_ge(s["lambda_exps"], 1)
            step(V.tensor_tensor(small[:, 4:5], small[:, 3:4], small[:, 2:3], ALU.subtract))
            step(V.tensor_scalar(small[:, 5:6], small[:, 4:5], -LAM_INIT, None, ALU.add))
            e, z, z2, acc = small[:, 16:24], small[:, 100:108], small[:, 108:116], small[:, 116:124]
            step(V.tensor_scalar(z, e, 2.0, None, ALU.add))
            step(V.reciprocal(z, z))
            step(V.tensor_tensor(z, z, e, ALU.mult))
            step(V.tensor_tensor(z2, z, z, ALU.mult))
            terms = 9
            step(V.tensor_scalar(acc, z2, 2.0 / (2 * terms + 1), 2.0 / (2 * terms - 1), ALU.mult, ALU.add))
            for n in range(terms - 2, -1, -1):
                step(V.tensor_tensor(acc, acc, z2, ALU.mult))
                step(V.tensor_scalar(acc, acc, 2.0 / (2 * n + 1), None, ALU.add))
            step(V.tensor_tensor(acc, acc, z, ALU.mult))
            step(V.scalar_tensor_tensor(out=acc, in0=small[:, 24:32], scalar=0.0, in1=acc, op0=ALU.max, op1=ALU.add))
            step(V.tensor_scalar(small[:, 32:40], acc, LRU_C, None, ALU.mult))
            dve.wait_ge(s["rgate_moved"], 1)
            step(V.tensor_tensor(rg3, rg3, small[:, 32:40].unsqueeze(2).broadcast_to([P, KC, SEQ]), ALU.mult),
                 "decay_log")
            dve.wait_ge(s["tanh_made"], 1)
            dve.wait_ge(s["act_step"], 1)
            step(V.tensor_scalar(rg[:, :], lt[:, :], 1.0, None, ALU.add))
            step(V.reciprocal(rg[:, :], rg[:, :]))
            step(V.scalar_tensor_tensor(out=lt[:, :], in0=lt[:, :], scalar=0.0, in1=rg[:, :], op0=ALU.max,
                                        op1=ALU.mult), "mult_sq")
            dve.wait_ge(s["igate_moved"], 1)
            step(V.tensor_tensor(ig[:, :], ig[:, :], xc[:, :], ALU.mult))

            def attention_scores(a):
                g, t = STEPS[a]
                n = P * (t + 1)
                if a == 0:
                    dve.wait_ge(s["consts_made"], 1)
                dve.wait_ge(s["scores_full"], a + 1)
                if a:
                    dve.wait_ge(s["weights_turned"], a)
                for c in range(2):
                    ins = V.tensor_tensor(score_sbuf(t)[:, c], score_bank(t)[:, c],
                                          mask1[:, SEQ - n:SEQ].unsqueeze(1).broadcast_to([P, GRP, n]), ALU.add)
                step(ins)
                step(V.tensor_reduce(small[:, 56 + 16:56 + 24], score_sbuf(t), AX, ALU.max))
                step(V.tensor_scalar(small[:, 40:48], small[:, 72:80], -SCALE1, None, ALU.mult), "bias_made")

            def attention_weights(a):
                g, t = STEPS[a]
                n = P * (t + 1)
                dve.wait_ge(s["probs_made"], a + 1)
                step(V.reciprocal(small[:, 84:92], small[:, 48:56]))
                step(V.tensor_scalar(small[:, 88:92], small[:, 88:92], small[:, 5:6], None, ALU.mult))
                for c in range(2):
                    sc = score_sbuf(t)[:, c]
                    ins = V.tensor_tensor(sc, sc, small[:, 84 + 4 * c:88 + 4 * c].unsqueeze(2)
                                          .broadcast_to([P, GRP, n]), ALU.mult)
                step(ins)
                step(V.tensor_tensor(score_sbuf(t)[:, 0], score_sbuf(t)[:, 0], score_sbuf(t)[:, 1], ALU.add),
                     "weights_made")

            def head_squares(a):
                dve.wait_ge(s["heads_moved"], a + 1)
                step(V.tensor_tensor(osq[:, :], oh[:, :], oh[:, :], ALU.mult))
                step(V.tensor_reduce(small[:, 60:64], osq[:, :].rearrange("p (h n) -> p h n", h=GRP), AX, ALU.add),
                     "head_sums")

            def attention_out(a):
                g, t = STEPS[a]
                dve.wait_ge(s["head_std"], a + 1)
                step(V.reciprocal(small[:, 92:96], small[:, 64:68]))
                o3 = oh[:, :].rearrange("p (h n) -> p h n", h=GRP)
                step(V.tensor_tensor(o3, o3, small[:, 92:96].unsqueeze(2).broadcast_to([P, GRP, P]), ALU.mult))
                dve.wait_ge(s["proj_moved"], OUT_AT[f"ga{g}"] + 1)
                gate = ga3[:, t, g * HALF:(g + 1) * HALF]
                step(V.tensor_tensor(gate, gate, oh[:, :], ALU.mult), "head_gated")

            def recurrence_gated(c):
                dve.wait_ge(s["proj_moved"], OUT_AT[f"gl{c}"] + 1)
                mine = slice(c * D, (c + 1) * D)
                step(V.tensor_tensor(gl[:, mine], gl[:, mine], xc[:, mine], ALU.mult), "lru_done")

            attention_scores(0)
            dve.wait_ge(s["mult_made"], 1)
            step(V.tensor_tensor(ig[:, :], ig[:, :], lt[:, :], ALU.mult))
            for k in range(KC):
                ins = V.tensor_tensor_scan(xc3[:, k, :], xl[:, k * SEQ:(k + 1) * SEQ], ig3[:, k, :], 0.0,
                                           ALU.mult, ALU.add)
            step(ins)
            attention_weights(0)
            for a in range(1, len(STEPS)):
                attention_scores(a)
                head_squares(a - 1)
                attention_weights(a)
                attention_out(a - 1)
                if a == 2:
                    recurrence_gated(0)
            recurrence_gated(1)
            head_squares(len(STEPS) - 1)
            attention_out(len(STEPS) - 1)

            dve.wait_ge(s["rows_loaded"], 16)
            for t in range(NT):
                dve.wait_ge(s["post_std"], t + 1)
                step(V.reciprocal(stat[:, 40 + t:41 + t], stat[:, 38 + t:39 + t]))
                y = vv[:, t * D:(t + 1) * D]
                for c in range(2):
                    mine = slice(c * HALF, (c + 1) * HALF)
                    ins = V.scalar_tensor_tensor(out=y[:, mine], in0=pp[:, c, t, :], scalar=stat[:, 40 + t:41 + t],
                                                 in1=post_g[:, mine], op0=ALU.mult, op1=ALU.mult)
                if t == NT - 1:
                    ins.then_inc(s["proj_moved"], 2)
                    dve.wait_ge(s["proj_moved"], OUT_AT["wo1"] + 1)
                else:
                    step(ins)
                step(V.tensor_tensor(x3[:, t, :], x3[:, t, :], y, ALU.add), "block1_done")
                norm(2 + t, x3[:, t, :], y)
                norm_out(2 + t, col("mix_g", 0, KC), t)

            def heads_rms(dst, src, sq, sums, stds, recips, made, std_made, n_made, out_name, heads, width):
                step(V.tensor_tensor(sq, src, src, ALU.mult))
                step(V.tensor_reduce(sums, sq.rearrange("p (h n) -> p h n", h=heads), AX, ALU.add), made)
                dve.wait_ge(s[std_made], n_made)
                step(V.reciprocal(recips, stds))
                d3 = dst.rearrange("p (h n) -> p h n", h=heads)
                ins = V.tensor_tensor(d3, src.rearrange("p (h n) -> p h n", h=heads),
                                      recips.unsqueeze(2).broadcast_to([recips.shape[0], heads, width]), ALU.mult)
                step(ins, out_name) if out_name else step(ins)

            l0, l1, mx = col("lb0", 0, 4), col("lb1", 0, 4), lbt[:, 0:4]
            step(V.tensor_tensor(mx, l0, l1, ALU.max))
            V.tensor_tensor(lbt[:, 4:8], l0, mx, ALU.subtract)
            step(V.tensor_tensor(lbt[:, 8:12], l1, mx, ALU.subtract), "lb_shifted")
            dve.wait_ge(s["lb_exp"], 1)
            step(V.tensor_tensor(lbt[:, 12:16], lbt[:, 4:8], lbt[:, 8:12], ALU.add))
            step(V.reciprocal(lbt[:, 12:16], lbt[:, 12:16]))
            step(V.tensor_tensor(lbt[:, 16:20], lbt[:, 4:8], lbt[:, 12:16], ALU.mult))
            step(V.tensor_scalar(lbt[:, 20:24], lbt[:, 16:20], -1.0, 1.0, ALU.mult, ALU.add))
            V.memset(hid_k, 0.0)
            V.memset(hid_v, 0.0)
            V.memset(gain8[:, 6:8], 1.0)
            V.tensor_copy(gain8[:, 4:6], col("nk_g", 1, 2))
            step(V.tensor_scalar(gain8[:, 0:4], col("nq_g").broadcast_to([P, 4]), DH ** -0.5, None, ALU.mult))

            dve.wait_ge(s["proj_moved"], OUT_AT["nk"] + 1)
            for t in range(NT):
                src = nq3[:, t, 0:NORMED]
                heads_rms(src, src, sm[:, 0:NORMED], st2[:, 40 + 12 * t:52 + 12 * t],
                          st2[:, 16 + 12 * t:28 + 12 * t], small[:, 150 + 12 * t:162 + 12 * t],
                          "nsa_sums", "nsa_std", t + 1, "nsa_scaled", NORMED // DH, DH)
            dve.wait_ge(s["proj_moved"], OUT_AT["hf"] + 1)
            for h in range(HG_HEADS):
                f = at2.key[:, h * SEQ:(h + 1) * SEQ]
                ins = V.tensor_scalar(f, f, lbt[:, 20 + h:21 + h], lbt[:, 16 + h:17 + h], ALU.mult, ALU.add)
            step(ins, "forget_made")
            for t in range(NT):
                dve.wait_ge(s["nsa_turned"], t + 1)
                step(V.tensor_tensor(nT3[:, :, t * P:(t + 1) * P],
                                     pa[:, t * D:(t + 1) * D].rearrange("p (k n) -> p k n", k=KC),
                                     gain8.unsqueeze(2).broadcast_to([P, KC, P]), ALU.mult), "nsa_normed")
            for kv in range(2):
                for n, dst in enumerate((at2.pe0, at2.pe1)):
                    ins = V.tensor_tensor(
                        dst[:, kv * SEQ:(kv + 1) * SEQ].rearrange("p (b j) -> p b j", j=CMP_STRIDE),
                        nT3[:, 6 + kv, :].rearrange("p (b j) -> p b j", j=CMP_STRIDE),
                        col("pe", kv * CMP_LEN + n * CMP_STRIDE, CMP_STRIDE).unsqueeze(1)
                        .broadcast_to([P, SEQ // CMP_STRIDE, CMP_STRIDE]), ALU.add)
            step(ins, "cmp_in")
            dve.wait_ge(s["log_made"], 1)
            step(V.tensor_scalar(at2.key, at2.key, -1.0, 1.0, ALU.mult, ALU.add))
            dve.wait_ge(s["scan_mask_made"], 1)
            step(V.tensor_tensor_scan(at2.cum, at2.scan_mask, at2.log_f, 0.0, ALU.mult, ALU.add))
            cum3 = at2.cum.rearrange("p (m n) -> p m n", n=CH)
            shift3 = at2.shift.rearrange("p (m n) -> p m n", n=CH)
            shape = [P, HG_HEADS * NCH, CH]
            step(V.tensor_tensor(shift3, cum3, cum3[:, :, CH // 2 - 1:CH // 2].broadcast_to(shape), ALU.subtract),
                 "shift_made")
            dve.wait_ge(s["shift_exp"], 1)
            step(V.tensor_tensor(shift3, cum3[:, :, CH - 1:CH].broadcast_to(shape), cum3, ALU.subtract), "last_made")
            dve.wait_ge(s["proj_moved"], OUT_AT["hq"] + 1)
            V.scalar_tensor_tensor(out=at2.q1, in0=at2.query, scalar=P ** -0.5, in1=at2.q1, op0=ALU.mult, op1=ALU.mult)
            V.tensor_tensor(at2.k2, at2.key, at2.k2, ALU.mult)
            V.scalar_tensor_tensor(out=at2.q3, in0=at2.query, scalar=P ** -0.5, in1=at2.q3, op0=ALU.mult, op1=ALU.mult)
            dve.wait_ge(s["last_exp"], 1)
            step(V.tensor_tensor(at2.k4, at2.key, at2.k4, ALU.mult), "recur_ready")

            dve.wait_ge(s["cmp_full"], 1)
            kc_raw = at2.tmp[0:32, DH:2 * DH]
            step(V.tensor_copy(kc_raw, kc_psum))
            step(V.tensor_tensor_reduce(out=at2.tmp[0:32, 0:DH], in0=kc_raw, in1=kc_raw, scale=1.0, scalar=0.0,
                                        op0=ALU.mult, op1=ALU.add, accum_out=st2[0:32, 64:65]), "cmp_sums")
            dve.wait_ge(s["bias2_made"], 1)
            step(V.tensor_tensor(at2.v_blocks.rearrange("p (h n) -> p h n", n=DH),
                                 vc_psum.unsqueeze(1).broadcast_to([P, NSA_HEADS, DH]),
                                 head_mask.unsqueeze(2).broadcast_to([P, NSA_HEADS, DH]), ALU.mult), "v_blocks_made")
            dve.wait_ge(s["cmp_std"], 1)
            step(V.reciprocal(st2[0:32, 66:67], st2[0:32, 65:66]))
            for g in range(NKV):
                ins = V.tensor_scalar(at2.kc[:, g * DH:(g + 1) * DH], kc_raw, st2[0:32, 66:67],
                                      group_mask[:, g:g + 1], ALU.mult, ALU.mult)
            step(ins, "cmp_ready")

            dve.wait_ge(s["update_full"], 1)
            u = [pa[:, b * HALF:(b + 1) * HALF] for b in UPDATE_BANKS]
            step(V.tensor_copy(at2.states[:, 0:HALF], u[0]))
            for c in range(1, NCH - 1):
                for h in range(HG_HEADS):
                    a = h * P
                    ins = V.scalar_tensor_tensor(out=at2.states[:, c * HALF + a:c * HALF + a + P],
                                                 in0=at2.states[:, (c - 1) * HALF + a:(c - 1) * HALF + a + P],
                                                 scalar=last_exp[:, h * NCH + c:h * NCH + c + 1],
                                                 in1=u[c][:, a:a + P], op0=ALU.mult, op1=ALU.add)
                if c < NCH - 2:
                    step(ins)
            step(ins, "states_made")

            gates3 = [nq3[:, t, NQW - GATES:NQW].rearrange("p (h b) -> p h b", b=3) for t in range(NT)]
            b3 = at2.bias[:, :].rearrange("p (h n) -> p h n", h=NSA_HEADS)

            def att_biased(b):
                t, w, heads = STEPS2[b]
                n, m = P * (t + 1), len(heads)
                sc = score2(at2.sc[b % 4], b)
                dve.wait_ge(s["att_full"], b + 1)
                step(V.tensor_tensor(sc, score2(att_psum[b], b), b3[:, heads.start:heads.stop, SEQ - n:SEQ], ALU.add))
                step(V.tensor_reduce(st2[:, 72:72 + m], sc, AX, ALU.max))
                step(V.tensor_scalar(att_shift[b][:, 0:m], st2[:, 72:72 + m], -1.0, None, ALU.mult), "att_bias")

            def att_out(b):
                t, w, heads = STEPS2[b]
                m = len(heads)
                over = small[:, 228:228 + m]
                dve.wait_ge(s["att_exp"], b + 1)
                step(V.tensor_scalar(over, att_sums[b][:, 0:m], 1e-30, None, ALU.max))
                step(V.reciprocal(over, over))
                step(V.tensor_tensor(over, over, gates3[t][:, heads.start:heads.stop, 1 + w], ALU.mult))
                dve.wait_ge(s["ao_full"], b + 1)
                tmp = at2.tmp[:, 0:m * DH]
                step(V.tensor_tensor(tmp.rearrange("p (h n) -> p h n", n=DH),
                                     att_psum[b][:, 0:m * DH].rearrange("p (h n) -> p h n", n=DH),
                                     over.unsqueeze(2).broadcast_to([P, m, DH]), ALU.mult), "ao_used")
                no = at2.no[:, t * HALF + heads.start * DH:t * HALF + heads.stop * DH]
                step(V.tensor_tensor(no, no, tmp, ALU.add))

            def sparse_sums(t):
                no = at2.no[:, t * HALF:(t + 1) * HALF]
                step(V.tensor_tensor(at2.osq[:, 0:HALF], no, no, ALU.mult))
                step(V.tensor_reduce(st2[:, 96 + 8 * t:104 + 8 * t],
                                     at2.osq[:, 0:HALF].rearrange("p (h n) -> p h n", n=DH), AX, ALU.add), "nsa_osums")

            def sparse_scaled(t):
                dve.wait_ge(s["nsa_ostd"], NT - t)
                recips = small[:, 124 + 8 * t:132 + 8 * t]
                step(V.reciprocal(recips, st2[:, 112 + 8 * t:120 + 8 * t]))
                no = at2.no[:, t * HALF:(t + 1) * HALF].rearrange("p (h n) -> p h n", n=DH)
                step(V.tensor_tensor(no, no, recips.unsqueeze(2).broadcast_to([P, NSA_HEADS, DH]), ALU.mult), "nsa_out")

            def mixed_gained(n, dst, src, chunks, width):
                dve.wait_ge(s["mix_turned"], n)
                step(V.tensor_tensor(dst, src.rearrange("p (k n) -> p k n", k=4),
                                     col("out2_g", chunks, 4).unsqueeze(2).broadcast_to([P, 4, width]), ALU.mult),
                     "mixT_made")

            att_biased(0)
            M = NT * NSA_HEADS
            ec = e_c.rearrange("p (m n) -> p m n", n=16)
            dve.wait_ge(s["cs_full"], 1)
            step(V.tensor_tensor(e_c, cs_psum, bias_c, ALU.add))
            cmax, csum = small[:, 180:196], small[:, 196:212]
            step(V.tensor_reduce(cmax, ec, AX, ALU.max))
            step(V.tensor_tensor(ec, ec, cmax.unsqueeze(2).broadcast_to([P, M, 16]), ALU.subtract), "cs_shifted")
            att_biased(1)
            dve.wait_ge(s["cs_exp"], 1)
            step(V.tensor_tensor(e_c, e_c, mask_c, ALU.mult))
            step(V.tensor_reduce(csum, ec, AX, ALU.add), "cs_ready")
            step(V.tensor_scalar(csum, csum, 1e-30, None, ALU.max))
            step(V.reciprocal(csum, csum))
            coef = small[:, 212:228]
            for t in range(NT):
                ins = V.tensor_tensor(coef[:, t * 8:(t + 1) * 8].rearrange("p (g r) -> p g r", g=NKV),
                                      csum.rearrange("p (t r g) -> p t g r", g=NKV, t=NT)[:, t, :, :],
                                      gates3[t][:, :, 0].rearrange("p (g r) -> p g r", g=NKV), ALU.mult)
            step(ins)
            dve.wait_ge(s["co_full"], 1)
            step(V.tensor_tensor(at2.no.rearrange("p (m n) -> p m n", n=DH),
                                 co_psum.rearrange("p (m n) -> p m n", n=DH),
                                 coef.unsqueeze(2).broadcast_to([P, M, DH]), ALU.mult), "co_used")
            dve.wait_ge(s["o_moved"], 1)
            step(V.tensor_tensor(at2.osq, at2.o, at2.o, ALU.mult))
            step(V.tensor_reduce(st2[:, 8:16], at2.osq.rearrange("p (h n) -> p h n", n=P), AX, ALU.add), "o_sums")
            att_biased(2)
            att_biased(3)
            att_out(0)
            att_out(1)
            dve.wait_ge(s["o_std"], 1)
            step(V.reciprocal(small[:, 140:148], st2[:, 0:8]))
            o3 = at2.o.rearrange("p (h n) -> p h n", n=P)
            step(V.tensor_tensor(o3, o3, small[:, 140:148].unsqueeze(2).broadcast_to([P, NT * HG_HEADS, P]), ALU.mult))
            step(V.tensor_tensor(at2.o, at2.o, at2.gate, ALU.mult), "o_gated")
            mixed_gained(1, h3[:, 0:4, :], pp_flat[:, 0:D], 0, SEQ)
            att_out(2)
            att_out(3)
            sparse_sums(1)
            att_biased(4)
            att_biased(5)
            sparse_scaled(1)
            att_out(4)
            mixed_gained(2, h3[:, 4:KC, P:2 * P], pa[:, HALF:2 * HALF], 4, P)
            att_out(5)
            sparse_sums(0)
            sparse_scaled(0)
            mixed_gained(3, h3[:, 4:KC, 0:P], pa[:, 3 * HALF:4 * HALF], 4, P)

            def joined(t):
                for c in range(2):
                    rows_x = x3[:, t, c * HALF:(c + 1) * HALF]
                    ins = V.tensor_tensor(rows_x, rows_x, pp[:, c, t, :], ALU.add)
                return ins

            dve.wait_ge(s["wp_full"], 1)
            step(joined(1))
            norm(4, x3[:, 1, :], vv[:, D:2 * D])
            dve.wait_ge(s["unit_used"], UNIT_AT["wp1"] + 1)
            joined(0).then_inc(s["proj_moved"], 2)
            dve.wait_ge(s["proj_moved"], OUT_AT["wp1"] + 1)
            norm(5, x3[:, 0, :], vv[:, 0:D])
            norm_out(4, col("ffn_g", 0, KC), 1)
            norm_out(5, col("ffn_g", 0, KC), 0)
            dve.wait_ge(s["rows_loaded"], 32)
            for t in range(NT):
                xt = vv[:, t * D:(t + 1) * D]
                step(V.tensor_tensor(xt, xt, post_g[:, :], ALU.mult))
            two = [P, 2, TOPK, TOPK]

            def choose(head, odd):
                count = [0]

                def then(ins):
                    count[0] += 1
                    ins.then_inc(s["choice_step"], 1)
                    dve.wait_ge(s["choice_step"], count[0])

                def top16(rows_in, values, at, n):
                    for half in range(2):
                        where = slice(half * 8, half * 8 + 8)
                        for j in range(n):
                            ins = V.max(values[:, j, where], rows_in[:, j, :])
                        then(ins)
                        for j in range(n):
                            ins = V.max_index(at[:, j, where], values[:, j, where], rows_in[:, j, :])
                        then(ins)
                        if half == 0:
                            for j in range(n):
                                ins = V.match_replace(rows_in[:, j, :], values[:, j, where], rows_in[:, j, :], LOWEST)
                            then(ins)

                then(V.tensor_copy(halves, xc_rg[:, bass.ds(head * (2 * NKEYS), 2 * NKEYS)]))
                v3 = v16.rearrange("p (c k) -> p c k", c=2)
                top16(halves.rearrange("p (c n) -> p c n", c=2), v3, i16.rearrange("p (c k) -> p c k", c=2), 2)
                V.tensor_copy(i16f, i16)
                then(V.tensor_tensor(pairs.rearrange("p (a b) -> p a b", a=TOPK),
                                     v3[:, 0, :].unsqueeze(2).broadcast_to([P, TOPK, TOPK]),
                                     v3[:, 1, :].unsqueeze(1).broadcast_to([P, TOPK, TOPK]), ALU.add))
                top16(pairs.unsqueeze(1), best.unsqueeze(1), best_at.unsqueeze(1), 1)
                V.tensor_scalar(top_w[odd], best, best[:, 0:1], None, ALU.subtract).then_inc(s["top_shift"], 1)
                V.tensor_scalar(places_i[:, 0:TOPK], best_at, 4, None, ALU.logical_shift_right)
                then(V.tensor_scalar(places_i[:, TOPK:2 * TOPK], best_at, TOPK - 1, None, ALU.bitwise_and))
                then(V.tensor_copy(places, places_i))
                for half in range(2):
                    mine = slice(half * TOPK, (half + 1) * TOPK)
                    square = [P, TOPK, TOPK]
                    h3d = hot.rearrange("p (k j) -> p k j", k=TOPK)
                    then(V.tensor_tensor(h3d, places[:, mine].unsqueeze(2).broadcast_to(square),
                                         iota16.unsqueeze(1).broadcast_to(square), ALU.is_equal))
                    then(V.tensor_tensor(h3d, h3d, i16f[:, mine].unsqueeze(1).broadcast_to(square), ALU.mult))
                    then(V.tensor_reduce(keys_f[:, mine], h3d, AX, ALU.add))
                V.scalar_tensor_tensor(out=keys_f[:, 0:TOPK], in0=keys_f[:, 0:TOPK], scalar=float(NKEYS),
                                       in1=keys_f[:, TOPK:2 * TOPK], op0=ALU.mult, op1=ALU.add)\
                    .then_inc(s["choice_step"], 1)
                dve.wait_ge(s["choice_step"], count[0] + 1)
                dve.sem_clear(s["choice_step"])
                V.tensor_copy(all_experts[:, bass.ds(head * TOPK, TOPK)], keys_f[:, 0:TOPK]).then_inc(s["chosen"], 1)

            def head_dots(head, odd, t):
                for k in range(TOPK):
                    rows_u = u_rows[k % NBUF]
                    a = odd * TOPK + k
                    dve.wait_ge(u_here[k % NBUF], (head * 2 + k // NBUF + 1) * 16)
                    V.tensor_tensor_reduce(out=rows_u, in0=rows_u, in1=vv[:, t * D:(t + 1) * D], scale=1.0,
                                           scalar=0.0, op0=ALU.mult, op1=ALU.add,
                                           accum_out=dots[:, a:a + 1]).then_inc(s["u_free"], 1)
                mine = slice(odd * TOPK, (odd + 1) * TOPK)
                dve.wait_ge(s["top_exp"], head + 1)
                V.tensor_reduce(top_sum, top_w[odd], AX, ALU.add).then_inc(s["top_summed"], 1)
                dve.wait_ge(s["top_summed"], head * 2 + 1)
                V.reciprocal(top_sum, top_sum).then_inc(s["top_summed"], 1)
                dve.wait_ge(s["gelu_made"], head + 1)
                dve.wait_ge(s["top_summed"], head * 2 + 2)
                V.scalar_tensor_tensor(out=wk[:, mine], in0=acts[:, mine], scalar=top_sum, in1=top_w[odd],
                                       op0=ALU.mult, op1=ALU.mult).then_inc(s["w_made"], 1)

            V.memset(small[:, 237:238], 0.0).then_inc(s["u_free"], NBUF)
            V.memset(small[:, 238:239], 0.0).then_inc(s["v_free"], NBUF)
            dve.wait_ge(s["first_taken"], 1)
            choose(0, 0)
            with dve.Fori(0, PEER_HEADS // 2) as pair:
                for odd in range(2):
                    dve.wait_ge(s["pscore_moved"], pair + odd + 1)
                    dve.sem_inc(s["dve_pace"], 1)
                    choose(pair * 2 + odd + 1, 1 - odd)
                    head_dots(pair * 2 + odd, odd, 0)
            def gate_input(t):
                dve.wait_ge(s["h2_made"], t + 1)
                step(V.tensor_tensor_reduce(out=vv[:, t * D:(t + 1) * D], in0=x3[:, t, :], in1=x3[:, t, :], scale=1.0,
                                            scalar=0.0, op0=ALU.mult, op1=ALU.add, accum_out=stat[:, 6 + t:7 + t]),
                     "squares_summed")

            def gate_scale(t):
                dve.wait_ge(s["std_made"], 7 + t)
                step(V.reciprocal(stat[:, 30 + t:31 + t], stat[:, 22 + t:23 + t]), "scaled")

            def gated(t):
                for c in range(2):
                    dve.wait_ge(s["gate_moved"], t * 2 + c + 1)
                    mine = slice(t * D + c * HALF, t * D + (c + 1) * HALF)
                    step(V.tensor_tensor(lt[:, mine], lt[:, mine], nq[:, mine], ALU.mult))
                    step(V.tensor_tensor(xs[:, mine], xs[:, mine], lt[:, mine], ALU.add), "y_made")

            choose(PEER_HEADS + 1, 1)
            head_dots(PEER_HEADS, 0, 1)
            gate_input(0)
            choose(PEER_HEADS + 2, 0)
            gate_scale(0)
            head_dots(PEER_HEADS + 1, 1, 1)
            norm_out(6, col("gate_g", 0, KC), 0)
            with dve.Fori(PEER_HEADS // 2 + 1, PEER_HEADS - 1) as pair:
                for odd in range(2):
                    choose(pair * 2 + odd + 1, 1 - odd)
                    head_dots(pair * 2 + odd, odd, 1)
            choose(LAST_HEAD, 1)
            head_dots(LAST_HEAD - 1, 0, 1)
            head_dots(LAST_HEAD, 1, 1)
            gated(0)
            gate_input(1)
            norm_out(7, col("gate_g", 0, KC), 1)
            gate_scale(1)
            gated(1)


def feature_columns(v):
    return np.asarray(v).reshape(-1, P).T


def unit_of(w, k0, c0, c1):
    w = np.asarray(w)[k0:k0 + D, c0:c1]
    out = np.zeros((P, KC, HALF), np.float32)
    out[:, :, 0:w.shape[1]] = w.reshape(KC, P, -1).transpose(1, 0, 2)
    return out.reshape(P, UNIT)


def padded(parts):
    out = np.zeros((P, UNIT), np.float32)
    at = 0
    for a in parts:
        out[:, at:at + a.shape[1]] = a
        at += a.shape[1]
    return out


def lay_out(i):
    w_in, w_out = np.asarray(i["w_in"])[0], np.asarray(i["w_out"])[0]
    at = {"q": 0, "k": D, "v": 2 * D, "ga": 3 * D, "xl": 4 * D, "gl": 5 * D}
    w2, wp = np.asarray(i["w_in_2"])[0], np.asarray(i["w_out_2"])[0]
    wq, gw = np.asarray(i["peer_wq_2"])[0], np.asarray(i["ple_gate_w_2"])[0]
    nsa, kv = 4 * HALF, 5 * HALF
    order = [np.arange(nsa, kv).reshape(NKV, REP, DH).transpose(1, 0, 2).ravel()]
    order += [np.arange(kv + n * P, kv + (n + 1) * P) for n in (2, 4, 0, 1, 3, 5)]
    order.append(np.arange(kv + 6 * P, kv + 6 * P + GATES))
    wn = w2[:, np.concatenate(order)]
    both = lambda a: np.concatenate([a, a], axis=0)
    units = []
    for name in UNITS:
        if name == "lru":
            units.append(padded([np.asarray(i[n])[0].transpose(1, 0, 2).reshape(P, D) for n in ("w_rgate", "w_igate")]))
        elif name[:3] == "wol":
            units.append(unit_of(w_out, D, int(name[3]) * HALF, (int(name[3]) + 1) * HALF))
        elif name[:3] == "woa":
            units.append(unit_of(w_out, 0, int(name[3]) * HALF, (int(name[3]) + 1) * HALF))
        elif name in ("hf", "hq", "hi", "hg"):
            a = {"hq": 0, "hf": 1, "hi": 2, "hg": 3}[name] * HALF
            units.append(unit_of(w2, 0, a, a + HALF))
        elif name in ("nq", "nk", "nv"):
            a = {"nq": 0, "nk": 1, "nv": 2}[name] * HALF
            units.append(unit_of(wn, 0, a, min(a + HALF, NQW)))
        elif name == "cmp":
            w = np.asarray(i["cmp_w1_2"])[0].reshape(2, CMP_LEN, DH, DH).transpose(2, 0, 1, 3).reshape(DH, UNIT)
            units.append(both(w))
        elif name == "ple":
            w = np.asarray(i["ple_proj_2"])[0].reshape(PLE // P, P, D)
            p = np.asarray(i["p_2"])[0, 0].T.reshape(PLE // P, P, SEQ)
            units.append(padded([*w, *p]))
        elif name[:2] in ("wp", "wq", "gw"):
            c = int(name[2]) * HALF
            units.append(unit_of({"wp": wp, "wq": wq, "gw": gw}[name[:2]], 0, c, c + HALF))
        else:
            a = at[name[:-1]] + int(name[-1]) * HALF
            units.append(unit_of(w_in, 0, a, a + HALF))
    named = {
        "pre_g": feature_columns(i["pre_norm_g"]), "conv_w": feature_columns(i["conv_w"]),
        "conv_b": feature_columns(i["conv_b"]), "b_r": feature_columns(i["b_rgate"]),
        "b_i": feature_columns(i["b_igate"]), "lam": feature_columns(i["lru_lambda"]),
        "sub_g": feature_columns(i["subln_g"]),
        "mix_g": feature_columns(i["mix_norm_2"]), "ffn_g": feature_columns(i["ffn_norm_2"]),
        "gate_g": feature_columns(i["ple_gate_norm_2"]),
        "lb0": feature_columns(np.asarray(i["hg_lb_logits_2"])[0]),
        "lb1": feature_columns(np.asarray(i["hg_lb_logits_2"])[1]),
        "out2_g": np.concatenate([feature_columns(i["hg_out_norm_2"]), feature_columns(i["nsa_out_norm_2"])], axis=1),
        "nq_g": both(np.asarray(i["nsa_q_norm_2"]).T), "nk_g": both(np.asarray(i["nsa_k_norm_2"])[0].T),
        "pe": both(np.asarray(i["cmp_pe_2"])[0].reshape(2 * CMP_LEN, DH).T),
        "cmp_w2": both(np.asarray(i["cmp_w2_2"])[0].transpose(1, 0, 2).reshape(DH, 2 * DH)),
    }
    return {
        "x": np.asarray(i["x"])[0],
        "wall": np.stack(units),
        "cols": np.ascontiguousarray(np.concatenate([named[n] for n, _ in COLS], axis=1)),
        "rows": np.stack([np.asarray(i["post_norm_g"])[0], np.asarray(i["ffn_norm_2"])[0]]),
        "sub_keys": np.ascontiguousarray(np.asarray(i["peer_keys_2"])[0].reshape(2 * PEER_HEADS, NKEYS, P)
                                         .transpose(2, 0, 1).reshape(P, -1)),
        "peer_u": np.asarray(i["peer_u_2"])[0],
        "peer_v": np.asarray(i["peer_v_2"])[0],
        "lambdas": np.concatenate([np.asarray(i[n]) for n in ("lambda_q1", "lambda_k1", "lambda_q2", "lambda_k2")], axis=1),
    }


def kernel(**inputs):
    import concourse.bacc as bacc
    from concourse.bass_utils import run_bass_kernel_spmd

    nc = bacc.Bacc("TRN2", target_bir_lowering=False, num_devices=1)
    arrays = {f"in_{n}": np.ascontiguousarray(a) for n, a in lay_out(inputs).items()}
    aps = {n[3:]: nc.dram_tensor(n, a.shape, mybir.dt.from_np(a.dtype), kind="ExternalInput").ap()
           for n, a in arrays.items()}
    out = nc.dram_tensor("out", (SEQ, D), F32, kind="ExternalOutput").ap()
    two_blocks(nc, out=out, **aps)
    r = run_bass_kernel_spmd(nc, [arrays], core_ids=[0])
    return r.results[0]["out"].reshape(1, SEQ, D)
```
